# Optimizing a Trainium2 kernel written in Bass

```python
import math
import jax, jax.numpy as jnp
from jax import lax
import numpy as np

D_MODEL = 1024
BATCH = 1
SEQ = 1024
DEPTH = 1

CHUNK = 64
SSM_GROUP = 16
D_SSM = D_MODEL // 4
SSM_GROUPS = D_SSM // SSM_GROUP
SSM_STATE = 64
DT_MIN = 0.001
DT_MAX = 0.1
D_POOL = D_MODEL // 2
POOL_WINDOWS = (2, 4, 8, 16)
POOL_GROUPS = len(POOL_WINDOWS)
POOL_GC = D_POOL // POOL_GROUPS
POOL_MAX = max(POOL_WINDOWS)
D_IN = D_SSM + D_POOL + 2 * D_MODEL
N_EXPERT_GROUPS = 4
EXPERTS_PER_GROUP = 8
N_EXPERTS = N_EXPERT_GROUPS * EXPERTS_PER_GROUP
TOP_K_FINE = 2
D_EXPERT = D_MODEL // 2
N_MOD = 6
EPS = 1e-6

kernel_name = "hybrid_s5_pool_hiermoe_block"

def rms_norm(x, g):
    xf = x.astype(jnp.float32)
    y = xf * lax.rsqrt(jnp.mean(xf * xf, axis=-1, keepdims=True) + EPS)
    return (y * g.astype(jnp.float32)).astype(x.dtype)

def modulate(h, g, shift, scale):
    return rms_norm(h, g) * (1.0 + scale[:, None, :]) + shift[:, None, :]

def s5_mixer(u, lam_re, lam_im, log_dt, b_re, b_im, c_re, c_im, d_skip, w_glu, b_glu):
    bsz, seq, _ = u.shape
    uf = u.astype(jnp.float32).reshape(bsz, seq, SSM_GROUPS, SSM_GROUP)
    lr = lam_re.astype(jnp.float32)
    li = lam_im.astype(jnp.float32)
    dt = jnp.exp(log_dt.astype(jnp.float32))[:, None]
    mag = jnp.exp(lr * dt)
    lb_re = mag * jnp.cos(li * dt)
    lb_im = mag * jnp.sin(li * dt)
    den = lr * lr + li * li
    nr = lb_re - 1.0
    f_re = (nr * lr + lb_im * li) / den
    f_im = (lb_im * lr - nr * li) / den
    br = b_re.astype(jnp.float32)
    bi = b_im.astype(jnp.float32)
    bb_re = f_re[..., None] * br - f_im[..., None] * bi
    bb_im = f_re[..., None] * bi + f_im[..., None] * br
    bu_re = jnp.einsum('bsgh,gph->bsgp', uf, bb_re)
    bu_im = jnp.einsum('bsgh,gph->bsgp', uf, bb_im)
    a_re = jnp.broadcast_to(lb_re, (1, seq, SSM_GROUPS, SSM_STATE))
    a_im = jnp.broadcast_to(lb_im, (1, seq, SSM_GROUPS, SSM_STATE))

    def combine(left, right):
        ar_l, ai_l, xr_l, xi_l = left
        ar_r, ai_r, xr_r, xi_r = right
        ar = ar_r * ar_l - ai_r * ai_l
        ai = ar_r * ai_l + ai_r * ar_l
        xr = ar_r * xr_l - ai_r * xi_l + xr_r
        xi = ar_r * xi_l + ai_r * xr_l + xi_r
        return (ar, ai, xr, xi)

    _, _, st_re, st_im = lax.associative_scan(combine, (a_re, a_im, bu_re, bu_im), axis=1)
    y = (jnp.einsum('bsgp,ghp->bsgh', st_re, c_re.astype(jnp.float32))
         - jnp.einsum('bsgp,ghp->bsgh', st_im, c_im.astype(jnp.float32))
         + d_skip.astype(jnp.float32).reshape(SSM_GROUPS, SSM_GROUP) * uf)
    y = jax.nn.gelu(y.reshape(bsz, seq, D_SSM))
    z = y * jax.nn.sigmoid(y @ w_glu.astype(jnp.float32) + b_glu.astype(jnp.float32))
    return z.astype(u.dtype)

def pool_mixer(u, w_pool, pool_scale):
    bsz, seq, _ = u.shape
    uf = u.astype(jnp.float32)
    cs = jnp.pad(jnp.cumsum(uf, axis=1), ((0, 0), (POOL_MAX, 0), (0, 0)))
    pos = jnp.arange(seq, dtype=jnp.float32)
    outs = []
    for gi, w in enumerate(POOL_WINDOWS):
        lo, hi = gi * POOL_GC, (gi + 1) * POOL_GC
        win = cs[:, POOL_MAX:POOL_MAX + seq, lo:hi] - cs[:, POOL_MAX - w:POOL_MAX - w + seq, lo:hi]
        cnt = jnp.minimum(pos + 1.0, float(w))[None, :, None]
        outs.append(win / cnt - uf[:, :, lo:hi])
    m = jnp.stack(outs, axis=2)
    y = jnp.einsum('bsgc,gcd->bsgd', m, w_pool.astype(jnp.float32)).reshape(bsz, seq, D_POOL)
    return (y * pool_scale.astype(jnp.float32)).astype(u.dtype)

def hier_moe(u, w_coarse, b_coarse, w_fine, b_fine, w_gate, w_up, w_down):
    bsz, seq, d = u.shape
    n_tok = bsz * seq
    xf = u.reshape(n_tok, d)
    x32 = xf.astype(jnp.float32)
    coarse = x32 @ w_coarse.astype(jnp.float32) + b_coarse.astype(jnp.float32)
    p_coarse = jax.nn.softmax(coarse, axis=-1)
    _, grp = lax.top_k(coarse, 1)
    p_grp = jnp.take_along_axis(p_coarse, grp, axis=-1)
    fine = (x32 @ w_fine.astype(jnp.float32) + b_fine.astype(jnp.float32)).reshape(
        n_tok, N_EXPERT_GROUPS, EXPERTS_PER_GROUP)
    fine_sel = jnp.take_along_axis(fine, grp[:, :, None], axis=1)[:, 0, :]
    p_fine = jax.nn.softmax(fine_sel, axis=-1)
    top_p, top_i = lax.top_k(p_fine, TOP_K_FINE)
    weights = p_grp * top_p / jnp.sum(top_p, axis=-1, keepdims=True)
    expert = grp * EXPERTS_PER_GROUP + top_i

    e_flat = expert.reshape(-1)
    w_flat = weights.reshape(-1)
    tok_flat = jnp.repeat(jnp.arange(n_tok, dtype=jnp.int32), TOP_K_FINE)
    order = jnp.argsort(e_flat)
    tok_sorted = tok_flat[order]
    w_sorted = w_flat[order]
    group_sizes = jnp.bincount(e_flat, length=N_EXPERTS).astype(jnp.int32)
    xs = xf[tok_sorted]
    h1 = lax.ragged_dot(xs, w_gate.astype(xs.dtype), group_sizes)
    h2 = lax.ragged_dot(xs, w_up.astype(xs.dtype), group_sizes)
    act = jax.nn.silu(h1) * h2
    ys = lax.ragged_dot(act, w_down.astype(act.dtype), group_sizes)
    ys = ys * w_sorted[:, None].astype(ys.dtype)
    out = jax.ops.segment_sum(ys, tok_sorted, num_segments=n_tok)
    return out.reshape(bsz, seq, d).astype(u.dtype)

def setup_inputs(seed: int = 0) -> dict:
    key = jax.random.key(seed)
    ks = jax.random.split(key, 32)
    f32 = jnp.float32
    L, D = DEPTH, D_MODEL
    nrm = lambda k, shape, s: jax.random.normal(k, shape, f32) * s
    n_idx = jnp.arange(SSM_STATE, dtype=f32)
    lam_re = -0.5 + 0.01 * jax.random.normal(ks[6], (L, SSM_GROUPS, SSM_STATE), f32)
    lam_im = math.pi * n_idx[None, None, :] + 0.01 * jax.random.normal(ks[7], (L, SSM_GROUPS, SSM_STATE), f32)
    log_dt = jax.random.uniform(ks[8], (L, SSM_GROUPS), f32, math.log(DT_MIN), math.log(DT_MAX))
    return {
        "x": nrm(ks[0], (BATCH, SEQ, D), 1.0),
        "c": nrm(ks[1], (BATCH, D), 1.0),
        "w_mod": nrm(ks[2], (L, D, N_MOD * D), D ** -0.5),
        "b_mod": nrm(ks[3], (L, N_MOD * D), 0.02),
        "norm1_g": 1.0 + nrm(ks[4], (L, D), 0.05),
        "w_in": nrm(ks[5], (L, D, D_IN), D ** -0.5),
        "b_in": nrm(ks[9], (L, D_IN), 0.02),
        "ssm_lam_re": lam_re,
        "ssm_lam_im": lam_im,
        "ssm_log_dt": log_dt,
        "ssm_b_re": nrm(ks[10], (L, SSM_GROUPS, SSM_STATE, SSM_GROUP), (2 * SSM_GROUP) ** -0.5),
        "ssm_b_im": nrm(ks[11], (L, SSM_GROUPS, SSM_STATE, SSM_GROUP), (2 * SSM_GROUP) ** -0.5),
        "ssm_c_re": nrm(ks[12], (L, SSM_GROUPS, SSM_GROUP, SSM_STATE), SSM_STATE ** -0.5),
        "ssm_c_im": nrm(ks[13], (L, SSM_GROUPS, SSM_GROUP, SSM_STATE), SSM_STATE ** -0.5),
        "ssm_d": nrm(ks[14], (L, D_SSM), 1.0),
        "ssm_w_glu": nrm(ks[15], (L, D_SSM, D_SSM), D_SSM ** -0.5),
        "ssm_b_glu": nrm(ks[16], (L, D_SSM), 0.02),
        "pool_w": nrm(ks[17], (L, POOL_GROUPS, POOL_GC, POOL_GC), POOL_GC ** -0.5),
        "pool_scale": 1.0 + nrm(ks[18], (L, D_POOL), 0.1),
        "w_proj_ssm": nrm(ks[19], (L, D_SSM, D), D_SSM ** -0.5),
        "w_proj_pool": nrm(ks[20], (L, D_POOL, D), D_POOL ** -0.5),
        "w_out": nrm(ks[21], (L, D, D), D ** -0.5),
        "norm2_g": 1.0 + nrm(ks[22], (L, D), 0.05),
        "router_coarse_w": nrm(ks[23], (L, D, N_EXPERT_GROUPS), D ** -0.5),
        "router_coarse_b": nrm(ks[24], (L, N_EXPERT_GROUPS), 0.01),
        "router_fine_w": nrm(ks[25], (L, D, N_EXPERTS), D ** -0.5),
        "router_fine_b": nrm(ks[26], (L, N_EXPERTS), 0.01),
        "moe_w_gate": nrm(ks[27], (L, N_EXPERTS, D, D_EXPERT), D ** -0.5),
        "moe_w_up": nrm(ks[28], (L, N_EXPERTS, D, D_EXPERT), D ** -0.5),
        "moe_w_down": nrm(ks[29], (L, N_EXPERTS, D_EXPERT, D), D_EXPERT ** -0.5),
        "norm_f_g": 1.0 + nrm(ks[30], (D,), 0.05),
    }

def reference(x, c, w_mod, b_mod, norm1_g, w_in, b_in, ssm_lam_re, ssm_lam_im, ssm_log_dt,
              ssm_b_re, ssm_b_im, ssm_c_re, ssm_c_im, ssm_d, ssm_w_glu, ssm_b_glu,
              pool_w, pool_scale, w_proj_ssm, w_proj_pool, w_out, norm2_g,
              router_coarse_w, router_coarse_b, router_fine_w, router_fine_b,
              moe_w_gate, moe_w_up, moe_w_down, norm_f_g):
    h = x
    c_act = jax.nn.silu(c)
    for l in range(DEPTH):
        mod = c_act @ w_mod[l] + b_mod[l]
        shift1, scale1, gate1, shift2, scale2, gate2 = jnp.split(mod, N_MOD, axis=-1)

        u = modulate(h, norm1_g[l], shift1, scale1)
        proj = u @ w_in[l] + b_in[l]
        u_ssm = proj[..., :D_SSM]
        u_pool = proj[..., D_SSM:D_SSM + D_POOL]
        g_ssm = jax.nn.sigmoid(proj[..., D_SSM + D_POOL:D_SSM + D_POOL + D_MODEL])
        g_pool = jax.nn.sigmoid(proj[..., D_SSM + D_POOL + D_MODEL:])
        a = s5_mixer(u_ssm, ssm_lam_re[l], ssm_lam_im[l], ssm_log_dt[l], ssm_b_re[l], ssm_b_im[l],
                     ssm_c_re[l], ssm_c_im[l], ssm_d[l], ssm_w_glu[l], ssm_b_glu[l])
        b = pool_mixer(u_pool, pool_w[l], pool_scale[l])
        merged = g_ssm * (a @ w_proj_ssm[l]) + g_pool * (b @ w_proj_pool[l])
        h = h + gate1[:, None, :] * (merged @ w_out[l])

        u2 = modulate(h, norm2_g[l], shift2, scale2)
        y = hier_moe(u2, router_coarse_w[l], router_coarse_b[l], router_fine_w[l], router_fine_b[l],
                     moe_w_gate[l], moe_w_up[l], moe_w_down[l])
        h = h + gate2[:, None, :] * y
    return rms_norm(h, norm_f_g)


_drawn_inputs = setup_inputs


def setup_inputs(seed=0):
    import zlib

    import numpy as np

    out = dict(_drawn_inputs(seed))
    spreads = {}
    factors = {'b_in': 4.137,
     'ssm_lam_re': 200.0,
     'ssm_b_glu': 16.768,
     'router_coarse_b': 8.0,
     'router_fine_b': 4.077,
     'ssm_lam_im': 32.56,
     'ssm_log_dt': 43.944,
     'ssm_b_re': 41.12,
     'ssm_b_im': 43.784,
     'ssm_c_re': 36.896,
     'ssm_c_im': 38.672}
    for name, (base, spread) in spreads.items():
        noise = np.random.default_rng([zlib.crc32(name.encode()), seed]).standard_normal(out[name].shape)
        drawn = base * np.exp(spread * noise) if base else spread * noise
        out[name] = __import__('jax').numpy.asarray(drawn.astype(out[name].dtype))
    for name, factor in factors.items():
        out[name] = (out[name] * factor).astype(out[name].dtype)
    return out
```

```python
from contextlib import ExitStack

import numpy as np

import concourse.bass as bass
from concourse import mybir

ALU = mybir.AluOpType
ACT = mybir.ActivationFunctionType
AX = mybir.AxisListType
F32 = mybir.dt.float32
I32 = mybir.dt.int32
ds = bass.ds

P = 128
D = 1024
SEQ = 1024
J = SEQ // P
KD = D // P
HALF = 512
D_SSM, D_POOL = 256, 512
G, CH, ST = 16, 16, 64
WINDOWS = (2, 4, 8, 16)
NG, EPG = 4, 8
NE = NG * EPG
DE = 512
KE = DE // P
EPS = 1e-6
TS = 64
MAX_TILES = 2 * SEQ // TS + NE
RING = 3
MODC = 256

V_BMOD, V_N1, V_N2, V_BIN, V_PSC, V_BGLU, V_C, V_ROWS = 0, 48, 56, 64, 86, 90, 92, 100

A_UT = 0
A_WRING = 8192
A_BT = 11264
A_MERGED = 15360
A_WSP = A_MERGED
A_TMP = A_MERGED + 6144
A_POOL = 23552
A_COS = A_POOL + 3096
A_T = A_COS + 2064
A_CA = A_T + 2048
A_BPT = A_CA + 2304
A_SIN = A_BPT + 2048
A_WOUT = A_POOL
A_ROUTE = A_WOUT + 8192
ARENA = A_SIN + 2048


def program(nc, a):
    ctx = ExitStack()
    sems = {}

    def sem(name):
        if name not in sems:
            sems[name] = ctx.enter_context(nc.semaphore(name))
        return sems[name]

    def sb(name, shape, dt=F32):
        return ctx.enter_context(nc.sbuf_tensor(name, shape, dt))

    with ctx:
        ps = ctx.enter_context(nc.psum_tensor("ps", [P, 8, HALF], F32))
        u2_rows = nc.dram_tensor("u2_rows", [SEQ, D], F32, kind="Internal").ap()
        y_rows = nc.dram_tensor("y_rows", [(MAX_TILES + 1) * TS, D], F32, kind="Internal").ap()

        H = sb("H", [P, J * D])
        arena = sb("arena", [P, ARENA])
        work = sb("work", [P, 3456])
        gf_bc = sb("gf_bc", [P, D])
        ident = sb("ident", [P, P])
        ones = sb("ones", [P, P])
        vec = sb("vec", [P, V_ROWS])
        small = sb("small", [P, 96])
        bias_bc = sb("bias_bc", [P, 512])
        route = sb("route", [P, 208])
        tstart_i = sb("tstart_i", [P, NE + 1], I32)
        slot_tok = sb("slot_tok", [P, MAX_TILES + 1], I32)
        idx_now = sb("idx_now", [P, 1], I32)
        ypos = sb("ypos", [P, 2 * J], I32)

        def ar(off, n):
            return arena[:, off:off + n]

        h = H[:, :].rearrange("p (j d) -> p j d", j=J)
        uT = ar(A_UT, 8192).rearrange("p (k t) -> p k t", k=KD)
        wring = [ar(A_WRING + 1536 * s, 1536) for s in range(2)]
        wgate = [w[:, 0:1024].rearrange("p (k n) -> p k n", k=KD) for w in wring]
        wproj = [w[:, 1024:1536].rearrange("p (k n) -> p k n", k=4) for w in wring]
        bT = ar(A_BT, 4096).rearrange("p (g t) -> p g t", g=4)
        merged = ar(A_MERGED, 8192).rearrange("p (k t) -> p k t", k=KD)
        wsp = ar(A_WSP, 6144).rearrange("p (k n) -> p k n", k=KD)
        pool_buf = [ar(A_POOL + 1032 * i, 1032).rearrange("p (j c) -> p j c", j=J) for i in range(3)]
        cos_t = ar(A_COS, 2048).rearrange("p (g c) -> p g c", g=G)
        Xs = ar(A_COS, 2064).rearrange("p (g c) -> p g c", g=G)
        Tm = ar(A_T, 2048).rearrange("p (g n) -> p g n", g=G)
        CA = ar(A_CA, 2304).rearrange("p (g t h) -> p g t h", g=G, t=9)
        BPT = ar(A_BPT, 2048).rearrange("p (g n) -> p g n", g=G)
        yT = ar(A_BPT, 2048).rearrange("p (k t) -> p k t", k=2)
        sin_t = ar(A_SIN, 2048).rearrange("p (g c) -> p g c", g=G)
        zT = ar(A_SIN, 2048).rearrange("p (k t) -> p k t", k=2)
        modw = [ar(A_BT, 2048), ar(A_BT + 2048, 2048), ar(A_TMP, 2048)]
        modw = [m.rearrange("p (k n) -> p k n", k=KD) for m in modw]
        wout = ar(A_WOUT, 8192).rearrange("p (k n) -> p k n", k=KD)
        BP = ar(A_UT, 2048).rearrange("p (g n) -> p g n", g=G)
        ptmp = ar(A_UT + 2048, 2304)
        K0 = arena[0:CH, A_UT + 4352:A_UT + 8192].rearrange("p (g n) -> p g n", g=G)
        B_st, B_sw, C_st, C_sw = (work[:, 256 * i:256 * i + 256].rearrange("p (g h) -> p g h", g=G) for i in range(4))
        C_rows = work[:, 1024:1536].rearrange("p (s b n) -> p s b n", s=2, b=2)
        lam_rows = work[0:G, 1536:1792].rearrange("p (s n) -> p s n", s=2)
        pw_re = work[:, 1792:1936].rearrange("p (g t) -> p g t", g=G)
        pw_im = work[:, 1936:2080].rearrange("p (g t) -> p g t", g=G)
        Bb_st = work[:, 2080:2336].rearrange("p (g h) -> p g h", g=G)
        Bb_sw = work[:, 2336:2592].rearrange("p (g h) -> p g h", g=G)
        t16 = work[:, 2592:3456].rearrange("p (v g) -> p v g", g=G)
        vrows = ar(A_POOL, P)
        tab_tmp = ar(A_POOL + P, 1024).rearrange("p (g c) -> p g c", g=G)
        d_bc = bias_bc[:, 0:256]
        bu_bc = bias_bc[:, 256:512]
        U = H[:, 0:2048].rearrange("p (g j h) -> p g j h", g=G, j=J)
        V = H[:, 2048:4096].rearrange("p (g c) -> p g c", g=G)
        SA = H[:, 4096:6144].rearrange("p (g c) -> p g c", g=G)
        SB = H[:, 6144:8192].rearrange("p (g c) -> p g c", g=G)
        Ysp = H[:, 4096:6144].rearrange("p (j g h) -> p j g h", j=J, g=G)

        gate1_bc, S2_bc, A2_bc = (work[:, 1024 * i:1024 * i + 1024] for i in range(3))
        slotw = [ar(12288 * s, 12288) for s in range(RING)]
        e_gate = [w[:, 0:4096].rearrange("p (k n) -> p k n", k=KD) for w in slotw]
        e_up = [w[:, 4096:8192].rearrange("p (k n) -> p k n", k=KD) for w in slotw]
        e_down = [w[:, 8192:12288].rearrange("p (k n) -> p k n", k=KE) for w in slotw]
        x_tile = work[0:TS, 0:1024]
        y_tile = work[0:TS, 1024:2048]
        xT = work[:, 2048:2560].rearrange("p (k t) -> p k t", k=KD)
        yTe = work[:, 2560:3072].rearrange("p (k t) -> p k t", k=KD)
        silu_b = work[:, 3072:3200].rearrange("p (b t) -> p b t", b=2)
        actT = work[:, 3200:3456].rearrange("p (f t) -> p f t", f=KE)
        u2t = [ar(A_ROUTE + 1024 * i, 1024) for i in range(2)]
        u2T = [ar(A_ROUTE + 2048 + 1024 * i, 1024).rearrange("p (k t) -> p k t", k=KD) for i in range(2)]
        ROUTERW = KD * (NG + NE)
        rw = ar(A_ROUTE + 4096, ROUTERW).rearrange("p (k n) -> p k n", k=KD)
        assert A_ROUTE + 4096 + ROUTERW <= ARENA
        aux = ar(24576, 6144)


        csil = small[:, 0:8]
        A1, S1 = small[:, 8:16], small[:, 16:24]
        gate2 = small[:, 24:32]
        ssq, rstd = small[:, 32:40], small[:, 40:48]
        half_neg = small[:, 48:49]
        phase_r8 = route[:, 0:16]
        sgn = small[:, 49:50]
        nsgn = small[:, 50:51]
        pool_rcp = route[:, 16:80].rearrange("p (w j c) -> p w j c", w=4, j=J)
        iota64 = route[:, 80:144]
        m64 = route[:, 144:160]
        tokid = route[:, 160:168]
        rbias = route[:, 168:204]
        sg = sb("sg", [P, 2 * HALF])

        ycomb = [ar(1024 * i, 1024) for i in range(4)]
        gtmp, Y_flat = H[:, 6144:8192], H[:, 4096:6144]
        m_buf = [1, 2, 1, 2]
        aux_at = [0]

        def table(n):
            aux_at[0] += n
            assert aux_at[0] <= 6144
            return aux[:, aux_at[0] - n:aux_at[0]]

        def per_tile(n):
            return table(J * n).rearrange("p (j n) -> p j n", j=J)

        later = table(P)
        L = per_tile(NG + NE)
        rsc = table(8 * J).rearrange("p (v j) -> p v j", j=J)
        falling = table(EPG)
        g_hot, cdiff, cexp = per_tile(NG), per_tile(NG), per_tile(NG)
        fsel4 = per_tile(NE).rearrange("p j (i g) -> p j i g", g=NG)
        fsel, fdiff = per_tile(EPG), table(J)
        hot = [per_tile(EPG), per_tile(EPG)]
        wpick = table(2 * J).rearrange("p (k j) -> p k j", k=2)
        pick = [per_tile(NE), per_tile(NE)]
        M_all, M_before = table(J * NE), table(J * NE)
        M3, Mb3 = (m.rearrange("p (j e) -> p j e", j=J) for m in (M_all, M_before))
        Mp3 = per_tile(NE)
        M_total, ntile, tstart = table(NE), table(NE), table(NE + 1)
        cmp_t = table(16 * NE).rearrange("p (e m) -> p e m", m=16)
        cmp_r = table(15 * 2 * J).rearrange("p (e m) -> p e m", m=15)
        fl = table(2 * J)
        rk, hi = (table(2 * J).rearrange("p (k j) -> p k j", k=2) for _ in range(2))
        oh_lo = table(2 * J * TS).rearrange("p (i s) -> p i s", s=TS)
        oh_hi = table(2 * J * MAX_TILES).rearrange("p (i s) -> p i s", s=MAX_TILES)
        wsave = small[:, 56:72].rearrange("p (k j) -> p k j", k=2)

        x_v = a["x"].rearrange("b (c j) d -> (b c) j d", j=J)
        out_v = a["out"].rearrange("b (c j) d -> (b c) j d", j=J)
        u2_v = u2_rows.rearrange("(c j) d -> c j d", j=J)
        wmod_v = a["w_mod"].rearrange("l (k p) n -> p (l k) n", p=P)
        win_v = a["w_in"].rearrange("l (k p) n -> p (l k) n", p=P)
        wps_v = a["w_proj_ssm"].rearrange("l (k p) n -> p (l k) n", p=P)
        wpp_v = a["w_proj_pool"].rearrange("l (k p) n -> p (l k) n", p=P)
        wout_v = a["w_out"].rearrange("l (k p) n -> p (l k) n", p=P)
        eg_v = a["moe_w_gate"].rearrange("l e (k p) n -> (l e) p k n", p=P)
        eu_v = a["moe_w_up"].rearrange("l e (k p) n -> (l e) p k n", p=P)
        ed_v = a["moe_w_down"].rearrange("l e (k p) n -> (l e) p k n", p=P)
        GP0 = D_SSM + D_POOL + D
        GS0 = D_SSM + D_POOL

        def rows128(ap):
            return ap.rearrange("l (r n) -> (l r) n", n=P)

        def bcast(ap, n):
            return ap.rearrange("(o n) -> o n", o=1).to_broadcast([P, n]) if len(ap.shape) == 1 else ap.to_broadcast([P, n])

        wglu = sb("wglu", [P, 2 * D_SSM])[:, :].rearrange("p (k n) -> p k n", k=2)
        wpool = sb("wpool", [P, 4 * P])[:, :].rearrange("p (k n) -> p k n", k=4)
        NMOD1 = 2 * D // MODC
        NMOD = 6 * D // MODC
        FREE_NE = NE - RING

        def stand(eng, name):
            eng.sem_inc(sem("stood_" + name), 1)

        block = ctx.enter_context(nc.Block())

        @block.sync
        def _(sp):
            def load(dst, src, name):
                sp.dma_start(dst, src).then_inc(sem(name), 16)

            at = 0
            for name in ("b_mod", "norm1_g", "norm2_g", "b_in", "pool_scale", "ssm_b_glu", "c"):
                src = rows128(a[name])
                load(vrows[at:at + src.shape[0], :], src, "vrows_in")
                at += src.shape[0]
            for s, name in enumerate(("ssm_lam_re", "ssm_lam_im")):
                for half in range(2):
                    load(lam_rows[:, s, ST * half:ST * half + ST],
                         a[name].rearrange("l g p -> (l g) p"), "ssm_in")
            load(t16[:, 0, :], bcast(a["ssm_log_dt"], G), "ssm_in")
            for s, (first, second) in enumerate((("re", "im"), ("im", "re"))):
                for half, part in enumerate((first, second)):
                    load((B_st, B_sw)[s][ST * half:ST * half + ST, :, :],
                         a["ssm_b_" + part].rearrange("l g p h -> p (l g) h"), "ssm_in")
                    load(C_rows[:, s, :, ST * half:ST * half + ST],
                         a["ssm_c_" + part].rearrange("l (b g) h p -> (l g h) b p", b=2), "ssm_in")
            for q in range(4):
                load(h[:, 2 * q:2 * q + 2, :], x_v[:, 2 * q:2 * q + 2, :], f"x_in{q}")
            for i in range(NMOD1):
                if i >= RING:
                    sp.wait_ge(sem("modw_used"), i - RING + 1)
                load(modw[i % RING], wmod_v[:, :, MODC * i:MODC * i + MODC], f"modw_in{i % RING}")
            load(wsp[:, :, 0:D_SSM], win_v[:, :, 0:D_SSM], "wsp_in")
            load(wsp[:, :, D_SSM:768], win_v[:, :, D_SSM:768], "wsp_pool_in")
            load(d_bc, bcast(a["ssm_d"], D_SSM), "bias_in")
            load(bu_bc, bcast(a["b_in"][:, 0:D_SSM], D_SSM), "bias_in")
            for i in range(NMOD1, NMOD):
                sp.wait_ge(sem("modw_used"), i - RING + 1)
                load(modw[i % RING], wmod_v[:, :, MODC * i:MODC * i + MODC], f"modw_in{i % RING}")
            load(wglu, a["ssm_w_glu"].rearrange("l (k p) n -> p (l k) n", p=P), "wglu_in")
            load(wpool, a["pool_w"].rearrange("l g c d -> c (l g) d"), "wpool_in")
            load(rbias[:, 0:NG], bcast(a["router_coarse_b"], NG), "rbias_in")
            load(rbias[:, NG:NG + NE], bcast(a["router_fine_b"], NE), "rbias_in")
            def gate_weights(item, step2, s, wait):
                proj_v, nk, first = (wps_v, 2, GS0) if step2 else (wpp_v, 4, GP0)
                if wait is not None:
                    sp.wait_ge(sem("gate_mm"), wait)
                sp.dma_start(wgate[s], win_v[:, :, ds(item * 128 + (first - step2 * D), P)]).then_inc(sem(f"wring_in{s}"), 16)
                sp.dma_start(wproj[s][:, 0:nk, :], proj_v[:, :, ds(item * 128 - step2 * D, P)]).then_inc(sem(f"wproj_in{s}"), 16)

            for s in range(2):
                gate_weights(s, 0, s, None)
            with sp.Fori(1, KD // 2) as n:
                for s in range(2):
                    gate_weights(n * 2 + s, 0, s, n * 4 + (2 * s - 2))
            with sp.Fori(KD // 2, KD) as n:
                for s in range(2):
                    gate_weights(n * 2 + s, 1, s, n * 4 + (2 * s - 2))
            sp.wait_ge(sem("z_done"), 4)
            load(wout, wout_v, "wout_in")
            load(h, x_v, "x_again")
            load(u2t[0], bcast(a["norm2_g"], D), "n2_in")
            sp.wait_ge(sem("gate_mm"), 4 * KD)
            load(rw[:, :, 0:NG], a["router_coarse_w"].rearrange("l (k p) n -> p (l k) n", p=P), "rw_in")
            load(rw[:, :, NG:NG + NE], a["router_fine_w"].rearrange("l (k p) n -> p (l k) n", p=P), "rw_in")

            def load_expert(e, s):
                sp.dma_start(e_gate[s], eg_v[ds(e, 1)].rearrange("e p k n -> p (e k) n")).then_inc(sem(f"gateup_in{s}"), 16)
                sp.dma_start(e_up[s], eu_v[ds(e, 1)].rearrange("e p k n -> p (e k) n")).then_inc(sem(f"gateup_in{s}"), 16)
                sp.dma_start(e_down[s], ed_v[ds(e, 1)].rearrange("e p k n -> p (e k) n")).then_inc(sem(f"down_in{s}"), 16)

            load_expert(0, 0)
            sp.wait_ge(sem("mod_rows_done"), 1)
            sp.wait_ge(sem("y_rows_out"), 16)
            load(gf_bc[:, :], bcast(a["norm_f_g"], D), "gf_in")
            sp.wait_ge(sem("wout_done"), J)
            load_expert(1, 1)
            sp.wait_ge(sem("routed"), 1)
            for s in range(2):
                sp.wait_ge(sem(f"u2_out{s}"), 16 * (J // 2))
            load_expert(2, 2)

            def next_expert(e, s):
                last = sp.value_load(tstart_i[0:1, ds(e - (RING - 1), 1)], min_val=1, max_val=MAX_TILES)
                sp.wait_ge(sem("tiles_done"), last)
                load_expert(e, s)

            with sp.Fori(1, NE // RING) as n:
                for s in range(RING):
                    next_expert(n * RING + s, s)
            for e in range(NE // RING * RING, NE):
                next_expert(e, e % RING)

        @block.gpsimd
        def _(pool):
            own = [0]

            def step(ins):
                own[0] += 1
                ins.then_inc(sem("pool_step"), 1)
                pool.wait_ge(sem("pool_step"), own[0])

            gp = nc.gpsimd
            gp.memset(ident[:, :], 0.0)
            gp.memset(ones[:, :], 1.0)
            gp.memset(half_neg, -0.5)
            gp.memset(nsgn, 1.0)
            step(gp.memset(sgn, -1.0))
            step(gp.memset(nsgn[ST:P, :], -1.0))
            step(gp.memset(sgn[ST:P, :], 1.0))
            gp.affine_select(out=ident[:, :], in_=ident[:, :], compare_op=ALU.not_equal, fill=1.0,
                             base=0, pattern=[[-1, P]], channel_multiplier=1).then_inc(sem("ident_done"), 1)
            gp.memset(K0, 0.0).then_inc(sem("k0_zero"), 1)
            gp.iota(iota64, [[1, TS]], base=0, channel_multiplier=0, allow_small_or_imprecise_dtypes=True)
            gp.iota(m64, [[TS, 16]], base=0, channel_multiplier=0, allow_small_or_imprecise_dtypes=True)
            gp.iota(tokid, [[1, J]], base=0, channel_multiplier=J, allow_small_or_imprecise_dtypes=True)
            for w in range(4):
                gp.iota(pool_rcp[:, w], [[1, J], [J, 2]], base=1, channel_multiplier=0,
                        allow_small_or_imprecise_dtypes=True)
            step(gp.memset(slot_tok[:, :], 0))
            for w in range(4):
                last = gp.tensor_scalar(pool_rcp[:, w], pool_rcp[:, w], float(WINDOWS[w]), None, ALU.min)
            last.then_inc(sem("consts_done"), 1)

            pool.wait_ge(sem("ms1_done"), 1)
            gp.tensor_tensor(rstd, rstd, half_neg.to_broadcast([P, J]), ALU.pow).then_inc(sem("rstd1_done"), 1)


            pool.wait_ge(sem("in_evac"), 12)
            gp.tensor_tensor(SA, SA, cos_t, ALU.mult)
            step(gp.tensor_tensor(SB, SB, sin_t, ALU.mult))
            gp.tensor_tensor(SA, SA, SB, ALU.subtract).then_inc(sem("turned"), 1)
            gp.memset(gf_bc[:, :], 0.0).then_inc(sem("zeros_ready"), 1)
            pool.wait_ge(sem("z_swapped"), 2)
            step(gp.tensor_tensor(SB, SB, cos_t, ALU.mult))
            step(gp.tensor_tensor(SA, SA, sin_t, ALU.mult))
            step(gp.memset(Xs[:, :, 0:1], 0.0))
            gp.tensor_tensor(Xs[:, :, 1:P + 1], SB, SA, ALU.add).then_inc(sem("state_done"), 1)

            for j in range(J):
                pool.wait_ge(sem("ssq2_done"), j + 1)
                step(gp.tensor_scalar(rstd[:, j:j + 1], ssq[:, j:j + 1], 1.0 / D, EPS, ALU.mult, ALU.add))
                gp.tensor_tensor(rstd[:, j:j + 1], rstd[:, j:j + 1], half_neg, ALU.pow).then_inc(sem("rstd2_done"), 1)

            pool.wait_ge(sem("wout_done"), J)
            step(gp.memset(later, 1.0))
            gp.affine_select(out=later, in_=later, compare_op=ALU.is_gt, fill=0.0,
                             base=0, pattern=[[1, P]], channel_multiplier=-1).then_inc(sem("later_done"), 1)
            pool.wait_ge(sem("routed"), 1)
            for s in range(2):
                pool.wait_ge(sem(f"u2_out{s}"), 16 * (J // 2))
            gp.memset(idx_now[:, :], 0).then_inc(sem("x_rows_used"), 1)
            n_tiles = pool.value_load(tstart_i[0:1, NE:NE + 1], min_val=NE, max_val=MAX_TILES)
            with pool.Fori(0, n_tiles + 1) as g:
                pool.wait_ge(sem("x_rows_used"), g + 1)
                gp.tensor_copy(idx_now[0:TS, :], slot_tok[0:TS, ds(g, 1)]).then_inc(sem("idx_ready"), 1)
                pool.wait_ge(sem("idx_ready"), g + 1)
                stand(pool, "pool")
                gp.indirect_dma_start(x_tile, None, u2_rows, bass.IndirectOffsetOnAxis(ap=idx_now[0:TS, 0:1], axis=0)).then_inc(sem("x_rows_in"), 16)

            pool.wait_ge(sem("y_rows_out"), n_tiles * 16 + 32)
            stand(pool, "pool")
            for t in range(J + 1):
                if t < J:
                    if t >= 2:
                        pool.wait_ge(sem("combined"), t - 1)
                    for k in range(2):
                        n = (2 * t + k) % 4
                        gp.indirect_dma_start(ycomb[n], None, y_rows, bass.IndirectOffsetOnAxis(
                            ap=ypos[:, J * k + t:J * k + t + 1], axis=0)).then_inc(sem(f"ycomb_in{n}"), 16)
                if t:
                    j = t - 1
                    pool.wait_ge(sem("ssq3_done"), j + 1)
                    step(gp.tensor_scalar(rstd[:, j:j + 1], ssq[:, j:j + 1], 1.0 / D, EPS, ALU.mult, ALU.add))
                    gp.tensor_tensor(rstd[:, j:j + 1], rstd[:, j:j + 1], half_neg, ALU.pow).then_inc(sem("rstd3_done"), 1)

        @block.tensor
        def _(pe):
            mm, tp = nc.tensor.matmul, nc.tensor.transpose

            def group(out, pairs):
                for i, (lhsT, rhs) in enumerate(pairs):
                    last = mm(out, lhsT, rhs, start=(i == 0), stop=(i == len(pairs) - 1))
                return last

            pe.wait_ge(sem("ident_done"), 1)
            pe.wait_ge(sem("vrows_in"), 16 * 7)
            tp(ps[:, 0, 0:V_ROWS], vrows[0:V_ROWS, :], ident[0:V_ROWS, 0:V_ROWS]).then_inc(sem("vec_mm"), 1)
            pe.wait_ge(sem("ssm_in"), 16 * 13)
            for s in range(2):
                tp(ps[:, 2, G * s:G * s + G], lam_rows[:, s, :], ident[0:G, 0:G])
            for s in range(2):
                for b in range(2):
                    last = tp(ps[:, 1, 256 * s + 128 * b:256 * s + 128 * b + 128], C_rows[:, s, b, :], ident[:, :])
            last.then_inc(sem("param_mm"), 1)

            def mod_columns(first, last_chunk, bank):
                for i in range(first, last_chunk):
                    pe.wait_ge(sem(f"modw_in{i % RING}"), 16 * (i // RING + 1))
                    for b in range(2):
                        last = group(ps[:, bank, 2 * i + b:2 * i + b + 1],
                                     [(modw[i % RING][:, k, 128 * b:128 * b + 128], csil[:, k:k + 1]) for k in range(KD)])
                    last.then_inc(sem("modw_used"), 1)

            pe.wait_ge(sem("csil_done"), 1)
            mod_columns(0, NMOD1, 6)

            pe.wait_ge(sem("tables_done"), 1)
            for g in range(G):
                last = mm(ps[0:CH, 2 + g // 4, 128 * (g % 4):128 * (g % 4) + 128], Bb_st[:, g, :], CA[:, g, 0:8, :],
                          start=True, stop=True)
            last.then_inc(sem("k0_mm"), 1)
            pe.wait_ge(sem("k0_evac"), 4)
            for g in range(G):
                last = tp(ps[:, 2 + g // 4, 128 * (g % 4):128 * (g % 4) + 128], BP[:, g, :], ident[:, :])
            last.then_inc(sem("bp_mm"), 1)

            pe.wait_ge(sem("bpt_evac"), 4)
            for half in range(2):
                pe.wait_ge(sem("xn_done"), 4 * half + 4)
                for k in range(KD):
                    n = KD * half + k
                    if n >= 4:
                        pe.wait_ge(sem(("ut_act", "ut_dve")[k % 2]), (n - 4) // 2 + 1)
                    for j in range(4):
                        last = tp(ps[:, n % 4, 128 * j:128 * j + 128], h[:, 4 * half + j, 128 * k:128 * k + 128], ident[:, :])
                    last.then_inc(sem("ut_mm"), 1)

            pe.wait_ge(sem("ut_act"), 8)
            pe.wait_ge(sem("ut_dve"), 8)
            pe.wait_ge(sem("wsp_in"), 16)
            for j in range(J):
                group(ps[:, j // 2, 256 * (j % 2):256 * (j % 2) + 256],
                      [(uT[:, k, 128 * j:128 * j + 128], wsp[:, k, 0:D_SSM]) for k in range(KD)]).then_inc(sem("u_mm"), 1)

            def pool_project(gi):
                if gi >= 2:
                    pe.wait_ge(sem("gate_bank_free"), 2 * (gi - 1))
                col = D_SSM + 128 * (3 - gi)
                for half in range(2):
                    group(ps[:, 4 + 2 * (gi % 2) + half, :],
                          [(wsp[:, k, col:col + 128], uT[:, k, HALF * half:HALF * half + HALF]) for k in range(KD)]).then_inc(sem("px_mm"), 1)

            def pool_mix(gi):
                pe.wait_ge(sem("m_ready"), gi + 1)
                if gi >= 2:
                    pe.wait_ge(sem("bt_evac"), 2 * (gi - 1))
                for half in range(2):
                    m = pool_buf[m_buf[gi]][:, 4 * half:4 * half + 4, 1:P + 1]
                    last = mm(ps[:, 2 * (gi % 2) + half, :], wpool[:, 3 - gi, :], m, start=True, stop=True)
                last.then_inc(sem("pmix_mm"), 1)

            mod_columns(NMOD1, 2 * NMOD1, 7)
            pe.wait_ge(sem("wsp_pool_in"), 16)
            pool_project(0)
            pe.wait_ge(sem("u_evac"), 4)
            for g in range(G):
                last = tp(ps[:, g // 4, 128 * (g % 4):128 * (g % 4) + 128], U[:, g].rearrange("p j h -> p (j h)"), ident[:, :])
                if g % 4 == 3:
                    last.then_inc(sem("v_mm"), 1)
            mod_columns(2 * NMOD1, NMOD, 7)
            pe.wait_ge(sem("mod2_done"), 1)
            pool_project(1)
            pe.wait_ge(sem("v_evac"), 4)
            for g in range(G):
                last = mm(ps[:, g // 4, 128 * (g % 4):128 * (g % 4) + 128], BPT[:, g, :], V[:, g, :], start=True, stop=True)
                if g % 4 == 3:
                    last.then_inc(sem("in_mm"), 1)
            pool_project(2)
            pe.wait_ge(sem("wpool_in"), 16)
            pe.wait_ge(sem("in_evac"), 12)
            pool_mix(0)
            pool_project(3)
            pool_mix(1)
            pool_mix(2)
            pool_mix(3)
            pe.wait_ge(sem("bt_evac"), 8)

            def gate_pair(n, step2):
                rhs, nk = (zT, 2) if step2 else (bT, 4)
                for s in range(2):
                    pe.wait_ge(sem(f"wring_in{s}"), n * 16 + 16 * (1 + 4 * step2))
                    pe.wait_ge(sem(f"wproj_in{s}"), n * 16 + 16 * (1 + 4 * step2))
                    for half in range(2):
                        it = n * 4 + (2 * s + half + 16 * step2)
                        pe.wait_ge(sem("gate_bank_free"), it + 7)
                        pe.wait_ge(sem("mul_done"), it + 1)
                        cols = slice(HALF * half, HALF * half + HALF)
                        group(ps[:, 5 + 2 * half, :], [(wproj[s][:, k, :], rhs[:, k, cols]) for k in range(nk)]).then_inc(sem("proj_mm"), 1)
                        group(ps[:, 4 + 2 * half, :], [(wgate[s][:, k, :], uT[:, k, cols]) for k in range(KD)]).then_inc(sem("gate_mm"), 1)

            with pe.Fori(0, 2) as n:
                gate_pair(n, 0)
            gate_pair(2, 0)
            pe.wait_ge(sem("state_done"), 1)
            pe.wait_ge(sem("t_in"), 16 * J)
            for g in range(G):
                last = group(ps[:, g // 4, 128 * (g % 4):128 * (g % 4) + 128],
                             [(V[:, g, :], Tm[:, g, :]), (Xs[:, g, 0:P], CA[:, g, 1:9, :])])
                if g % 4 == 3:
                    last.then_inc(sem("y_mm"), 1)
            gate_pair(3, 0)
            pe.wait_ge(sem("gelu_done"), 1)
            for cb in range(2):
                for half in range(2):
                    for j in range(4):
                        last = tp(ps[:, 2 * cb + half, 128 * j:128 * j + 128],
                                  Ysp[:, 4 * half + j, 8 * cb:8 * cb + 8].rearrange("p g h -> p (g h)"), ident[:, :])
                    last.then_inc(sem("yt_mm"), 1)
            pe.wait_ge(sem("yt_evac"), 4)
            pe.wait_ge(sem("wglu_in"), 16)
            for ob in range(2):
                for half in range(2):
                    group(ps[:, 2 * ob + half, :], [(wglu[:, k, 128 * ob:128 * ob + 128], yT[:, k, HALF * half:HALF * half + HALF])
                                                   for k in range(2)]).then_inc(sem("glu_mm"), 1)
            pe.wait_ge(sem("z_done"), 4)
            with pe.Fori(0, KD // 2) as n:
                gate_pair(n, 1)

            pe.wait_ge(sem("mul_done"), 4 * KD + 2)
            for q in range(6):
                last = mm(ps[:, q, :], ones[:, :], work[:, HALF * q:HALF * q + HALF], start=True, stop=True)
            last.then_inc(sem("mod_mm"), 1)
            pe.wait_ge(sem("mod_rows_done"), 1)
            pe.wait_ge(sem("wout_in"), 16)
            pe.wait_ge(sem("rw_in"), 32)
            for t in range(J + 2):
                if t < J:
                    if t >= 2:
                        pe.wait_ge(sem("h_psum_read"), 2 * (t - 1))
                    for half in range(2):
                        last = group(ps[:, 2 * (t % 2) + half, :],
                                     [(merged[:, k, 128 * t:128 * t + 128], wout[:, k, HALF * half:HALF * half + HALF]) for k in range(KD)])
                    last.then_inc(sem("wout_done"), 1)
                if 1 <= t <= J:
                    pe.wait_ge(sem("u2_done"), t)
                    if t >= 2:
                        pe.wait_ge(sem("u2t_evac"), 2 * (t - 1))
                    for k in range(KD):
                        last = tp(ps[:, 4 + k // 4, 128 * (k % 4):128 * (k % 4) + 128], u2t[(t - 1) % 2][:, 128 * k:128 * k + 128], ident[:, :])
                    last.then_inc(sem("u2t_mm"), 1)
                if t >= 2:
                    j = t - 2
                    pe.wait_ge(sem("u2t_evac"), 2 * (j + 1))
                    group(ps[:, 6, (NG + NE) * j:(NG + NE) * (j + 1)],
                          [(u2T[j % 2][:, k, :], rw[:, k, :]) for k in range(KD)]).then_inc(sem("router_mm"), 1)

            pe.wait_ge(sem("picks_done"), 1)
            pe.wait_ge(sem("later_done"), 1)
            group(ps[:, 7, 0:J * NE], [(later, M_all), (ones[:, :], M_before)])
            mm(ps[:, 7, J * NE:J * NE + NE], ones[:, :], M_total, start=True, stop=True).then_inc(sem("rank_mm"), 1)
            pe.wait_ge(sem("onehots_done"), 1)
            group(ps[0:TS, 0, 0:MAX_TILES], [(oh_lo[:, i, :], oh_hi[:, i, :]) for i in range(2 * J)]).then_inc(sem("slot_mm"), 1)

            def transpose_x(g1):
                pe.wait_ge(sem("x_rows_in"), g1 * 16)
                stand(pe, "pe")
                for k in range(KD):
                    last = tp(ps[:, 3, TS * k:TS * k + TS], x_tile[:, 128 * k:128 * k + 128], ident[0:TS, 0:TS])
                last.then_inc(sem("x_rows_used"), 1)

            def transpose_y(g):
                pe.wait_ge(sem("yt_ready"), g + 1)
                stand(pe, "pe")
                for k in range(KD):
                    last = tp(ps[0:TS, 4 + k // 4, 128 * (k % 4):128 * (k % 4) + 128], yTe[:, k, :], ident[:, :])
                last.then_inc(sem("y_mm2"), 1)

            def expert(e, s, n):
                t0 = pe.value_load(tstart_i[0:1, ds(e, 1)], min_val=0, max_val=MAX_TILES)
                t1 = pe.value_load(tstart_i[0:1, ds(e + 1, 1)], min_val=1, max_val=MAX_TILES)
                pe.wait_ge(sem(f"gateup_in{s}"), n * 32 + 32)
                pe.wait_ge(sem(f"down_in{s}"), n * 16 + 16)
                stand(pe, "pe")
                with pe.Fori(t0, t1) as g:
                    pe.wait_ge(sem("xt_ready"), g + 1)

                    def gate_up(f):
                        for w, at in ((e_gate[s], 0), (e_up[s], TS)):
                            last = group(ps[:, f % 2, at:at + TS], [(w[:, k, 128 * f:128 * f + 128], xT[:, k, :]) for k in range(KD)])
                        last.then_inc(sem("gu_mm"), 1)

                    def down(f):
                        pe.wait_ge(sem("act_ready"), g * KE + (f + 1))
                        for b in range(KD):
                            last = mm(ps[:, 2, TS * b:TS * b + TS], e_down[s][:, f, 128 * b:128 * b + 128], actT[:, f, :],
                                      start=(f == 0 and b == 0), stop=(f == KE - 1), skip_group_check=True)
                        return last

                    gate_up(0)
                    transpose_y(g)
                    gate_up(1)
                    down(0)
                    gate_up(2)
                    down(1)
                    gate_up(3)
                    down(2)
                    transpose_x(g + 2)
                    down(3).then_inc(sem("tiles_done"), 1)

            pe.wait_ge(sem("routed"), 1)
            n_tiles = pe.value_load(tstart_i[0:1, NE:NE + 1], min_val=NE, max_val=MAX_TILES)
            transpose_x(1)
            with pe.Fori(0, NE // RING) as n:
                for s in range(RING):
                    expert(n * RING + s, s, n)
            for e in range(NE // RING * RING, NE):
                expert(e, e % RING, NE // RING)
            transpose_y(n_tiles)

        @block.scalar
        def _(act):
            fn = nc.scalar.activation

            act.wait_ge(sem("vec_done"), 1)
            fn(csil, vec[:, V_C:V_C + 8], ACT.Sigmoid).then_inc(sem("csig_done"), 1)
            for j in range(J):
                act.wait_ge(sem(f"x_in{j // 2}"), 16)
                if j:
                    act.wait_ge(sem("ssq1_done"), j)
                fn(sg[:, :], h[:, j, :], ACT.Square, accum_out=ssq[:, j:j + 1]).then_inc(sem("ssq1_done"), 1)

            act.wait_ge(sem("k0_mm"), 1)
            act.wait_ge(sem("k0_zero"), 1)
            for q in range(4):
                fn(K0[:, 4 * q:4 * q + 4, 112:240], ps[0:CH, 2 + q, :].rearrange("p (g n) -> p g n", g=4), ACT.Copy).then_inc(sem("k0_evac"), 1)
            act.wait_ge(sem("k0_evac"), 4)
            for j1 in range(J):
                act.dma_start(Tm[CH * j1:CH * j1 + CH, :, :], K0[:, :, 112 - CH * j1:240 - CH * j1]).then_inc(sem("t_in"), 16)
            act.wait_ge(sem("bp_mm"), 1)
            for q in range(4):
                fn(BPT[:, 4 * q:4 * q + 4, :], ps[:, 2 + q, :].rearrange("p (g n) -> p g n", g=4), ACT.Copy).then_inc(sem("bpt_evac"), 1)

            act.wait_ge(sem("mod1_done"), 1)
            act.wait_ge(sem("t_in"), 16 * J)
            for half in range(2):
                for k in range(0, KD, 2):
                    n = KD * half + k
                    act.wait_ge(sem("ut_mm"), n + 1)
                    fn(uT[:, k, HALF * half:HALF * half + HALF], ps[:, n % 4, :], ACT.Identity,
                       scale=A1[:, k:k + 1], bias=S1[:, k:k + 1]).then_inc(sem("ut_act"), 1)

            def pool_in(gi):
                if gi:
                    act.wait_ge(sem("m_ready"), gi)
                else:
                    act.wait_ge(sem("pads_done"), 1)
                for half in range(2):
                    act.wait_ge(sem("px_mm"), 2 * gi + half + 1)
                    fn(pool_buf[0][:, 4 * half:4 * half + 4, 1:P + 1],
                       ps[:, 4 + 2 * (gi % 2) + half, :].rearrange("p (j c) -> p j c", j=4), ACT.Identity,
                       bias=vec[:, V_BIN + 2 + 3 - gi:V_BIN + 3 + 3 - gi]).then_inc(sem("gate_bank_free"), 1)

            def pool_out(gi):
                act.wait_ge(sem("pmix_mm"), gi + 1)
                if gi == 0:
                    act.wait_ge(sem("modw_used"), NMOD)
                for half in range(2):
                    fn(bT[:, 3 - gi, HALF * half:HALF * half + HALF], ps[:, 2 * (gi % 2) + half, :], ACT.Copy,
                       scale=vec[:, V_PSC + 3 - gi:V_PSC + 4 - gi]).then_inc(sem("bt_evac"), 1)

            pool_in(0)
            for q in range(4):
                act.wait_ge(sem("v_mm"), q + 1)
                fn(V[:, 4 * q:4 * q + 4, :], ps[:, q, :].rearrange("p (g n) -> p g n", g=4), ACT.Copy).then_inc(sem("v_evac"), 1)
            pool_in(1)
            for q in range(4):
                act.wait_ge(sem("in_mm"), q + 1)
                src = ps[:, q, :].rearrange("p (g n) -> p g n", g=4)
                dst = slice(4 * q, 4 * q + 4)
                fn(SA[:, dst, :], src, ACT.Copy).then_inc(sem("in_evac"), 1)
                fn(SB[0:ST, dst, :], src[ST:P], ACT.Copy).then_inc(sem("in_evac"), 1)
                fn(SB[ST:P, dst, :], src[0:ST], ACT.Copy).then_inc(sem("in_evac"), 1)
            pool_in(2)
            pool_out(0)
            pool_in(3)
            for gi in range(1, 4):
                pool_out(gi)

            def gate_pair(n, step2):
                for s in range(2):
                    for half in range(2):
                        it = n * 4 + (2 * s + half + 16 * step2)
                        act.wait_ge(sem("gate_mm"), it + 1)
                        act.wait_ge(sem("mul_done"), it + 1)
                        stand(act, "act")
                        col = V_BIN + (6 if step2 else 14) + s
                        fn(sg[:, HALF * half:HALF * half + HALF], ps[:, 4 + 2 * half, :], ACT.Sigmoid,
                           bias=vec[:, ds(n * 2 + col, 1)] if not isinstance(n, int) else vec[:, n * 2 + col:n * 2 + col + 1]).then_inc(sem("gate_bank_free"), 1)

            spare = y_rows[(NE + 1) * TS:, :].rearrange("(r p) d -> p r d", p=P)
            act.wait_ge(sem("zeros_ready"), 1)
            act.dma_start(spare, gf_bc[:, :].unsqueeze(1).to_broadcast([P, spare.shape[1], D])).then_inc(sem("y_rows_out"), 16)

            with act.Fori(0, 2) as n:
                gate_pair(n, 0)
            gate_pair(2, 0)
            act.wait_ge(sem("y_evac"), 1)
            fn(gtmp, Y_flat, ACT.Square).then_inc(sem("ysq_done"), 1)
            act.wait_ge(sem("gelu_arg"), 1)
            fn(gtmp, gtmp, ACT.Sigmoid, scale=2.0 * (2.0 / np.pi) ** 0.5).then_inc(sem("gelu_sig"), 1)
            gate_pair(3, 0)
            for cb in range(2):
                for half in range(2):
                    act.wait_ge(sem("yt_mm"), 2 * cb + half + 1)
                    fn(yT[:, cb, HALF * half:HALF * half + HALF], ps[:, 2 * cb + half, :], ACT.Copy).then_inc(sem("yt_evac"), 1)
            for ob in range(2):
                for half in range(2):
                    act.wait_ge(sem("glu_mm"), 2 * ob + half + 1)
                    act.wait_ge(sem("mul_done"), 2 * KD + half + 1)
                    if ob:
                        act.wait_ge(sem("z_done"), half + 1)
                    fn(sg[:, HALF * half:HALF * half + HALF], ps[:, 2 * ob + half, :], ACT.Sigmoid,
                       bias=vec[:, V_BGLU + ob:V_BGLU + ob + 1]).then_inc(sem("glu_sig"), 1)
            act.wait_ge(sem("z_done"), 4)
            with act.Fori(0, KD // 2) as n:
                gate_pair(n, 1)

            def second_norm(j):
                act.wait_ge(sem("h_done"), j + 1)
                if j:
                    act.wait_ge(sem("ssq2_done"), j)
                fn(sg[:, :], h[:, j, :], ACT.Square, accum_out=ssq[:, j:j + 1]).then_inc(sem("ssq2_done"), 1)

            def rows_out(j):
                act.wait_ge(sem("u2_done"), j + 1)
                act.dma_start(u2_v[:, j, :], u2t[j % 2]).then_inc(sem(f"u2_out{j % 2}"), 16)
                act.wait_ge(sem("u2t_mm"), j + 1)
                if j >= 2:
                    act.wait_ge(sem("router_mm"), j - 1)
                for b in range(2):
                    fn(u2T[j % 2][:, 4 * b:4 * b + 4, :], ps[:, 4 + b, :].rearrange("p (k t) -> p k t", k=4), ACT.Copy).then_inc(sem("u2t_evac"), 1)

            for j in range(J + 1):
                if j < J:
                    second_norm(j)
                if j:
                    rows_out(j - 1)

            act.wait_ge(sem("coarse_diff"), 1)
            fn(cexp, cdiff, ACT.Exp).then_inc(sem("coarse_exp"), 1)
            act.wait_ge(sem("fine_diff"), 1)
            fn(wpick[:, 0, :], fdiff, ACT.Sigmoid, scale=-1.0)
            fn(wpick[:, 1, :], fdiff, ACT.Sigmoid).then_inc(sem("fine_sig"), 1)

            act.wait_ge(sem("routed"), 1)
            n_tiles = act.value_load(tstart_i[0:1, NE:NE + 1], min_val=NE, max_val=MAX_TILES)

            def rows_to_dram(g):
                act.wait_ge(sem("y_mm2"), g + 1)
                act.wait_ge(sem("y_rows_out"), g * 16 + 16)
                fn(y_tile[:, 0:HALF], ps[0:TS, 4, :], ACT.Copy).then_inc(sem("y_copy_act"), 1)
                act.wait_ge(sem("y_copy_act"), g + 1)
                act.wait_ge(sem("y_copy_dve"), g + 1)
                act.dma_start(y_rows[ds(g * TS, TS), :], y_tile).then_inc(sem("y_rows_out"), 16)

            with act.Fori(0, n_tiles) as g:
                for f in range(KE):
                    act.wait_ge(sem("gu_mm"), g * KE + (f + 1))
                    if f >= 2:
                        act.wait_ge(sem("act_ready"), g * KE + (f - 1))
                    fn(silu_b[:, f % 2, :], ps[:, f % 2, 0:TS], ACT.Silu).then_inc(sem("silu_done"), 1)
                    if f == 0:
                        rows_to_dram(g)
            rows_to_dram(n_tiles)

            for j in range(J):
                act.wait_ge(sem("combined"), j + 1)
                if j:
                    act.wait_ge(sem("ssq3_done"), j)
                fn(sg[:, :], h[:, j, :], ACT.Square, accum_out=ssq[:, j:j + 1]).then_inc(sem("ssq3_done"), 1)
                if j:
                    act.wait_ge(sem("out_done"), j)
                    act.dma_start(out_v[:, j - 1, :], h[:, j - 1, :]).then_inc(sem("out_sent"), 16)
            act.wait_ge(sem("out_done"), J)
            act.dma_start(out_v[:, J - 1, :], h[:, J - 1, :]).then_inc(sem("out_sent"), 16)
            act.wait_ge(sem("out_sent"), 16 * J)

        @block.vector
        def _(dve):
            v = nc.vector
            own = [0]

            def step(ins):
                own[0] += 1
                ins.then_inc(sem("dve_step"), 1)
                dve.wait_ge(sem("dve_step"), own[0])

            def tt(out, in0, in1, op):
                return v.tensor_tensor(out, in0, in1, op)

            def bc(ap, axis, n):
                ap = ap.unsqueeze(axis)
                shape = list(ap.shape)
                shape[axis] = n
                return ap.to_broadcast(shape)

            dve.wait_ge(sem("vec_mm"), 1)
            v.tensor_copy(vec[:, :], ps[:, 0, 0:V_ROWS]).then_inc(sem("vec_done"), 1)
            dve.wait_ge(sem("param_mm"), 1)
            LR, LI, DT, Y, N, R, Q, S, C, H1, H2 = (t16[:, i, :] for i in (1, 2, 0, 3, 4, 5, 6, 7, 8, 9, 10))
            MAG, CT, SN, LBR, LBI, FR, FI, FIS, T1, T2, DEN, NRE, CR, CI = (t16[:, i, :] for i in range(11, 25))
            NI = t16[:, 25, :].bitcast(I32)
            PR2, PI2, PR4, PI4 = (t16[:, i, :] for i in range(26, 30))
            v.tensor_copy(LR, ps[:, 2, 0:G])
            v.tensor_copy(LI, ps[:, 2, G:2 * G])
            v.tensor_copy(work[:, 512:1024], ps[:, 1, :])
            dve.wait_ge(sem("csig_done"), 1)
            dve.wait_ge(sem("ssm_in"), 16 * 13)
            step(v.tensor_scalar(T1, DT, 0.0, None, ALU.add))
            tt(csil, csil, vec[:, V_C:V_C + 8], ALU.mult).then_inc(sem("csil_done"), 1)

            MAGIC = 12582912.0

            def exp(out, y):
                step(v.tensor_scalar(Y, y, -110.0, 100.0, ALU.max, ALU.min))
                step(v.tensor_scalar(N, Y, 1.4426950408889634, MAGIC, ALU.mult, ALU.add))
                step(v.tensor_scalar(N, N, -MAGIC, None, ALU.add))
                step(v.scalar_tensor_tensor(R, N, -0.693359375, Y, ALU.mult, ALU.add))
                step(v.scalar_tensor_tensor(R, N, 2.12194440e-4, R, ALU.mult, ALU.add))
                step(v.tensor_scalar(Q, R, 1.0 / 5040, None, ALU.mult))
                for c in (1.0 / 720, 1.0 / 120, 1.0 / 24, 1.0 / 6, 0.5, 1.0):
                    step(v.scalar_tensor_tensor(Q, Q, c, R, ALU.add, ALU.mult))
                step(v.tensor_scalar(N, N, -127.0, 128.0, ALU.max, ALU.min))
                step(v.tensor_scalar(NI, N, 127.0, 8388608.0, ALU.add, ALU.mult))
                step(v.scalar_tensor_tensor(out, Q, 1.0, NI.bitcast(F32), ALU.add, ALU.mult))

            exp(T1, DT)
            step(tt(T2, T1, LR, ALU.mult))
            exp(MAG, T2)
            step(tt(Y, T1, LI, ALU.mult))
            step(v.tensor_scalar(N, Y, 1.0 / (2.0 * np.pi), MAGIC, ALU.mult, ALU.add))
            step(v.tensor_scalar(N, N, -MAGIC, None, ALU.add))
            TURN1, TURN2 = 6.28125, 0.0019350051879882812
            step(v.scalar_tensor_tensor(R, N, -TURN1, Y, ALU.mult, ALU.add))
            step(v.scalar_tensor_tensor(R, N, -TURN2, R, ALU.mult, ALU.add))
            step(v.scalar_tensor_tensor(R, N, -(2.0 * np.pi - TURN1 - TURN2), R, ALU.mult, ALU.add))
            step(v.tensor_scalar(R, R, 0.5, None, ALU.mult))
            step(tt(H2, R, R, ALU.mult))
            fact = [1.0]
            for i in range(1, 17):
                fact.append(fact[-1] * i)
            step(v.tensor_scalar(S, H2, 1.0 / fact[13], None, ALU.mult))
            for i, c in enumerate((11, 9, 7, 5, 3)):
                step(v.scalar_tensor_tensor(S, S, (-1.0) ** (i + 1) / fact[c], H2, ALU.add, ALU.mult))
            step(v.scalar_tensor_tensor(S, S, 1.0, R, ALU.add, ALU.mult))
            step(v.tensor_scalar(C, H2, 1.0 / fact[16], None, ALU.mult))
            for i, c in enumerate((14, 12, 10, 8, 6, 4, 2)):
                step(v.scalar_tensor_tensor(C, C, (-1.0) ** (i + 1) / fact[c], H2, ALU.add, ALU.mult))
            step(v.tensor_scalar(C, C, 1.0, None, ALU.add))
            step(v.scalar_tensor_tensor(SN, S, 2.0, C, ALU.mult, ALU.mult))
            step(tt(CT, S, S, ALU.mult))
            step(v.tensor_scalar(CT, CT, -2.0, 1.0, ALU.mult, ALU.add))
            step(tt(LBR, MAG, CT, ALU.mult))
            step(tt(LBI, MAG, SN, ALU.mult))
            step(tt(DEN, LR, LR, ALU.mult))
            step(tt(H1, LI, LI, ALU.mult))
            step(tt(DEN, DEN, H1, ALU.add))
            step(v.reciprocal(DEN, DEN))
            step(v.tensor_scalar(NRE, LBR, -1.0, None, ALU.add))
            step(tt(FR, NRE, LR, ALU.mult))
            step(tt(H1, LBI, LI, ALU.mult))
            step(tt(FR, FR, H1, ALU.add))
            step(tt(FR, FR, DEN, ALU.mult))
            step(tt(FI, LBI, LR, ALU.mult))
            step(tt(H1, NRE, LI, ALU.mult))
            step(tt(FI, FI, H1, ALU.subtract))
            step(tt(FI, FI, DEN, ALU.mult))
            dve.wait_ge(sem("ident_done"), 1)
            step(v.tensor_scalar(FIS, FI, sgn, None, ALU.mult))
            step(tt(Bb_st, B_st, bc(FR, 2, CH), ALU.mult))
            step(tt(Bb_sw, B_sw, bc(FIS, 2, CH), ALU.mult))
            step(tt(Bb_st, Bb_st, Bb_sw, ALU.add))
            step(tt(Bb_sw, B_sw, bc(FR, 2, CH), ALU.mult))
            step(tt(B_st, B_st, bc(FIS, 2, CH), ALU.mult))
            step(tt(Bb_sw, Bb_sw, B_st, ALU.subtract))

            def cmul(or_, oi, ar_, ai, br_, bi, t):
                step(tt(or_, ar_, br_, ALU.mult))
                step(tt(t, ai, bi, ALU.mult))
                step(tt(or_, or_, t, ALU.subtract))
                step(tt(oi, ar_, bi, ALU.mult))
                step(tt(t, ai, br_, ALU.mult))
                step(tt(oi, oi, t, ALU.add))

            step(v.memset(pw_re[:, :, 0:1], 1.0))
            step(v.memset(pw_im[:, :, 0:1], 0.0))
            step(v.tensor_copy(pw_re[:, :, 1], LBR))
            step(v.tensor_copy(pw_im[:, :, 1], LBI))
            pt = ptmp[:, 0:64].rearrange("p (g t) -> p g t", g=G)
            for n in (1, 2, 4):
                src, dst = slice(1, n + 1), slice(n + 1, 2 * n + 1)
                cmul(pw_re[:, :, dst], pw_im[:, :, dst], pw_re[:, :, src], pw_im[:, :, src],
                     bc(pw_re[:, :, n], 2, n), bc(pw_im[:, :, n], 2, n), pt[:, :, 0:n])
            ptm = ptmp[:, 0:2304].rearrange("p (g t h) -> p g t h", g=G, t=9)
            BP4 = BP.rearrange("p g (t h) -> p g t h", t=J)
            for j in range(J):
                step(tt(BP4[:, :, j, :], Bb_st, bc(pw_re[:, :, 7 - j], 2, CH), ALU.mult))
                step(tt(ptm[:, :, j, :], Bb_sw, bc(pw_im[:, :, 7 - j], 2, CH), ALU.mult))
            step(v.scalar_tensor_tensor(BP4, ptm[:, :, 0:J, :], sgn, BP4, ALU.mult, ALU.add))
            for t in range(9):
                step(tt(CA[:, :, t, :], C_st, bc(pw_re[:, :, t], 2, CH), ALU.mult))
                step(tt(ptm[:, :, t, :], C_sw, bc(pw_im[:, :, t], 2, CH), ALU.mult))
            step(v.scalar_tensor_tensor(CA, CA, nsgn, ptm, ALU.mult, ALU.subtract))
            v.memset(pool_buf[0][:, 0, 0:1], 0.0).then_inc(sem("tables_done"), 1)
            step(tt(MAG, MAG, MAG, ALU.mult))
            step(tt(MAG, MAG, MAG, ALU.mult))
            step(tt(phase_r8, MAG, MAG, ALU.mult))

            def csquare(c, s):
                step(tt(T1, c, c, ALU.mult))
                step(tt(T2, s, s, ALU.mult))
                step(v.scalar_tensor_tensor(s, c, 2.0, s, ALU.mult, ALU.mult))
                step(tt(c, T1, T2, ALU.subtract))

            for _ in range(3):
                csquare(CT, SN)
            step(v.memset(cos_t[:, :, 0:1], 1.0))
            step(v.memset(sin_t[:, :, 0:1], 0.0))
            n = 1
            while n < P:
                cmul(cos_t[:, :, n:2 * n], sin_t[:, :, n:2 * n], cos_t[:, :, 0:n], sin_t[:, :, 0:n],
                     bc(CT, 2, n), bc(SN, 2, n), tab_tmp[:, :, 0:n])
                n *= 2
                if n < P:
                    csquare(CT, SN)
            step(v.tensor_scalar(sin_t, sin_t, sgn, None, ALU.mult))
            dve.wait_ge(sem("k0_mm"), 1)
            v.memset(pool_buf[0][:, 0, 0:1], 0.0).then_inc(sem("raw_used"), 1)

            dve.wait_ge(sem("ssq1_done"), J)
            step(v.tensor_scalar(rstd, ssq, 1.0 / D, EPS, ALU.mult, ALU.add))
            v.memset(pool_buf[0][:, 0, 0:1], 0.0).then_inc(sem("ms1_done"), 1)
            dve.wait_ge(sem("rstd1_done"), 1)
            for j in range(J):
                v.tensor_scalar(h[:, j, :], h[:, j, :], rstd[:, j:j + 1], None, ALU.mult).then_inc(sem("xn_done"), 1)
            dve.wait_ge(sem("modw_used"), NMOD1)
            step(tt(S1, ps[:, 6, 0:8], vec[:, V_BMOD:V_BMOD + 8], ALU.add))
            step(tt(A1, ps[:, 6, 8:16], vec[:, V_BMOD + 8:V_BMOD + 16], ALU.add))
            step(v.scalar_tensor_tensor(A1, A1, 1.0, vec[:, V_N1:V_N1 + 8], ALU.add, ALU.mult))
            v.memset(pool_buf[0][:, 0, 0:1], 0.0).then_inc(sem("mod1_done"), 1)
            dve.wait_ge(sem("t_in"), 16 * J)
            dve.wait_ge(sem("bp_mm"), 1)
            for half in range(2):
                for k in range(1, KD, 2):
                    n = KD * half + k
                    dve.wait_ge(sem("ut_mm"), n + 1)
                    v.tensor_scalar(uT[:, k, HALF * half:HALF * half + HALF], ps[:, n % 4, :],
                                    A1[:, k:k + 1], S1[:, k:k + 1], ALU.mult, ALU.add).then_inc(sem("ut_dve"), 1)

            dve.wait_ge(sem("bias_in"), 32)
            dve.wait_ge(sem("ut_mm"), 2 * KD)
            for q in range(4):
                dve.wait_ge(sem("u_mm"), 2 * q + 2)
                tt(U[:, :, 2 * q:2 * q + 2, :].rearrange("p g j h -> p j g h"),
                   ps[:, q, :].rearrange("p (j g h) -> p j g h", j=2, g=G),
                   bc(bu_bc.rearrange("p (g h) -> p g h", g=G), 1, 2), ALU.add).then_inc(sem("u_evac"), 1)

            dve.wait_ge(sem("modw_used"), NMOD)
            mod2 = small[:, 72:96]
            step(tt(mod2, ps[:, 7, 16:40], vec[:, V_BMOD + 16:V_BMOD + 40], ALU.add))
            tt(gate2, ps[:, 7, 40:48], vec[:, V_BMOD + 40:V_BMOD + 48], ALU.add).then_inc(sem("mod2_done"), 1)
            for b in range(3 * KD):
                last = v.tensor_scalar(work[:, 128 * b:128 * b + 128], ident[:, :], mod2[:, b:b + 1], None, ALU.mult)
            last.then_inc(sem("diagonals_done"), 1)

            dve.wait_ge(sem("consts_done"), 1)
            step(v.reciprocal(pool_rcp, pool_rcp))
            for i in range(3):
                last = v.memset(pool_buf[i][:, :, 0:1], 0.0)
            last.then_inc(sem("pads_done"), 1)
            dve.wait_ge(sem("pads_done"), 1)
            for gi in range(4):
                wi = 3 - gi
                dve.wait_ge(sem("gate_bank_free"), 2 * gi + 2)
                if gi:
                    dve.wait_ge(sem("pmix_mm"), gi)
                src, dst = 0, 1
                for lvl in range(wi + 1):
                    sh = 1 << lvl
                    X_, Y_ = pool_buf[src], pool_buf[dst]
                    if sh < J:
                        tt(Y_[:, sh:J, :], X_[:, sh:J, :], X_[:, 0:J - sh, :], ALU.add)
                    step(tt(Y_[:, 0:sh, 1:P + 1], X_[:, 0:sh, 1:P + 1], X_[:, J - sh:J, 0:P], ALU.add))
                    src, dst = dst, (2 if dst == 1 else 1)
                assert dst == m_buf[gi]
                win, m, X_ = pool_buf[src], pool_buf[dst], pool_buf[0]
                step(v.scalar_tensor_tensor(m[:, :, 1:P + 1], win[:, :, 1:P + 1], 1.0 / WINDOWS[wi], X_[:, :, 1:P + 1], ALU.mult, ALU.subtract))
                step(tt(m[:, :, 1:3], win[:, :, 1:3], pool_rcp[:, wi], ALU.mult))
                tt(m[:, :, 1:3], m[:, :, 1:3], X_[:, :, 1:3], ALU.subtract).then_inc(sem("m_ready"), 1)

            v.memset(small[:, 51:52], 0.0).then_inc(sem("mul_done"), 2)

            def gate_pair(n, step2):
                for s in range(2):
                    for half in range(2):
                        it = n * 4 + (2 * s + half + 16 * step2)
                        dve.wait_ge(sem("gate_bank_free"), it + 9)
                        dve.wait_ge(sem("proj_mm"), it + 1)
                        sgh = sg[:, HALF * half:HALF * half + HALF]
                        if isinstance(n, int):
                            dst = merged[:, 2 * n + s, HALF * half:HALF * half + HALF]
                        else:
                            dst = merged[:, ds(n * 2 + s, 1), HALF * half:HALF * half + HALF].rearrange("p k t -> p (k t)")
                        if not step2:
                            tt(dst, sgh, ps[:, 5 + 2 * half, :], ALU.mult).then_inc(sem("mul_done"), 1)
                        else:
                            tt(sgh, sgh, ps[:, 5 + 2 * half, :], ALU.mult).then_inc(sem("sg_mul"), 1)
                            dve.wait_ge(sem("sg_mul"), it - 15)
                            tt(dst, dst, sgh, ALU.add).then_inc(sem("mul_done"), 1)

            with dve.Fori(0, 2) as n:
                gate_pair(n, 0)
            dve.wait_ge(sem("turned"), 1)
            for g in range(G):
                last = v.tensor_tensor_scan(SB[:, g, :], phase_r8[:, g:g + 1].to_broadcast([P, P]), SA[:, g, :], 0.0, ALU.mult, ALU.add)
            step(last)
            v.tensor_copy(SA[0:ST], SB[ST:P]).then_inc(sem("z_swapped"), 1)
            v.tensor_copy(SA[ST:P], SB[0:ST]).then_inc(sem("z_swapped"), 1)
            step(tt(U.rearrange("p g j h -> p j g h"), U.rearrange("p g j h -> p j g h"),
                    bc(d_bc.rearrange("p (g h) -> p g h", g=G), 1, J), ALU.mult))
            gate_pair(2, 0)
            for q in range(4):
                dve.wait_ge(sem("y_mm"), q + 1)
                gs = slice(4 * q, 4 * q + 4)
                last = tt(Ysp[:, :, gs, :].rearrange("p j g h -> p g j h"), ps[:, q, :].rearrange("p (g j h) -> p g j h", g=4, j=J),
                          U[:, gs], ALU.add)
            last.then_inc(sem("y_evac"), 1)
            dve.wait_ge(sem("ysq_done"), 1)
            step(v.tensor_scalar(gtmp, gtmp, 0.044715, 1.0, ALU.mult, ALU.add))
            tt(gtmp, gtmp, Y_flat, ALU.mult).then_inc(sem("gelu_arg"), 1)
            dve.wait_ge(sem("gelu_sig"), 1)
            tt(Y_flat, Y_flat, gtmp, ALU.mult).then_inc(sem("gelu_done"), 1)
            gate_pair(3, 0)
            for ob in range(2):
                for half in range(2):
                    dve.wait_ge(sem("glu_sig"), 2 * ob + half + 1)
                    cols = slice(HALF * half, HALF * half + HALF)
                    tt(zT[:, ob, cols], yT[:, ob, cols], sg[:, cols], ALU.mult).then_inc(sem("z_done"), 1)
            with dve.Fori(0, KD // 2) as n:
                gate_pair(n, 1)

            dve.wait_ge(sem("mod_mm"), 1)
            dve.wait_ge(sem("n2_in"), 16)
            v.tensor_copy(work[:, 0:2048], ps[:, 0:4, :].rearrange("p b n -> p (b n)"))
            v.scalar_tensor_tensor(A2_bc, ps[:, 4:6, :].rearrange("p b n -> p (b n)"), 1.0, u2t[0], ALU.add, ALU.mult)
            step(v.memset(small[:, 51:52], 0.0))
            v.memset(small[:, 51:52], 0.0).then_inc(sem("mod_rows_done"), 1)
            dve.wait_ge(sem("x_again"), 16)

            hs = [0]
            for t in range(J + 1):
                if t < J:
                    dve.wait_ge(sem("wout_done"), t + 1)
                    if t >= 2:
                        dve.wait_ge(sem("u2t_mm"), t - 1)
                        dve.wait_ge(sem(f"u2_out{t % 2}"), 16 * (t // 2))
                    for half in range(2):
                        cols = slice(HALF * half, HALF * half + HALF)
                        tt(u2t[t % 2][:, cols], ps[:, 2 * (t % 2) + half, :], gate1_bc[:, cols], ALU.mult).then_inc(sem("h_psum_read"), 1)
                    dve.wait_ge(sem("h_psum_read"), 2 * t + 2)
                    tt(h[:, t, :], h[:, t, :], u2t[t % 2], ALU.add).then_inc(sem("h_done"), 1)
                if t:
                    j = t - 1
                    dve.wait_ge(sem("rstd2_done"), j + 1)
                    step(v.scalar_tensor_tensor(u2t[j % 2], h[:, j, :], rstd[:, j:j + 1], A2_bc, ALU.mult, ALU.mult))
                    tt(u2t[j % 2], u2t[j % 2], S2_bc, ALU.add).then_inc(sem("u2_done"), 1)

            dve.wait_ge(sem("router_mm"), J)
            dve.wait_ge(sem("rbias_in"), 32)
            step(tt(L, ps[:, 6, 0:J * (NG + NE)].rearrange("p (j n) -> p j n", j=J), bc(rbias, 1, J), ALU.add))
            coarse, fine = L[:, :, 0:NG], L[:, :, NG:NG + NE].rearrange("p j (g i) -> p j g i", g=NG)
            m1, m2, mc, csum, t8 = (rsc[:, i, :] for i in range(5))

            def first_best(out, val, n, best, scratch):
                step(v.tensor_reduce(best, val, AX.X, ALU.max))
                step(tt(out, val, bc(best, 2, n), ALU.is_equal))
                step(tt(out, out, bc(falling[:, 0:n], 1, J), ALU.mult))
                step(v.tensor_reduce(scratch, out, AX.X, ALU.max))
                step(tt(out, out, bc(scratch, 2, n), ALU.is_equal))

            step(v.tensor_scalar(falling, iota64[:, 0:8], -1.0, 9.0, ALU.mult, ALU.add))
            first_best(g_hot, coarse, NG, mc, t8)
            tt(cdiff, coarse, bc(mc, 2, NG), ALU.subtract).then_inc(sem("coarse_diff"), 1)
            step(tt(fsel4, fine.rearrange("p j g i -> p j i g"), bc(g_hot, 2, EPG), ALU.mult))
            step(v.tensor_reduce(fsel, fsel4, AX.X, ALU.add))
            first_best(hot[0], fsel, EPG, m1, t8)
            step(v.scalar_tensor_tensor(fsel, hot[0], -3.0e38, fsel, ALU.mult, ALU.add))
            first_best(hot[1], fsel, EPG, m2, t8)
            tt(fdiff, m2, m1, ALU.subtract).then_inc(sem("fine_diff"), 1)
            dve.wait_ge(sem("coarse_exp"), 1)
            step(v.tensor_reduce(csum, cexp, AX.X, ALU.add))
            step(v.reciprocal(csum, csum))
            dve.wait_ge(sem("fine_sig"), 1)
            step(tt(wpick, wpick, bc(csum, 1, 2), ALU.mult))
            for k in range(2):
                step(tt(pick[k].rearrange("p j (g i) -> p j g i", g=NG), bc(g_hot, 3, EPG), bc(hot[k], 2, NG), ALU.mult))
            step(tt(M3, pick[0], pick[1], ALU.add))
            step(v.memset(Mb3[:, 0, :], 0.0))
            for j in range(1, J):
                step(tt(Mb3[:, j, :], Mb3[:, j - 1, :], M3[:, j - 1, :], ALU.add))
            tt(M_total, Mb3[:, J - 1, :], M3[:, J - 1, :], ALU.add).then_inc(sem("picks_done"), 1)
            dve.wait_ge(sem("rank_mm"), 1)
            rank = ps[:, 7, 0:J * NE].rearrange("p (j e) -> p j e", j=J)
            step(tt(cmp_t, bc(ps[:, 7, J * NE:J * NE + NE], 2, 16), bc(m64, 1, NE), ALU.is_gt))
            step(v.tensor_reduce(ntile, cmp_t, AX.X, ALU.add))
            step(v.tensor_scalar(ntile, ntile, 1.0, None, ALU.max))
            step(v.memset(tstart[:, 0:1], 0.0))
            step(v.tensor_tensor_scan(tstart[:, 1:NE + 1], ones[:, 0:NE], ntile, 0.0, ALU.mult, ALU.add))
            step(v.tensor_copy(tstart_i[:, :], tstart))
            for k in range(2):
                step(tt(Mp3, rank, pick[k], ALU.mult))
                step(v.tensor_reduce(rk[:, k, :], Mp3, AX.X, ALU.add))
                step(tt(Mp3, bc(tstart[:, 0:NE], 1, J), pick[k], ALU.mult))
                step(v.tensor_reduce(hi[:, k, :], Mp3, AX.X, ALU.add))
            step(tt(cmp_r, bc(rk.rearrange("p k j -> p (k j)"), 2, 15), bc(m64[:, 1:16], 1, 2 * J), ALU.is_ge))
            step(v.tensor_reduce(fl, cmp_r, AX.X, ALU.add))
            hi_f, rk_f = hi.rearrange("p k j -> p (k j)"), rk.rearrange("p k j -> p (k j)")
            step(tt(hi_f, hi_f, fl, ALU.add))
            step(v.scalar_tensor_tensor(rk_f, fl, -float(TS), rk_f, ALU.mult, ALU.add))
            step(tt(oh_lo, bc(iota64, 1, 2 * J), bc(rk_f, 2, TS), ALU.is_equal))
            step(tt(oh_hi, bc(iota64, 1, 2 * J), bc(hi_f, 2, MAX_TILES), ALU.is_equal))
            for k in range(2):
                last = tt(oh_hi[:, J * k:J * k + J, :], oh_hi[:, J * k:J * k + J, :], bc(tokid, 2, MAX_TILES), ALU.mult)
            last.then_inc(sem("onehots_done"), 1)
            step(v.tensor_scalar(fl, hi_f, float(TS), float(TS), ALU.mult, ALU.add))
            step(tt(fl, fl, rk_f, ALU.add))
            step(v.tensor_copy(ypos[:, :], fl))
            step(v.tensor_copy(wsave, wpick))
            v.memset(yTe, 0.0).then_inc(sem("yt_ready"), 1)
            dve.wait_ge(sem("slot_mm"), 1)
            v.tensor_copy(slot_tok[0:TS, 0:MAX_TILES], ps[0:TS, 0, 0:MAX_TILES]).then_inc(sem("routed"), 1)

            dve.wait_ge(sem("routed"), 1)
            n_tiles = dve.value_load(tstart_i[0:1, NE:NE + 1], min_val=NE, max_val=MAX_TILES)

            def take_x(g1):
                dve.wait_ge(sem("x_rows_used"), g1 + 1)
                v.tensor_copy(xT, ps[:, 3, :].rearrange("p (k t) -> p k t", k=KD)).then_inc(sem("xt_ready"), 1)

            def copy_rows(g):
                dve.wait_ge(sem("y_mm2"), g + 1)
                dve.wait_ge(sem("y_rows_out"), g * 16 + 16)
                v.tensor_copy(y_tile[:, HALF:D], ps[0:TS, 5, :]).then_inc(sem("y_copy_dve"), 1)

            take_x(1)
            with dve.Fori(0, n_tiles) as g:
                for f in range(KE):
                    dve.wait_ge(sem("silu_done"), g * KE + (f + 1))
                    tt(actT[:, f, :], silu_b[:, f % 2, :], ps[:, f % 2, TS:2 * TS], ALU.mult).then_inc(sem("act_ready"), 1)
                    if f == 0:
                        copy_rows(g)
                take_x(g + 2)
                dve.wait_ge(sem("tiles_done"), g + 1)
                tt(yTe, ps[:, 2, :].rearrange("p (k t) -> p k t", k=KD), bc(gate2, 2, TS), ALU.mult).then_inc(sem("yt_ready"), 1)
            copy_rows(n_tiles)

            dve.wait_ge(sem("gf_in"), 16)
            for t in range(J + 1):
                if t < J:
                    for k in range(2):
                        n = (2 * t + k) % 4
                        dve.wait_ge(sem(f"ycomb_in{n}"), 16 * (t // 2 + 1))
                        ins = v.scalar_tensor_tensor(h[:, t, :], ycomb[n], wsave[:, k, t:t + 1], h[:, t, :], ALU.mult, ALU.add)
                        if k == 0:
                            ins.then_inc(sem("first_added"), 1)
                            dve.wait_ge(sem("first_added"), t + 1)
                    ins.then_inc(sem("combined"), 1)
                if t:
                    j = t - 1
                    dve.wait_ge(sem("rstd3_done"), j + 1)
                    v.scalar_tensor_tensor(h[:, j, :], h[:, j, :], rstd[:, j:j + 1], gf_bc[:, :], ALU.mult, ALU.mult).then_inc(sem("out_done"), 1)


_OUTS = [((1, SEQ, D), "float32")]


def kernel(**inputs):
    import numpy as _np
    import concourse.bacc as _bacc
    from concourse import mybir as _mybir
    from concourse.bass_utils import run_bass_kernel_spmd as _run

    nc = _bacc.Bacc("TRN2", target_bir_lowering=False, num_devices=1)
    arrays, args = {}, {}
    for name, value in inputs.items():
        value = _np.ascontiguousarray(value)
        arrays[f"in_{name}_dram"] = value
        args[name] = nc.dram_tensor(f"in_{name}_dram", value.shape, _mybir.dt.from_np(value.dtype), kind="ExternalInput").ap()
    for shape, dtype in _OUTS:
        args["out"] = nc.dram_tensor("out_0_dram", shape, _mybir.dt.from_np(_np.dtype(dtype)), kind="ExternalOutput").ap()
    program(nc, args)
    r = _run(nc, [arrays], core_ids=[0])
    return r.results[0]["out_0_dram"]
```

```python
from contextlib import ExitStack

import numpy as np

import concourse.bass as bass
from concourse import mybir

ALU = mybir.AluOpType
ACT = mybir.ActivationFunctionType
AX = mybir.AxisListType
F32 = mybir.dt.float32
I32 = mybir.dt.int32
ds = bass.ds

P = 128
D = 1024
SEQ = 1024
J = SEQ // P
KD = D // P
HALF = 512
D_SSM, D_POOL = 256, 512
G, CH, ST = 16, 16, 64
WINDOWS = (2, 4, 8, 16)
NG, EPG = 4, 8
NE = NG * EPG
DE = 512
KE = DE // P
EPS = 1e-6
TS = 64
MAX_TILES = 2 * SEQ // TS + NE
RING = 3
MODC = 256

V_BMOD, V_N1, V_N2, V_BIN, V_PSC, V_BGLU, V_C, V_ROWS = 0, 48, 56, 64, 86, 90, 92, 100

A_UT = 0
A_WRING = 8192
A_BT = 11264
A_MERGED = 15360
A_WSP = A_MERGED
A_TMP = A_MERGED + 6144
A_POOL = 23552
A_COS = A_POOL + 3096
A_T = A_COS + 2064
A_CA = A_T + 2048
A_BPT = A_CA + 2304
A_SIN = A_BPT + 2048
A_WOUT = A_POOL
A_ROUTE = A_WOUT + 8192
ARENA = A_SIN + 2048


def program(nc, a):
    ctx = ExitStack()
    sems = {}

    def sem(name):
        if name not in sems:
            sems[name] = ctx.enter_context(nc.semaphore(name))
        return sems[name]

    def sb(name, shape, dt=F32):
        return ctx.enter_context(nc.sbuf_tensor(name, shape, dt))

    with ctx:
        ps = ctx.enter_context(nc.psum_tensor("ps", [P, 8, HALF], F32))
        u2_rows = nc.dram_tensor("u2_rows", [SEQ, D], F32, kind="Internal").ap()
        y_rows = nc.dram_tensor("y_rows", [MAX_TILES * TS, D], F32, kind="Internal").ap()

        H = sb("H", [P, J * D])
        arena = sb("arena", [P, ARENA])
        work = sb("work", [P, 3456])
        gate2_bc = sb("gate2_bc", [P, D])
        ident = sb("ident", [P, P])
        ones = sb("ones", [P, P])
        vec = sb("vec", [P, V_ROWS])
        small = sb("small", [P, 96])
        bias_bc = sb("bias_bc", [P, 512])
        route = sb("route", [P, 204])
        tstart_i = sb("tstart_i", [P, NE + 1], I32)
        slot_tok = sb("slot_tok", [P, MAX_TILES + 1], I32)
        idx_now = sb("idx_now", [P, 1], I32)
        ypos = sb("ypos", [P, 2 * J], I32)

        def ar(off, n):
            return arena[:, off:off + n]

        h = H[:, :].rearrange("p (j d) -> p j d", j=J)
        uT = ar(A_UT, 8192).rearrange("p (k t) -> p k t", k=KD)
        wring = [ar(A_WRING + 1536 * s, 1536) for s in range(2)]
        wgate = [w[:, 0:1024].rearrange("p (k n) -> p k n", k=KD) for w in wring]
        wproj = [w[:, 1024:1536].rearrange("p (k n) -> p k n", k=4) for w in wring]
        bT = ar(A_BT, 4096).rearrange("p (g t) -> p g t", g=4)
        merged = ar(A_MERGED, 8192).rearrange("p (k t) -> p k t", k=KD)
        wsp = ar(A_WSP, 6144).rearrange("p (k n) -> p k n", k=KD)
        pool_buf = [ar(A_POOL + 1032 * i, 1032).rearrange("p (j c) -> p j c", j=J) for i in range(3)]
        cos_t = ar(A_COS, 2048).rearrange("p (g c) -> p g c", g=G)
        Xs = ar(A_COS, 2064).rearrange("p (g c) -> p g c", g=G)
        Tm = ar(A_T, 2048).rearrange("p (g n) -> p g n", g=G)
        CA = ar(A_CA, 2304).rearrange("p (g t h) -> p g t h", g=G, t=9)
        BPT = ar(A_BPT, 2048).rearrange("p (g n) -> p g n", g=G)
        yT = ar(A_BPT, 2048).rearrange("p (k t) -> p k t", k=2)
        sin_t = ar(A_SIN, 2048).rearrange("p (g c) -> p g c", g=G)
        zT = ar(A_SIN, 2048).rearrange("p (k t) -> p k t", k=2)
        modw = [ar(A_BT, 2048), ar(A_BT + 2048, 2048), ar(A_TMP, 2048), ar(A_WRING, 2048)]
        modw = [m.rearrange("p (k n) -> p k n", k=KD) for m in modw]
        MODR = len(modw)
        wout = ar(A_WOUT, 8192).rearrange("p (k n) -> p k n", k=KD)
        BP = ar(A_UT, 2048).rearrange("p (g n) -> p g n", g=G)
        ptmp = ar(A_UT + 2048, 2304)
        K0 = arena[0:CH, A_UT + 4352:A_UT + 8192].rearrange("p (g n) -> p g n", g=G)
        B_st, B_sw, C_st, C_sw = (work[:, 256 * i:256 * i + 256].rearrange("p (g h) -> p g h", g=G) for i in range(4))
        C_rows = work[:, 1024:1536].rearrange("p (s b n) -> p s b n", s=2, b=2)
        lam_rows = work[0:G, 1536:1792].rearrange("p (s n) -> p s n", s=2)
        pw_re = work[:, 1792:1936].rearrange("p (g t) -> p g t", g=G)
        pw_im = work[:, 1936:2080].rearrange("p (g t) -> p g t", g=G)
        Bb_st = work[:, 2080:2336].rearrange("p (g h) -> p g h", g=G)
        Bb_sw = work[:, 2336:2592].rearrange("p (g h) -> p g h", g=G)
        t16 = work[:, 2592:3456].rearrange("p (v g) -> p v g", g=G)
        vrows = ar(A_POOL, P)
        tab_tmp = ar(A_POOL + P, 1024).rearrange("p (g c) -> p g c", g=G)
        d_bc = bias_bc[:, 0:256]
        bu_bc = bias_bc[:, 256:512]
        U = H[:, 0:2048].rearrange("p (g j h) -> p g j h", g=G, j=J)
        V = H[:, 2048:4096].rearrange("p (g c) -> p g c", g=G)
        SA = H[:, 4096:6144].rearrange("p (g c) -> p g c", g=G)
        SB = H[:, 6144:8192].rearrange("p (g c) -> p g c", g=G)
        Ysp = H[:, 4096:6144].rearrange("p (j g h) -> p j g h", j=J, g=G)

        zeros = work[:, 3072:3328]
        mod1_rows = [ar(A_POOL + 1160, D)[0:1, :], gate2_bc[0:1, :]]
        gate1_bc, S2_bc, A2_bc = (work[:, 1024 * i:1024 * i + 1024] for i in range(3))
        slotw = [ar(12288 * s, 12288) for s in range(RING)]
        e_gate = [w[:, 0:4096].rearrange("p (k n) -> p k n", k=KD) for w in slotw]
        e_up = [w[:, 4096:8192].rearrange("p (k n) -> p k n", k=KD) for w in slotw]
        e_down = [w[:, 8192:12288].rearrange("p (k n) -> p k n", k=KE) for w in slotw]
        x_tile = work[0:TS, 0:1024]
        y_tile = work[:, 1024:1536]
        xT = work[:, 2048:2560].rearrange("p (k t) -> p k t", k=KD)
        u2t = [ar(A_ROUTE + 1024 * i, 1024) for i in range(2)]
        u2T = [ar(A_ROUTE + 2048 + 1024 * i, 1024).rearrange("p (k t) -> p k t", k=KD) for i in range(2)]
        ROUTERW = KD * (NG + NE)
        rw = ar(A_ROUTE + 4096, ROUTERW).rearrange("p (k n) -> p k n", k=KD)
        assert A_ROUTE + 4096 + ROUTERW <= ARENA
        AUX = A_ROUTE - 24576
        aux = ar(24576, AUX)


        csil = small[:, 0:8]
        A1, S1 = small[:, 8:16], small[:, 16:24]
        ssq, rstd = small[:, 32:40], small[:, 40:48]
        half_neg = small[:, 48:49]
        phase_r8 = route[:, 0:16]
        sgn = small[:, 49:50]
        nsgn = small[:, 50:51]
        pool_rcp = route[:, 16:80].rearrange("p (w j c) -> p w j c", w=4, j=J)
        iota = route[:, 16:16 + TS]
        tokid = route[:, 144:152]
        rbias = route[:, 152:188]
        whole = route[:, 188:204]
        sg = sb("sg", [P, 2 * HALF])
        HE, HD = DE // 2, D // 2
        hidden = sg[:, 0:HE]
        hiddenT = sg[:, HALF:HALF + HE].rearrange("p (f h t) -> p h f t", f=2, h=2)

        ycomb = [ar(1024 * i, 1024) for i in range(2 * J)]
        gf_bc = ar(12288 * 2, D)
        gtmp, Y_flat = H[:, 6144:8192], H[:, 4096:6144]
        m_buf = [1, 2, 1, 2]
        aux_at = [0]

        def table(n):
            aux_at[0] += n
            assert aux_at[0] <= AUX
            return aux[:, aux_at[0] - n:aux_at[0]]

        def per_tile(n):
            return table(J * n).rearrange("p (j n) -> p j n", j=J)

        later = table(P)
        L = per_tile(NG + NE)
        rsc = table(8 * J).rearrange("p (v j) -> p v j", j=J)
        falling = table(EPG)
        g_hot, cdiff, cexp = per_tile(NG), per_tile(NG), per_tile(NG)
        fsel4 = per_tile(NE).rearrange("p j (i g) -> p j i g", g=NG)
        fsel, fdiff = per_tile(EPG), table(J)
        hot = [per_tile(EPG), per_tile(EPG)]
        wpick = table(2 * J).rearrange("p (k j) -> p k j", k=2)
        pick = [per_tile(NE), per_tile(NE)]
        M_all, M_before = table(J * NE), table(J * NE)
        M3, Mb3 = (m.rearrange("p (j e) -> p j e", j=J) for m in (M_all, M_before))
        Mp3 = per_tile(NE)
        M_total, ntile, tstart = table(NE), table(NE), table(NE + 1)
        cmp_t = table(16 * NE).rearrange("p (e m) -> p e m", m=16)
        cmp_r = table(15 * 2 * J).rearrange("p (e m) -> p e m", m=15)
        fl = table(2 * J)
        rk, hi = (table(2 * J).rearrange("p (k j) -> p k j", k=2) for _ in range(2))
        oh_lo = table(2 * J * TS).rearrange("p (i s) -> p i s", s=TS)
        oh_hi = table(2 * J * MAX_TILES).rearrange("p (i s) -> p i s", s=MAX_TILES)
        wsave = small[:, 56:72].rearrange("p (k j) -> p k j", k=2)

        x_v = a["x"].rearrange("b (c j) d -> (b c) j d", j=J)
        out_v = a["out"].rearrange("b (c j) d -> (b c) j d", j=J)
        u2_v = u2_rows.rearrange("(c j) d -> c j d", j=J)
        wmod_v = a["w_mod"].rearrange("l (k p) n -> p (l k) n", p=P)
        win_v = a["w_in"].rearrange("l (k p) n -> p (l k) n", p=P)
        wps_v = a["w_proj_ssm"].rearrange("l (k p) n -> p (l k) n", p=P)
        wpp_v = a["w_proj_pool"].rearrange("l (k p) n -> p (l k) n", p=P)
        wout_v = a["w_out"].rearrange("l (k p) n -> p (l k) n", p=P)
        eg_v = a["moe_w_gate"].rearrange("l e (k p) n -> (l e) p k n", p=P)
        eu_v = a["moe_w_up"].rearrange("l e (k p) n -> (l e) p k n", p=P)
        ed_v = a["moe_w_down"].rearrange("l e (k p) n -> (l e) p k n", p=P)
        GP0 = D_SSM + D_POOL + D
        GS0 = D_SSM + D_POOL

        def rows128(ap):
            return ap.rearrange("l (r n) -> (l r) n", n=P)

        def bcast(ap, n):
            return ap.rearrange("(o n) -> o n", o=1).to_broadcast([P, n]) if len(ap.shape) == 1 else ap.to_broadcast([P, n])

        wglu = sb("wglu", [P, 2 * D_SSM])[:, :].rearrange("p (k n) -> p k n", k=2)
        wpool = sb("wpool", [P, 4 * P])[:, :].rearrange("p (k n) -> p k n", k=4)
        NMOD1 = 2 * D // MODC
        NMOD = 6 * D // MODC
        FREE_NE = NE - RING

        def stand(eng, name):
            eng.sem_inc(sem("stood_" + name), 1)

        block = ctx.enter_context(nc.Block())

        @block.sync
        def _(sp):
            def load(dst, src, name):
                sp.dma_start(dst, src).then_inc(sem(name), 16)

            at = 0
            for name in ("b_mod", "norm1_g", "norm2_g", "b_in", "pool_scale", "ssm_b_glu", "c"):
                src = rows128(a[name])
                load(vrows[at:at + src.shape[0], :], src, "vrows_in")
                at += src.shape[0]
            for s, name in enumerate(("ssm_lam_re", "ssm_lam_im")):
                for half in range(2):
                    load(lam_rows[:, s, ST * half:ST * half + ST],
                         a[name].rearrange("l g p -> (l g) p"), "ssm_in")
            load(t16[:, 0, :], bcast(a["ssm_log_dt"], G), "ssm_in")
            for s, (first, second) in enumerate((("re", "im"), ("im", "re"))):
                for half, part in enumerate((first, second)):
                    load((B_st, B_sw)[s][ST * half:ST * half + ST, :, :],
                         a["ssm_b_" + part].rearrange("l g p h -> p (l g) h"), "ssm_in")
                    load(C_rows[:, s, :, ST * half:ST * half + ST],
                         a["ssm_c_" + part].rearrange("l (b g) h p -> (l g h) b p", b=2), "ssm_in")
            for q in range(4):
                load(h[:, 2 * q:2 * q + 2, :], x_v[:, 2 * q:2 * q + 2, :], f"x_in{q}")
            for i in range(NMOD1):
                if i >= MODR:
                    sp.wait_ge(sem("modw_used"), i - MODR + 1)
                load(modw[i % MODR], wmod_v[:, :, MODC * i:MODC * i + MODC], f"modw_in{i % MODR}")
            load(wsp[:, :, 0:D_SSM], win_v[:, :, 0:D_SSM], "wsp_in")
            load(wsp[:, :, D_SSM:768], win_v[:, :, D_SSM:768], "wsp_pool_in")
            load(d_bc, bcast(a["ssm_d"], D_SSM), "bias_in")
            load(bu_bc, bcast(a["b_in"][:, 0:D_SSM], D_SSM), "bias_in")
            for i in range(NMOD1, NMOD):
                if i - MODR < NMOD1:
                    sp.wait_ge(sem("modw_used"), i - MODR + 1)
                else:
                    sp.wait_ge(sem("mod_sum"), KD * (i - MODR - NMOD1 + 1))
                load(modw[i % MODR], wmod_v[:, :, MODC * i:MODC * i + MODC], f"modw_in{i % MODR}")
            load(wglu, a["ssm_w_glu"].rearrange("l (k p) n -> p (l k) n", p=P), "wglu_in")
            load(wpool, a["pool_w"].rearrange("l g c d -> c (l g) d"), "wpool_in")
            load(rbias[:, 0:NG], bcast(a["router_coarse_b"], NG), "rbias_in")
            load(rbias[:, NG:NG + NE], bcast(a["router_fine_b"], NE), "rbias_in")
            def gate_weights(item, step2, s, wait):
                proj_v, nk, first = (wps_v, 2, GS0) if step2 else (wpp_v, 4, GP0)
                if wait is not None:
                    sp.wait_ge(sem("gate_mm"), wait)
                sp.dma_start(wgate[s], win_v[:, :, ds(item * 128 + (first - step2 * D), P)]).then_inc(sem(f"wring_in{s}"), 16)
                sp.dma_start(wproj[s][:, 0:nk, :], proj_v[:, :, ds(item * 128 - step2 * D, P)]).then_inc(sem(f"wproj_in{s}"), 16)

            sp.wait_ge(sem("mod_sum"), KD * (NMOD - NMOD1))
            for s in range(2):
                gate_weights(s, 0, s, None)
            with sp.Fori(1, KD // 2) as n:
                for s in range(2):
                    gate_weights(n * 2 + s, 0, s, n * 4 + (2 * s - 2))
            with sp.Fori(KD // 2, KD) as n:
                for s in range(2):
                    gate_weights(n * 2 + s, 1, s, n * 4 + (2 * s - 2))
            sp.wait_ge(sem("z_done"), 4)
            load(wout, wout_v, "wout_in")
            load(h, x_v, "x_again")
            load(u2t[0], bcast(a["norm2_g"], D), "n2_in")
            sp.wait_ge(sem("gate_mm"), 4 * KD)
            load(rw[:, :, 0:NG], a["router_coarse_w"].rearrange("l (k p) n -> p (l k) n", p=P), "rw_in")
            load(rw[:, :, NG:NG + NE], a["router_fine_w"].rearrange("l (k p) n -> p (l k) n", p=P), "rw_in")

            def load_expert(e, s):
                sp.dma_start(e_gate[s], eg_v[ds(e, 1)].rearrange("e p k n -> p (e k) n")).then_inc(sem(f"gateup_in{s}"), 16)
                sp.dma_start(e_up[s], eu_v[ds(e, 1)].rearrange("e p k n -> p (e k) n")).then_inc(sem(f"gateup_in{s}"), 16)
                sp.dma_start(e_down[s], ed_v[ds(e, 1)].rearrange("e p k n -> p (e k) n")).then_inc(sem(f"down_in{s}"), 16)

            load_expert(0, 0)
            sp.wait_ge(sem("mod_rows_done"), 1)
            sp.wait_ge(sem("wout_done"), J)
            load_expert(1, 1)
            sp.wait_ge(sem("routed"), 1)
            for s in range(2):
                sp.wait_ge(sem(f"u2_out{s}"), 16 * (J // 2))
            load_expert(2, 2)

            def next_expert(e, s):
                last = sp.value_load(tstart_i[0:1, ds(e - (RING - 1), 1)], min_val=1, max_val=MAX_TILES)
                sp.wait_ge(sem("tiles_done"), last)
                load_expert(e, s)

            with sp.Fori(1, NE // RING) as n:
                for s in range(RING):
                    next_expert(n * RING + s, s)
            for e in range(NE // RING * RING, NE):
                next_expert(e, e % RING)
            last = sp.value_load(tstart_i[0:1, NE - 2:NE - 1], min_val=1, max_val=MAX_TILES)
            sp.wait_ge(sem("tiles_done"), last)
            load(gf_bc, bcast(a["norm_f_g"], D), "gf_in")

        @block.gpsimd
        def _(pool):
            own = [0]

            def step(ins):
                own[0] += 1
                ins.then_inc(sem("pool_step"), 1)
                pool.wait_ge(sem("pool_step"), own[0])

            gp = nc.gpsimd
            gp.memset(ident[:, :], 0.0)
            gp.memset(ones[:, :], 1.0)
            gp.memset(half_neg, -0.5)
            gp.memset(nsgn, 1.0)
            step(gp.memset(sgn, -1.0))
            step(gp.memset(nsgn[ST:P, :], -1.0))
            step(gp.memset(sgn[ST:P, :], 1.0))
            gp.affine_select(out=ident[:, :], in_=ident[:, :], compare_op=ALU.not_equal, fill=1.0,
                             base=0, pattern=[[-1, P]], channel_multiplier=1).then_inc(sem("ident_done"), 1)
            gp.memset(K0, 0.0).then_inc(sem("k0_zero"), 1)
            gp.iota(whole, [[TS, 16]], base=0, channel_multiplier=0, allow_small_or_imprecise_dtypes=True)
            gp.iota(tokid, [[1, J]], base=0, channel_multiplier=J, allow_small_or_imprecise_dtypes=True)
            for w in range(4):
                gp.iota(pool_rcp[:, w], [[1, J], [J, 2]], base=1, channel_multiplier=0,
                        allow_small_or_imprecise_dtypes=True)
            step(gp.memset(slot_tok[:, :], 0))
            for w in range(4):
                last = gp.tensor_scalar(pool_rcp[:, w], pool_rcp[:, w], float(WINDOWS[w]), None, ALU.min)
            last.then_inc(sem("consts_done"), 1)

            pool.wait_ge(sem("ms1_done"), 1)
            gp.tensor_tensor(rstd, rstd, half_neg.to_broadcast([P, J]), ALU.pow).then_inc(sem("rstd1_done"), 1)


            pool.wait_ge(sem("in_evac"), 12)
            gp.tensor_tensor(SA, SA, cos_t, ALU.mult)
            step(gp.tensor_tensor(SB, SB, sin_t, ALU.mult))
            gp.tensor_tensor(SA, SA, SB, ALU.subtract).then_inc(sem("turned"), 1)
            pool.wait_ge(sem("z_swapped"), 2)
            step(gp.tensor_tensor(SB, SB, cos_t, ALU.mult))
            step(gp.tensor_tensor(SA, SA, sin_t, ALU.mult))
            step(gp.memset(Xs[:, :, 0:1], 0.0))
            gp.tensor_tensor(Xs[:, :, 1:P + 1], SB, SA, ALU.add).then_inc(sem("state_done"), 1)

            gp.iota(iota, [[1, TS]], base=0, channel_multiplier=0, allow_small_or_imprecise_dtypes=True)

            for j in range(J):
                pool.wait_ge(sem("ssq2_done"), j + 1)
                step(gp.tensor_scalar(rstd[:, j:j + 1], ssq[:, j:j + 1], 1.0 / D, EPS, ALU.mult, ALU.add))
                gp.tensor_tensor(rstd[:, j:j + 1], rstd[:, j:j + 1], half_neg, ALU.pow).then_inc(sem("rstd2_done"), 1)

            pool.wait_ge(sem("wout_done"), J)
            step(gp.memset(later, 1.0))
            gp.affine_select(out=later, in_=later, compare_op=ALU.is_gt, fill=0.0,
                             base=0, pattern=[[1, P]], channel_multiplier=-1).then_inc(sem("later_done"), 1)
            pool.wait_ge(sem("routed"), 1)
            for s in range(2):
                pool.wait_ge(sem(f"u2_out{s}"), 16 * (J // 2))
            gp.memset(idx_now[:, :], 0).then_inc(sem("x_rows_used"), 1)
            n_tiles = pool.value_load(tstart_i[0:1, NE:NE + 1], min_val=NE, max_val=MAX_TILES)
            with pool.Fori(0, n_tiles + 1) as g:
                pool.wait_ge(sem("x_rows_used"), g + 1)
                gp.tensor_copy(idx_now[0:TS, :], slot_tok[0:TS, ds(g, 1)]).then_inc(sem("idx_ready"), 1)
                pool.wait_ge(sem("idx_ready"), g + 1)
                stand(pool, "pool")
                gp.indirect_dma_start(x_tile, None, u2_rows, bass.IndirectOffsetOnAxis(ap=idx_now[0:TS, 0:1], axis=0)).then_inc(sem("x_rows_in"), 16)

            pool.wait_ge(sem("y_rows_out"), n_tiles * 32 + 32)
            stand(pool, "pool")
            for t in range(J):
                for k in range(2):
                    gp.indirect_dma_start(ycomb[2 * t + k], None, y_rows, bass.IndirectOffsetOnAxis(
                        ap=ypos[:, J * k + t:J * k + t + 1], axis=0)).then_inc(sem(f"ycomb_in{t}"), 16)
            for j in range(J):
                pool.wait_ge(sem("ssq3_done"), j + 1)
                step(gp.tensor_scalar(rstd[:, j:j + 1], ssq[:, j:j + 1], 1.0 / D, EPS, ALU.mult, ALU.add))
                gp.tensor_tensor(rstd[:, j:j + 1], rstd[:, j:j + 1], half_neg, ALU.pow).then_inc(sem("rstd3_done"), 1)

        @block.tensor
        def _(pe):
            mm, tp = nc.tensor.matmul, nc.tensor.transpose

            def group(out, pairs):
                for i, (lhsT, rhs) in enumerate(pairs):
                    last = mm(out, lhsT, rhs, start=(i == 0), stop=(i == len(pairs) - 1))
                return last

            pe.wait_ge(sem("ident_done"), 1)
            pe.wait_ge(sem("vrows_in"), 16 * 7)
            tp(ps[:, 0, 0:V_ROWS], vrows[0:V_ROWS, :], ident[0:V_ROWS, 0:V_ROWS]).then_inc(sem("vec_mm"), 1)
            pe.wait_ge(sem("ssm_in"), 16 * 13)
            for s in range(2):
                tp(ps[:, 2, G * s:G * s + G], lam_rows[:, s, :], ident[0:G, 0:G])
            for s in range(2):
                for b in range(2):
                    last = tp(ps[:, 1, 256 * s + 128 * b:256 * s + 128 * b + 128], C_rows[:, s, b, :], ident[:, :])
            last.then_inc(sem("param_mm"), 1)

            pe.wait_ge(sem("csil_done"), 1)
            for i in range(NMOD1):
                pe.wait_ge(sem(f"modw_in{i % MODR}"), 16 * (i // MODR + 1))
                group(ps[0:1, (6, 7, 0, 1)[i // 2], MODC * (i % 2):MODC * (i % 2) + MODC],
                      [(csil[:, k:k + 1], modw[i % MODR][:, k, :]) for k in range(KD)]).then_inc(sem("modw_used"), 1)
            pe.wait_ge(sem("mod1_rows"), 4)
            for b in range(2 * KD):
                last = mm(ps[:, 6, b:b + 1], mod1_rows[b // KD][:, 128 * (b % KD):128 * (b % KD) + 128], ones[0:1, 0:1], start=True, stop=True)
            last.then_inc(sem("mod1_mm"), 1)

            pe.wait_ge(sem("tables_done"), 1)
            for g in range(G):
                last = mm(ps[0:CH, 2 + g // 4, 128 * (g % 4):128 * (g % 4) + 128], Bb_st[:, g, :], CA[:, g, 0:8, :],
                          start=True, stop=True)
            last.then_inc(sem("k0_mm"), 1)
            pe.wait_ge(sem("k0_evac"), 4)
            for g in range(G):
                last = tp(ps[:, 2 + g // 4, 128 * (g % 4):128 * (g % 4) + 128], BP[:, g, :], ident[:, :])
            last.then_inc(sem("bp_mm"), 1)

            pe.wait_ge(sem("bpt_evac"), 4)
            for half in range(2):
                pe.wait_ge(sem("xn_done"), 4 * half + 4)
                for k in range(KD):
                    n = KD * half + k
                    if n >= 4:
                        pe.wait_ge(sem(("ut_act", "ut_dve")[k % 2]), (n - 4) // 2 + 1)
                    for j in range(4):
                        last = tp(ps[:, n % 4, 128 * j:128 * j + 128], h[:, 4 * half + j, 128 * k:128 * k + 128], ident[:, :])
                    last.then_inc(sem("ut_mm"), 1)

            pe.wait_ge(sem("ut_act"), 8)
            pe.wait_ge(sem("ut_dve"), 8)
            pe.wait_ge(sem("wsp_in"), 16)
            for j in range(J):
                group(ps[:, j // 2, 256 * (j % 2):256 * (j % 2) + 256],
                      [(uT[:, k, 128 * j:128 * j + 128], wsp[:, k, 0:D_SSM]) for k in range(KD)]).then_inc(sem("u_mm"), 1)

            def pool_project(gi):
                if gi >= 2:
                    pe.wait_ge(sem("gate_bank_free"), 2 * (gi - 1))
                col = D_SSM + 128 * (3 - gi)
                for half in range(2):
                    group(ps[:, 4 + 2 * (gi % 2) + half, :],
                          [(wsp[:, k, col:col + 128], uT[:, k, HALF * half:HALF * half + HALF]) for k in range(KD)]).then_inc(sem("px_mm"), 1)

            def pool_mix(gi):
                pe.wait_ge(sem("m_ready"), gi + 1)
                if gi >= 2:
                    pe.wait_ge(sem("bt_evac"), 2 * (gi - 1))
                for half in range(2):
                    m = pool_buf[m_buf[gi]][:, 4 * half:4 * half + 4, 1:P + 1]
                    last = mm(ps[:, 2 * (gi % 2) + half, :], wpool[:, 3 - gi, :], m, start=True, stop=True)
                last.then_inc(sem("pmix_mm"), 1)

            pe.wait_ge(sem("wsp_pool_in"), 16)
            pool_project(0)
            pe.wait_ge(sem("u_evac"), 4)
            for g in range(G):
                last = tp(ps[:, g // 4, 128 * (g % 4):128 * (g % 4) + 128], U[:, g].rearrange("p j h -> p (j h)"), ident[:, :])
                if g % 4 == 3:
                    last.then_inc(sem("v_mm"), 1)
            pool_project(1)
            pe.wait_ge(sem("v_evac"), 4)
            for g in range(G):
                last = mm(ps[:, g // 4, 128 * (g % 4):128 * (g % 4) + 128], BPT[:, g, :], V[:, g, :], start=True, stop=True)
                if g % 4 == 3:
                    last.then_inc(sem("in_mm"), 1)
            pool_project(2)
            pe.wait_ge(sem("wpool_in"), 16)
            pe.wait_ge(sem("in_evac"), 12)
            pool_mix(0)
            pool_project(3)
            pool_mix(1)
            pool_mix(2)
            pool_mix(3)
            pe.wait_ge(sem("bt_evac"), 8)

            def gate_pair(n, step2):
                rhs, nk = (zT, 2) if step2 else (bT, 4)
                for s in range(2):
                    pe.wait_ge(sem(f"wring_in{s}"), n * 16 + 16 * (1 + 4 * step2))
                    pe.wait_ge(sem(f"wproj_in{s}"), n * 16 + 16 * (1 + 4 * step2))
                    for half in range(2):
                        it = n * 4 + (2 * s + half + 16 * step2)
                        pe.wait_ge(sem("gate_bank_free"), it + 7)
                        pe.wait_ge(sem("mul_done"), it + 1)
                        cols = slice(HALF * half, HALF * half + HALF)
                        group(ps[:, 5 + 2 * half, :], [(wproj[s][:, k, :], rhs[:, k, cols]) for k in range(nk)]).then_inc(sem("proj_mm"), 1)
                        group(ps[:, 4 + 2 * half, :], [(wgate[s][:, k, :], uT[:, k, cols]) for k in range(KD)]).then_inc(sem("gate_mm"), 1)

            with pe.Fori(0, 2) as n:
                gate_pair(n, 0)
            gate_pair(2, 0)
            pe.wait_ge(sem("state_done"), 1)
            pe.wait_ge(sem("t_in"), 16 * J)
            for g in range(G):
                last = group(ps[:, g // 4, 128 * (g % 4):128 * (g % 4) + 128],
                             [(V[:, g, :], Tm[:, g, :]), (Xs[:, g, 0:P], CA[:, g, 1:9, :])])
                if g % 4 == 3:
                    last.then_inc(sem("y_mm"), 1)
            gate_pair(3, 0)
            pe.wait_ge(sem("gelu_done"), 1)
            for cb in range(2):
                for half in range(2):
                    for j in range(4):
                        last = tp(ps[:, 2 * cb + half, 128 * j:128 * j + 128],
                                  Ysp[:, 4 * half + j, 8 * cb:8 * cb + 8].rearrange("p g h -> p (g h)"), ident[:, :])
                    last.then_inc(sem("yt_mm"), 1)
            pe.wait_ge(sem("yt_evac"), 4)
            pe.wait_ge(sem("wglu_in"), 16)
            for ob in range(2):
                for half in range(2):
                    group(ps[:, 2 * ob + half, :], [(wglu[:, k, 128 * ob:128 * ob + 128], yT[:, k, HALF * half:HALF * half + HALF])
                                                   for k in range(2)]).then_inc(sem("glu_mm"), 1)
            pe.wait_ge(sem("z_done"), 4)
            with pe.Fori(0, KD // 2) as n:
                gate_pair(n, 1)

            pe.wait_ge(sem("mod_sums_done"), 1)
            pe.wait_ge(sem("mul_done"), 4 * KD + 2)
            for q in range(6):
                last = mm(ps[:, q, :], ones[:, :], work[:, HALF * q:HALF * q + HALF], start=True, stop=True)
            last.then_inc(sem("mod_mm"), 1)
            pe.wait_ge(sem("mod_rows_done"), 1)
            pe.wait_ge(sem("wout_in"), 16)
            pe.wait_ge(sem("rw_in"), 32)
            for t in range(J + 2):
                if t < J:
                    if t >= 2:
                        pe.wait_ge(sem("h_psum_read"), 2 * (t - 1))
                    for half in range(2):
                        last = group(ps[:, 2 * (t % 2) + half, :],
                                     [(merged[:, k, 128 * t:128 * t + 128], wout[:, k, HALF * half:HALF * half + HALF]) for k in range(KD)])
                    last.then_inc(sem("wout_done"), 1)
                if 1 <= t <= J:
                    pe.wait_ge(sem("u2_done"), t)
                    if t >= 2:
                        pe.wait_ge(sem("u2t_evac"), 2 * (t - 1))
                    for k in range(KD):
                        last = tp(ps[:, 4 + k // 4, 128 * (k % 4):128 * (k % 4) + 128], u2t[(t - 1) % 2][:, 128 * k:128 * k + 128], ident[:, :])
                    last.then_inc(sem("u2t_mm"), 1)
                if t >= 2:
                    j = t - 2
                    pe.wait_ge(sem("u2t_evac"), 2 * (j + 1))
                    group(ps[:, 6, (NG + NE) * j:(NG + NE) * (j + 1)],
                          [(u2T[j % 2][:, k, :], rw[:, k, :]) for k in range(KD)]).then_inc(sem("router_mm"), 1)

            pe.wait_ge(sem("picks_done"), 1)
            pe.wait_ge(sem("later_done"), 1)
            group(ps[:, 7, 0:J * NE], [(later, M_all), (ones[:, :], M_before)])
            mm(ps[:, 7, J * NE:J * NE + NE], ones[:, :], M_total, start=True, stop=True).then_inc(sem("rank_mm"), 1)
            for q in range(2):
                last = mm(ps[:, 4 + q, :], ones[:, :], gate2_bc[:, HALF * q:HALF * q + HALF], start=True, stop=True)
            last.then_inc(sem("gate2_mm"), 1)
            pe.wait_ge(sem("onehots_done"), 1)
            group(ps[0:TS, 0, 0:MAX_TILES], [(oh_lo[:, i, :], oh_hi[:, i, :]) for i in range(2 * J)]).then_inc(sem("slot_mm"), 1)

            def both(bank, pairs):
                for i, (lhsT, *halves) in enumerate(pairs):
                    for c in range(2):
                        last = mm(ps[TS * c:TS * c + TS, bank, 0:halves[c].shape[-1]], lhsT[c], halves[c],
                                  start=(i == 0), stop=(i == len(pairs) - 1))
                return last

            def hidden_product(bank, w):
                return both(bank, [((xT[:, k, :],) * 2, w[:, k, 0:HE], w[:, k, HE:DE]) for k in range(KD)])

            def gate(g, s):
                pe.wait_ge(sem("xt_ready"), g + 1)
                hidden_product(0, e_gate[s]).then_inc(sem("gate_done"), 1)

            def up(s):
                hidden_product(1, e_up[s]).then_inc(sem("up_done"), 1)

            def transpose_x(g1):
                pe.wait_ge(sem("x_rows_in"), g1 * 16)
                stand(pe, "pe")
                for k in range(KD):
                    last = tp(ps[:, 4, TS * k:TS * k + TS], x_tile[:, 128 * k:128 * k + 128], ident[0:TS, 0:TS])
                last.then_inc(sem("x_rows_used"), 1)

            def transpose_hidden(g):
                pe.wait_ge(sem("hidden_ready"), g)
                for f in range(2):
                    last = tp(ps[:, 6, 128 * f:128 * f + 128], hidden[:, 128 * f:128 * f + 128], ident[:, :])
                last.then_inc(sem("hidden_used"), 1)

            def down(g, s):
                pe.wait_ge(sem("hiddent_ready"), g)
                pe.wait_ge(sem("y_copied"), g)
                both(2, [((hiddenT[:, f // 2, f % 2, :],) * 2, e_down[s][:, f, 0:HD], e_down[s][:, f, HD:D]) for f in range(KE)]).then_inc(sem("tiles_done"), 1)

            def tile(g, s, s_before):
                transpose_hidden(g)
                gate(g, s)
                up(s)
                transpose_x(g + 2)
                down(g, s_before)

            def expert(e, s, n):
                t0 = pe.value_load(tstart_i[0:1, ds(e, 1)], min_val=1, max_val=MAX_TILES)
                t1 = pe.value_load(tstart_i[0:1, ds(e + 1, 1)], min_val=1, max_val=MAX_TILES)
                transpose_hidden(t0)
                pe.wait_ge(sem(f"gateup_in{s}"), n * 32 + 32)
                stand(pe, "pe")
                gate(t0, s)
                up(s)
                transpose_x(t0 + 2)
                down(t0, (s - 1) % RING)
                pe.wait_ge(sem(f"down_in{s}"), n * 16 + 16)
                stand(pe, "pe")
                with pe.If(t1 > t0 + 1):
                    with pe.Fori(t0 + 1, t1) as g:
                        tile(g, s, s)

            pe.wait_ge(sem("routed"), 1)
            n_tiles = pe.value_load(tstart_i[0:1, NE:NE + 1], min_val=NE, max_val=MAX_TILES)
            t1 = pe.value_load(tstart_i[0:1, 1:2], min_val=1, max_val=MAX_TILES)
            pe.wait_ge(sem("gate2_rows"), 2)
            transpose_x(1)
            pe.wait_ge(sem("gateup_in0"), 32)
            gate(0, 0)
            up(0)
            transpose_x(2)
            pe.wait_ge(sem("down_in0"), 16)
            with pe.If(t1 > 1):
                with pe.Fori(1, t1) as g:
                    tile(g, 0, 0)
            with pe.Fori(0, (NE - 1) // RING) as n:
                expert(n * RING + 1, 1, n)
                expert(n * RING + 2, 2, n)
                expert(n * RING + 3, 0, n + 1)
            for e in range((NE - 1) // RING * RING + 1, NE):
                expert(e, e % RING, e // RING)
            transpose_hidden(n_tiles)
            down(n_tiles, (NE - 1) % RING)

        @block.scalar
        def _(act):
            fn = nc.scalar.activation

            act.wait_ge(sem("vec_done"), 1)
            fn(csil, vec[:, V_C:V_C + 8], ACT.Sigmoid).then_inc(sem("csig_done"), 1)
            for j in range(J):
                act.wait_ge(sem(f"x_in{j // 2}"), 16)
                if j:
                    act.wait_ge(sem("ssq1_done"), j)
                fn(sg[:, :], h[:, j, :], ACT.Square, accum_out=ssq[:, j:j + 1]).then_inc(sem("ssq1_done"), 1)

            for i in range(4):
                act.wait_ge(sem("modw_used"), 2 * i + 2)
                fn(mod1_rows[i // 2][:, HALF * (i % 2):HALF * (i % 2) + HALF], ps[0:1, (6, 7, 0, 1)[i], :], ACT.Copy).then_inc(sem("mod1_rows"), 1)
            act.wait_ge(sem("k0_mm"), 1)
            act.wait_ge(sem("k0_zero"), 1)
            for q in range(4):
                fn(K0[:, 4 * q:4 * q + 4, 112:240], ps[0:CH, 2 + q, :].rearrange("p (g n) -> p g n", g=4), ACT.Copy).then_inc(sem("k0_evac"), 1)
            act.wait_ge(sem("k0_evac"), 4)
            for j1 in range(J):
                act.dma_start(Tm[CH * j1:CH * j1 + CH, :, :], K0[:, :, 112 - CH * j1:240 - CH * j1]).then_inc(sem("t_in"), 16)
            act.wait_ge(sem("bp_mm"), 1)
            for q in range(4):
                fn(BPT[:, 4 * q:4 * q + 4, :], ps[:, 2 + q, :].rearrange("p (g n) -> p g n", g=4), ACT.Copy).then_inc(sem("bpt_evac"), 1)

            act.wait_ge(sem("mod1_done"), 1)
            act.wait_ge(sem("t_in"), 16 * J)
            for half in range(2):
                for k in range(0, KD, 2):
                    n = KD * half + k
                    act.wait_ge(sem("ut_mm"), n + 1)
                    fn(uT[:, k, HALF * half:HALF * half + HALF], ps[:, n % 4, :], ACT.Identity,
                       scale=A1[:, k:k + 1], bias=S1[:, k:k + 1]).then_inc(sem("ut_act"), 1)

            def pool_in(gi):
                if gi:
                    act.wait_ge(sem("m_ready"), gi)
                else:
                    act.wait_ge(sem("pads_done"), 1)
                for half in range(2):
                    act.wait_ge(sem("px_mm"), 2 * gi + half + 1)
                    fn(pool_buf[0][:, 4 * half:4 * half + 4, 1:P + 1],
                       ps[:, 4 + 2 * (gi % 2) + half, :].rearrange("p (j c) -> p j c", j=4), ACT.Identity,
                       bias=vec[:, V_BIN + 2 + 3 - gi:V_BIN + 3 + 3 - gi]).then_inc(sem("gate_bank_free"), 1)

            def pool_out(gi):
                act.wait_ge(sem("pmix_mm"), gi + 1)
                if gi == 0:
                    act.wait_ge(sem("mod_sum"), KD * (NMOD - NMOD1))
                for half in range(2):
                    fn(bT[:, 3 - gi, HALF * half:HALF * half + HALF], ps[:, 2 * (gi % 2) + half, :], ACT.Copy,
                       scale=vec[:, V_PSC + 3 - gi:V_PSC + 4 - gi]).then_inc(sem("bt_evac"), 1)

            pool_in(0)
            for q in range(4):
                act.wait_ge(sem("v_mm"), q + 1)
                fn(V[:, 4 * q:4 * q + 4, :], ps[:, q, :].rearrange("p (g n) -> p g n", g=4), ACT.Copy).then_inc(sem("v_evac"), 1)
            pool_in(1)
            for q in range(4):
                act.wait_ge(sem("in_mm"), q + 1)
                src = ps[:, q, :].rearrange("p (g n) -> p g n", g=4)
                dst = slice(4 * q, 4 * q + 4)
                fn(SA[:, dst, :], src, ACT.Copy).then_inc(sem("in_evac"), 1)
                fn(SB[0:ST, dst, :], src[ST:P], ACT.Copy).then_inc(sem("in_evac"), 1)
                fn(SB[ST:P, dst, :], src[0:ST], ACT.Copy).then_inc(sem("in_evac"), 1)
            pool_in(2)
            pool_out(0)
            pool_in(3)
            for gi in range(1, 4):
                pool_out(gi)

            def gate_pair(n, step2):
                for s in range(2):
                    for half in range(2):
                        it = n * 4 + (2 * s + half + 16 * step2)
                        act.wait_ge(sem("gate_mm"), it + 1)
                        act.wait_ge(sem("mul_done"), it + 1)
                        stand(act, "act")
                        col = V_BIN + (6 if step2 else 14) + s
                        fn(sg[:, HALF * half:HALF * half + HALF], ps[:, 4 + 2 * half, :], ACT.Sigmoid,
                           bias=vec[:, ds(n * 2 + col, 1)] if not isinstance(n, int) else vec[:, n * 2 + col:n * 2 + col + 1]).then_inc(sem("gate_bank_free"), 1)

            spare = y_rows[NE * TS:, :].rearrange("(p r) (c n) -> p (r c) n", p=P, n=256)
            act.wait_ge(sem("zeros_ready"), 1)
            for c in range(2):
                part = spare[:, c * spare.shape[1] // 2:(c + 1) * spare.shape[1] // 2]
                act.dma_start(part, zeros.unsqueeze(1).to_broadcast([P, part.shape[1], 256])).then_inc(sem("y_rows_out"), 16)

            with act.Fori(0, 2) as n:
                gate_pair(n, 0)
            gate_pair(2, 0)
            act.wait_ge(sem("y_evac"), 1)
            fn(gtmp, Y_flat, ACT.Square).then_inc(sem("ysq_done"), 1)
            act.wait_ge(sem("gelu_arg"), 1)
            fn(gtmp, gtmp, ACT.Sigmoid, scale=2.0 * (2.0 / np.pi) ** 0.5).then_inc(sem("gelu_sig"), 1)
            gate_pair(3, 0)
            for cb in range(2):
                for half in range(2):
                    act.wait_ge(sem("yt_mm"), 2 * cb + half + 1)
                    fn(yT[:, cb, HALF * half:HALF * half + HALF], ps[:, 2 * cb + half, :], ACT.Copy).then_inc(sem("yt_evac"), 1)
            for ob in range(2):
                for half in range(2):
                    act.wait_ge(sem("glu_mm"), 2 * ob + half + 1)
                    act.wait_ge(sem("mul_done"), 2 * KD + half + 1)
                    if ob:
                        act.wait_ge(sem("z_done"), half + 1)
                    fn(sg[:, HALF * half:HALF * half + HALF], ps[:, 2 * ob + half, :], ACT.Sigmoid,
                       bias=vec[:, V_BGLU + ob:V_BGLU + ob + 1]).then_inc(sem("glu_sig"), 1)
            act.wait_ge(sem("z_done"), 4)
            with act.Fori(0, KD // 2) as n:
                gate_pair(n, 1)

            def second_norm(j):
                act.wait_ge(sem("h_done"), j + 1)
                if j:
                    act.wait_ge(sem("ssq2_done"), j)
                fn(sg[:, :], h[:, j, :], ACT.Square, accum_out=ssq[:, j:j + 1]).then_inc(sem("ssq2_done"), 1)

            def rows_out(j):
                act.wait_ge(sem("u2_done"), j + 1)
                act.dma_start(u2_v[:, j, :], u2t[j % 2]).then_inc(sem(f"u2_out{j % 2}"), 16)
                act.wait_ge(sem("u2t_mm"), j + 1)
                if j >= 2:
                    act.wait_ge(sem("router_mm"), j - 1)
                for b in range(2):
                    fn(u2T[j % 2][:, 4 * b:4 * b + 4, :], ps[:, 4 + b, :].rearrange("p (k t) -> p k t", k=4), ACT.Copy).then_inc(sem("u2t_evac"), 1)

            for j in range(J):
                second_norm(j)
                rows_out(j)

            act.wait_ge(sem("coarse_diff"), 1)
            fn(cexp, cdiff, ACT.Exp).then_inc(sem("coarse_exp"), 1)
            act.wait_ge(sem("fine_diff"), 1)
            fn(wpick[:, 0, :], fdiff, ACT.Sigmoid, scale=-1.0)
            fn(wpick[:, 1, :], fdiff, ACT.Sigmoid).then_inc(sem("fine_sig"), 1)

            act.wait_ge(sem("routed"), 1)
            n_tiles = act.value_load(tstart_i[0:1, NE:NE + 1], min_val=NE, max_val=MAX_TILES)

            def silu(g):
                act.wait_ge(sem("gate_done"), g + 1)
                fn(hidden, ps[:, 0, 0:HE], ACT.Silu).then_inc(sem("silu_done"), 1)

            def take_x(g1):
                act.wait_ge(sem("x_rows_used"), g1 + 1)
                fn(xT, ps[:, 4, :].rearrange("p (k t) -> p k t", k=KD), ACT.Copy).then_inc(sem("xt_ready"), 1)

            def rows_to_dram(g):
                act.wait_ge(sem("y_copied"), g + 1)
                for c in range(2):
                    act.dma_start(y_rows[ds((g - 1) * TS, TS), HD * c:HD * c + HD], y_tile[TS * c:TS * c + TS, :]).then_inc(sem("y_rows_out"), 16)

            take_x(1)
            silu(0)
            take_x(2)
            with act.Fori(1, n_tiles) as g:
                silu(g)
                take_x(g + 2)
                rows_to_dram(g)
            rows_to_dram(n_tiles)

            for j in range(J):
                act.wait_ge(sem("combined"), j + 1)
                if j:
                    act.wait_ge(sem("ssq3_done"), j)
                fn(sg[:, :], h[:, j, :], ACT.Square, accum_out=ssq[:, j:j + 1]).then_inc(sem("ssq3_done"), 1)
                if j:
                    act.wait_ge(sem("out_done"), j)
                    act.dma_start(out_v[:, j - 1, :], h[:, j - 1, :]).then_inc(sem("out_sent"), 16)
            act.wait_ge(sem("out_done"), J)
            act.dma_start(out_v[:, J - 1, :], h[:, J - 1, :]).then_inc(sem("out_sent"), 16)
            act.wait_ge(sem("out_sent"), 16 * J)

        @block.vector
        def _(dve):
            v = nc.vector
            own = [0]

            def step(ins):
                own[0] += 1
                ins.then_inc(sem("dve_step"), 1)
                dve.wait_ge(sem("dve_step"), own[0])

            def tt(out, in0, in1, op):
                return v.tensor_tensor(out, in0, in1, op)

            def bc(ap, axis, n):
                ap = ap.unsqueeze(axis)
                shape = list(ap.shape)
                shape[axis] = n
                return ap.to_broadcast(shape)

            dve.wait_ge(sem("vec_mm"), 1)
            v.tensor_copy(vec[:, :], ps[:, 0, 0:V_ROWS]).then_inc(sem("vec_done"), 1)
            dve.wait_ge(sem("param_mm"), 1)
            LR, LI, DT, Y, N, R, Q, S, C, H1, H2 = (t16[:, i, :] for i in (1, 2, 0, 3, 4, 5, 6, 7, 8, 9, 10))
            MAG, CT, SN, LBR, LBI, FR, FI, FIS, T1, T2, DEN, NRE, CR, CI = (t16[:, i, :] for i in range(11, 25))
            NI = t16[:, 25, :].bitcast(I32)
            PR2, PI2, PR4, PI4 = (t16[:, i, :] for i in range(26, 30))
            v.tensor_copy(LR, ps[:, 2, 0:G])
            v.tensor_copy(LI, ps[:, 2, G:2 * G])
            v.tensor_copy(work[:, 512:1024], ps[:, 1, :])
            dve.wait_ge(sem("csig_done"), 1)
            dve.wait_ge(sem("ssm_in"), 16 * 13)
            step(v.tensor_scalar(T1, DT, 0.0, None, ALU.add))
            tt(csil, csil, vec[:, V_C:V_C + 8], ALU.mult).then_inc(sem("csil_done"), 1)

            MAGIC = 12582912.0

            def exp(out, y):
                step(v.tensor_scalar(Y, y, -110.0, 100.0, ALU.max, ALU.min))
                step(v.tensor_scalar(N, Y, 1.4426950408889634, MAGIC, ALU.mult, ALU.add))
                step(v.tensor_scalar(N, N, -MAGIC, None, ALU.add))
                step(v.scalar_tensor_tensor(R, N, -0.693359375, Y, ALU.mult, ALU.add))
                step(v.scalar_tensor_tensor(R, N, 2.12194440e-4, R, ALU.mult, ALU.add))
                step(v.tensor_scalar(Q, R, 1.0 / 5040, None, ALU.mult))
                for c in (1.0 / 720, 1.0 / 120, 1.0 / 24, 1.0 / 6, 0.5, 1.0):
                    step(v.scalar_tensor_tensor(Q, Q, c, R, ALU.add, ALU.mult))
                step(v.tensor_scalar(N, N, -127.0, 128.0, ALU.max, ALU.min))
                step(v.tensor_scalar(NI, N, 127.0, 8388608.0, ALU.add, ALU.mult))
                step(v.scalar_tensor_tensor(out, Q, 1.0, NI.bitcast(F32), ALU.add, ALU.mult))

            exp(T1, DT)
            step(tt(T2, T1, LR, ALU.mult))
            exp(MAG, T2)
            step(tt(Y, T1, LI, ALU.mult))
            step(v.tensor_scalar(N, Y, 1.0 / (2.0 * np.pi), MAGIC, ALU.mult, ALU.add))
            step(v.tensor_scalar(N, N, -MAGIC, None, ALU.add))
            TURN1, TURN2 = 6.28125, 0.0019350051879882812
            step(v.scalar_tensor_tensor(R, N, -TURN1, Y, ALU.mult, ALU.add))
            step(v.scalar_tensor_tensor(R, N, -TURN2, R, ALU.mult, ALU.add))
            step(v.scalar_tensor_tensor(R, N, -(2.0 * np.pi - TURN1 - TURN2), R, ALU.mult, ALU.add))
            step(v.tensor_scalar(R, R, 0.5, None, ALU.mult))
            step(tt(H2, R, R, ALU.mult))
            fact = [1.0]
            for i in range(1, 17):
                fact.append(fact[-1] * i)
            step(v.tensor_scalar(S, H2, 1.0 / fact[13], None, ALU.mult))
            for i, c in enumerate((11, 9, 7, 5, 3)):
                step(v.scalar_tensor_tensor(S, S, (-1.0) ** (i + 1) / fact[c], H2, ALU.add, ALU.mult))
            step(v.scalar_tensor_tensor(S, S, 1.0, R, ALU.add, ALU.mult))
            step(v.tensor_scalar(C, H2, 1.0 / fact[16], None, ALU.mult))
            for i, c in enumerate((14, 12, 10, 8, 6, 4, 2)):
                step(v.scalar_tensor_tensor(C, C, (-1.0) ** (i + 1) / fact[c], H2, ALU.add, ALU.mult))
            step(v.tensor_scalar(C, C, 1.0, None, ALU.add))
            step(v.scalar_tensor_tensor(SN, S, 2.0, C, ALU.mult, ALU.mult))
            step(tt(CT, S, S, ALU.mult))
            step(v.tensor_scalar(CT, CT, -2.0, 1.0, ALU.mult, ALU.add))
            step(tt(LBR, MAG, CT, ALU.mult))
            step(tt(LBI, MAG, SN, ALU.mult))
            step(tt(DEN, LR, LR, ALU.mult))
            step(tt(H1, LI, LI, ALU.mult))
            step(tt(DEN, DEN, H1, ALU.add))
            step(v.reciprocal(DEN, DEN))
            step(v.tensor_scalar(NRE, LBR, -1.0, None, ALU.add))
            step(tt(FR, NRE, LR, ALU.mult))
            step(tt(H1, LBI, LI, ALU.mult))
            step(tt(FR, FR, H1, ALU.add))
            step(tt(FR, FR, DEN, ALU.mult))
            step(tt(FI, LBI, LR, ALU.mult))
            step(tt(H1, NRE, LI, ALU.mult))
            step(tt(FI, FI, H1, ALU.subtract))
            step(tt(FI, FI, DEN, ALU.mult))
            dve.wait_ge(sem("ident_done"), 1)
            step(v.tensor_scalar(FIS, FI, sgn, None, ALU.mult))
            step(tt(Bb_st, B_st, bc(FR, 2, CH), ALU.mult))
            step(tt(Bb_sw, B_sw, bc(FIS, 2, CH), ALU.mult))
            step(tt(Bb_st, Bb_st, Bb_sw, ALU.add))
            step(tt(Bb_sw, B_sw, bc(FR, 2, CH), ALU.mult))
            step(tt(B_st, B_st, bc(FIS, 2, CH), ALU.mult))
            step(tt(Bb_sw, Bb_sw, B_st, ALU.subtract))

            def cmul(or_, oi, ar_, ai, br_, bi, t):
                step(tt(or_, ar_, br_, ALU.mult))
                step(tt(t, ai, bi, ALU.mult))
                step(tt(or_, or_, t, ALU.subtract))
                step(tt(oi, ar_, bi, ALU.mult))
                step(tt(t, ai, br_, ALU.mult))
                step(tt(oi, oi, t, ALU.add))

            step(v.memset(pw_re[:, :, 0:1], 1.0))
            step(v.memset(pw_im[:, :, 0:1], 0.0))
            step(v.tensor_copy(pw_re[:, :, 1], LBR))
            step(v.tensor_copy(pw_im[:, :, 1], LBI))
            pt = ptmp[:, 0:64].rearrange("p (g t) -> p g t", g=G)
            for n in (1, 2, 4):
                src, dst = slice(1, n + 1), slice(n + 1, 2 * n + 1)
                cmul(pw_re[:, :, dst], pw_im[:, :, dst], pw_re[:, :, src], pw_im[:, :, src],
                     bc(pw_re[:, :, n], 2, n), bc(pw_im[:, :, n], 2, n), pt[:, :, 0:n])
            ptm = ptmp[:, 0:2304].rearrange("p (g t h) -> p g t h", g=G, t=9)
            BP4 = BP.rearrange("p g (t h) -> p g t h", t=J)
            for j in range(J):
                step(tt(BP4[:, :, j, :], Bb_st, bc(pw_re[:, :, 7 - j], 2, CH), ALU.mult))
                step(tt(ptm[:, :, j, :], Bb_sw, bc(pw_im[:, :, 7 - j], 2, CH), ALU.mult))
            step(v.scalar_tensor_tensor(BP4, ptm[:, :, 0:J, :], sgn, BP4, ALU.mult, ALU.add))
            for t in range(9):
                step(tt(CA[:, :, t, :], C_st, bc(pw_re[:, :, t], 2, CH), ALU.mult))
                step(tt(ptm[:, :, t, :], C_sw, bc(pw_im[:, :, t], 2, CH), ALU.mult))
            step(v.scalar_tensor_tensor(CA, CA, nsgn, ptm, ALU.mult, ALU.subtract))
            v.memset(pool_buf[0][:, 0, 0:1], 0.0).then_inc(sem("tables_done"), 1)
            step(tt(MAG, MAG, MAG, ALU.mult))
            step(tt(MAG, MAG, MAG, ALU.mult))
            step(tt(phase_r8, MAG, MAG, ALU.mult))

            def csquare(c, s):
                step(tt(T1, c, c, ALU.mult))
                step(tt(T2, s, s, ALU.mult))
                step(v.scalar_tensor_tensor(s, c, 2.0, s, ALU.mult, ALU.mult))
                step(tt(c, T1, T2, ALU.subtract))

            for _ in range(3):
                csquare(CT, SN)
            step(v.memset(cos_t[:, :, 0:1], 1.0))
            step(v.memset(sin_t[:, :, 0:1], 0.0))
            n = 1
            while n < P:
                cmul(cos_t[:, :, n:2 * n], sin_t[:, :, n:2 * n], cos_t[:, :, 0:n], sin_t[:, :, 0:n],
                     bc(CT, 2, n), bc(SN, 2, n), tab_tmp[:, :, 0:n])
                n *= 2
                if n < P:
                    csquare(CT, SN)
            step(v.tensor_scalar(sin_t, sin_t, sgn, None, ALU.mult))
            dve.wait_ge(sem("k0_mm"), 1)
            v.memset(pool_buf[0][:, 0, 0:1], 0.0).then_inc(sem("raw_used"), 1)

            dve.wait_ge(sem("ssq1_done"), J)
            step(v.tensor_scalar(rstd, ssq, 1.0 / D, EPS, ALU.mult, ALU.add))
            v.memset(pool_buf[0][:, 0, 0:1], 0.0).then_inc(sem("ms1_done"), 1)
            dve.wait_ge(sem("rstd1_done"), 1)
            for j in range(J):
                v.tensor_scalar(h[:, j, :], h[:, j, :], rstd[:, j:j + 1], None, ALU.mult).then_inc(sem("xn_done"), 1)
            dve.wait_ge(sem("mod1_mm"), 1)
            step(tt(S1, ps[:, 6, 0:8], vec[:, V_BMOD:V_BMOD + 8], ALU.add))
            step(tt(A1, ps[:, 6, 8:16], vec[:, V_BMOD + 8:V_BMOD + 16], ALU.add))
            step(v.scalar_tensor_tensor(A1, A1, 1.0, vec[:, V_N1:V_N1 + 8], ALU.add, ALU.mult))
            v.memset(pool_buf[0][:, 0, 0:1], 0.0).then_inc(sem("mod1_done"), 1)
            dve.wait_ge(sem("t_in"), 16 * J)
            dve.wait_ge(sem("bp_mm"), 1)
            for half in range(2):
                for k in range(1, KD, 2):
                    n = KD * half + k
                    dve.wait_ge(sem("ut_mm"), n + 1)
                    v.tensor_scalar(uT[:, k, HALF * half:HALF * half + HALF], ps[:, n % 4, :],
                                    A1[:, k:k + 1], S1[:, k:k + 1], ALU.mult, ALU.add).then_inc(sem("ut_dve"), 1)

            v.memset(zeros, 0.0).then_inc(sem("zeros_ready"), 1)

            def mod_part(n):
                return work[:, MODC * n:MODC * n + MODC] if n < 3 * D // MODC else gate2_bc[:, MODC * n - 3 * D:MODC * n - 3 * D + MODC]

            def mod_sums(first, end):
                for n in range(first, end):
                    i = NMOD1 + n
                    dve.wait_ge(sem(f"modw_in{i % MODR}"), 16 * (i // MODR + 1))
                    w, dst = modw[i % MODR], mod_part(n)
                    for k in range(KD):
                        if k == 0:
                            ins = v.tensor_scalar(dst, w[:, 0, :], csil[:, 0:1], None, ALU.mult)
                        else:
                            dve.wait_ge(sem("mod_sum"), KD * n + k)
                            ins = v.scalar_tensor_tensor(dst, w[:, k, :], csil[:, k:k + 1], dst, ALU.mult, ALU.add)
                        ins.then_inc(sem("mod_sum"), 1)

            def mod_biases(first, end):
                dve.wait_ge(sem("mod_sum"), KD * (NMOD - NMOD1))
                for b in range(first, end):
                    dst = mod_part(b // 2)[:, 128 * (b % 2):128 * (b % 2) + 128]
                    last = v.scalar_tensor_tensor(dst, ident[:, :], vec[:, V_BMOD + 2 * KD + b:V_BMOD + 2 * KD + b + 1], dst, ALU.mult, ALU.add)
                return last

            dve.wait_ge(sem("bias_in"), 32)
            dve.wait_ge(sem("ut_mm"), 2 * KD)
            mod_sums(0, 2)
            for q in range(4):
                dve.wait_ge(sem("u_mm"), 2 * q + 2)
                tt(U[:, :, 2 * q:2 * q + 2, :].rearrange("p g j h -> p j g h"),
                   ps[:, q, :].rearrange("p (j g h) -> p j g h", j=2, g=G),
                   bc(bu_bc.rearrange("p (g h) -> p g h", g=G), 1, 2), ALU.add).then_inc(sem("u_evac"), 1)
                mod_sums(2 + 2 * q, 4 + 2 * q)

            dve.wait_ge(sem("consts_done"), 1)
            step(v.reciprocal(pool_rcp, pool_rcp))
            for i in range(3):
                last = v.memset(pool_buf[i][:, :, 0:1], 0.0)
            last.then_inc(sem("pads_done"), 1)
            dve.wait_ge(sem("pads_done"), 1)
            mod_sums(10, 13)
            for gi in range(4):
                wi = 3 - gi
                dve.wait_ge(sem("gate_bank_free"), 2 * gi + 2)
                if gi:
                    dve.wait_ge(sem("pmix_mm"), gi)
                src, dst = 0, 1
                for lvl in range(wi + 1):
                    sh = 1 << lvl
                    X_, Y_ = pool_buf[src], pool_buf[dst]
                    if sh < J:
                        tt(Y_[:, sh:J, :], X_[:, sh:J, :], X_[:, 0:J - sh, :], ALU.add)
                    step(tt(Y_[:, 0:sh, 1:P + 1], X_[:, 0:sh, 1:P + 1], X_[:, J - sh:J, 0:P], ALU.add))
                    src, dst = dst, (2 if dst == 1 else 1)
                assert dst == m_buf[gi]
                win, m, X_ = pool_buf[src], pool_buf[dst], pool_buf[0]
                step(v.scalar_tensor_tensor(m[:, :, 1:P + 1], win[:, :, 1:P + 1], 1.0 / WINDOWS[wi], X_[:, :, 1:P + 1], ALU.mult, ALU.subtract))
                step(tt(m[:, :, 1:3], win[:, :, 1:3], pool_rcp[:, wi], ALU.mult))
                tt(m[:, :, 1:3], m[:, :, 1:3], X_[:, :, 1:3], ALU.subtract).then_inc(sem("m_ready"), 1)
                if gi == 0:
                    mod_sums(13, NMOD - NMOD1)
                if gi == 1:
                    mod_biases(0, 2 * KD)
                if gi == 2:
                    mod_biases(2 * KD, 4 * KD).then_inc(sem("mod_sums_done"), 1)

            v.memset(small[:, 51:52], 0.0).then_inc(sem("mul_done"), 2)

            def gate_pair(n, step2):
                for s in range(2):
                    for half in range(2):
                        it = n * 4 + (2 * s + half + 16 * step2)
                        dve.wait_ge(sem("gate_bank_free"), it + 9)
                        dve.wait_ge(sem("proj_mm"), it + 1)
                        sgh = sg[:, HALF * half:HALF * half + HALF]
                        if isinstance(n, int):
                            dst = merged[:, 2 * n + s, HALF * half:HALF * half + HALF]
                        else:
                            dst = merged[:, ds(n * 2 + s, 1), HALF * half:HALF * half + HALF].rearrange("p k t -> p (k t)")
                        if not step2:
                            tt(dst, sgh, ps[:, 5 + 2 * half, :], ALU.mult).then_inc(sem("mul_done"), 1)
                        else:
                            tt(sgh, sgh, ps[:, 5 + 2 * half, :], ALU.mult).then_inc(sem("sg_mul"), 1)
                            dve.wait_ge(sem("sg_mul"), it - 15)
                            tt(dst, dst, sgh, ALU.add).then_inc(sem("mul_done"), 1)

            with dve.Fori(0, 2) as n:
                gate_pair(n, 0)
            dve.wait_ge(sem("turned"), 1)
            for g in range(G):
                last = v.tensor_tensor_scan(SB[:, g, :], phase_r8[:, g:g + 1].to_broadcast([P, P]), SA[:, g, :], 0.0, ALU.mult, ALU.add)
            step(last)
            v.tensor_copy(SA[0:ST], SB[ST:P]).then_inc(sem("z_swapped"), 1)
            v.tensor_copy(SA[ST:P], SB[0:ST]).then_inc(sem("z_swapped"), 1)
            step(tt(U.rearrange("p g j h -> p j g h"), U.rearrange("p g j h -> p j g h"),
                    bc(d_bc.rearrange("p (g h) -> p g h", g=G), 1, J), ALU.mult))
            gate_pair(2, 0)
            for q in range(4):
                dve.wait_ge(sem("y_mm"), q + 1)
                gs = slice(4 * q, 4 * q + 4)
                last = tt(Ysp[:, :, gs, :].rearrange("p j g h -> p g j h"), ps[:, q, :].rearrange("p (g j h) -> p g j h", g=4, j=J),
                          U[:, gs], ALU.add)
            last.then_inc(sem("y_evac"), 1)
            dve.wait_ge(sem("ysq_done"), 1)
            step(v.tensor_scalar(gtmp, gtmp, 0.044715, 1.0, ALU.mult, ALU.add))
            tt(gtmp, gtmp, Y_flat, ALU.mult).then_inc(sem("gelu_arg"), 1)
            dve.wait_ge(sem("gelu_sig"), 1)
            tt(Y_flat, Y_flat, gtmp, ALU.mult).then_inc(sem("gelu_done"), 1)
            gate_pair(3, 0)
            for ob in range(2):
                for half in range(2):
                    dve.wait_ge(sem("glu_sig"), 2 * ob + half + 1)
                    cols = slice(HALF * half, HALF * half + HALF)
                    tt(zT[:, ob, cols], yT[:, ob, cols], sg[:, cols], ALU.mult).then_inc(sem("z_done"), 1)
            with dve.Fori(0, KD // 2) as n:
                gate_pair(n, 1)

            dve.wait_ge(sem("mod_mm"), 1)
            dve.wait_ge(sem("n2_in"), 16)
            v.tensor_copy(work[:, 0:2048], ps[:, 0:4, :].rearrange("p b n -> p (b n)"))
            v.scalar_tensor_tensor(A2_bc, ps[:, 4:6, :].rearrange("p b n -> p (b n)"), 1.0, u2t[0], ALU.add, ALU.mult)
            step(v.memset(small[:, 51:52], 0.0))
            v.memset(small[:, 51:52], 0.0).then_inc(sem("mod_rows_done"), 1)
            dve.wait_ge(sem("x_again"), 16)

            for t in range(J):
                dve.wait_ge(sem("wout_done"), t + 1)
                if t >= 2:
                    dve.wait_ge(sem("u2t_mm"), t - 1)
                    dve.wait_ge(sem(f"u2_out{t % 2}"), 16 * (t // 2))
                for half in range(2):
                    cols = slice(HALF * half, HALF * half + HALF)
                    tt(u2t[t % 2][:, cols], ps[:, 2 * (t % 2) + half, :], gate1_bc[:, cols], ALU.mult).then_inc(sem("h_psum_read"), 1)
                dve.wait_ge(sem("h_psum_read"), 2 * t + 2)
                tt(h[:, t, :], h[:, t, :], u2t[t % 2], ALU.add).then_inc(sem("h_done"), 1)
                dve.wait_ge(sem("rstd2_done"), t + 1)
                step(v.scalar_tensor_tensor(u2t[t % 2], h[:, t, :], rstd[:, t:t + 1], A2_bc, ALU.mult, ALU.mult))
                tt(u2t[t % 2], u2t[t % 2], S2_bc, ALU.add).then_inc(sem("u2_done"), 1)

            dve.wait_ge(sem("router_mm"), J)
            dve.wait_ge(sem("rbias_in"), 32)
            step(tt(L, ps[:, 6, 0:J * (NG + NE)].rearrange("p (j n) -> p j n", j=J), bc(rbias, 1, J), ALU.add))
            coarse, fine = L[:, :, 0:NG], L[:, :, NG:NG + NE].rearrange("p j (g i) -> p j g i", g=NG)
            m1, m2, mc, csum, t8 = (rsc[:, i, :] for i in range(5))

            def first_best(out, val, n, best, scratch):
                step(v.tensor_reduce(best, val, AX.X, ALU.max))
                step(tt(out, val, bc(best, 2, n), ALU.is_equal))
                step(tt(out, out, bc(falling[:, 0:n], 1, J), ALU.mult))
                step(v.tensor_reduce(scratch, out, AX.X, ALU.max))
                step(tt(out, out, bc(scratch, 2, n), ALU.is_equal))

            step(v.tensor_scalar(falling, iota[:, 0:8], -1.0, 9.0, ALU.mult, ALU.add))
            first_best(g_hot, coarse, NG, mc, t8)
            tt(cdiff, coarse, bc(mc, 2, NG), ALU.subtract).then_inc(sem("coarse_diff"), 1)
            step(tt(fsel4, fine.rearrange("p j g i -> p j i g"), bc(g_hot, 2, EPG), ALU.mult))
            step(v.tensor_reduce(fsel, fsel4, AX.X, ALU.add))
            first_best(hot[0], fsel, EPG, m1, t8)
            step(v.scalar_tensor_tensor(fsel, hot[0], -3.0e38, fsel, ALU.mult, ALU.add))
            first_best(hot[1], fsel, EPG, m2, t8)
            tt(fdiff, m2, m1, ALU.subtract).then_inc(sem("fine_diff"), 1)
            dve.wait_ge(sem("coarse_exp"), 1)
            step(v.tensor_reduce(csum, cexp, AX.X, ALU.add))
            step(v.reciprocal(csum, csum))
            dve.wait_ge(sem("fine_sig"), 1)
            step(tt(wpick, wpick, bc(csum, 1, 2), ALU.mult))
            for k in range(2):
                step(tt(pick[k].rearrange("p j (g i) -> p j g i", g=NG), bc(g_hot, 3, EPG), bc(hot[k], 2, NG), ALU.mult))
            step(tt(M3, pick[0], pick[1], ALU.add))
            step(v.memset(Mb3[:, 0, :], 0.0))
            for j in range(1, J):
                step(tt(Mb3[:, j, :], Mb3[:, j - 1, :], M3[:, j - 1, :], ALU.add))
            tt(M_total, Mb3[:, J - 1, :], M3[:, J - 1, :], ALU.add).then_inc(sem("picks_done"), 1)
            dve.wait_ge(sem("rank_mm"), 1)
            rank = ps[:, 7, 0:J * NE].rearrange("p (j e) -> p j e", j=J)
            step(tt(cmp_t, bc(ps[:, 7, J * NE:J * NE + NE], 2, 16), bc(whole, 1, NE), ALU.is_gt))
            step(v.tensor_reduce(ntile, cmp_t, AX.X, ALU.add))
            step(v.tensor_scalar(ntile, ntile, 1.0, None, ALU.max))
            step(v.memset(tstart[:, 0:1], 0.0))
            step(v.tensor_tensor_scan(tstart[:, 1:NE + 1], ones[:, 0:NE], ntile, 0.0, ALU.mult, ALU.add))
            step(v.tensor_copy(tstart_i[:, :], tstart))
            for k in range(2):
                step(tt(Mp3, rank, pick[k], ALU.mult))
                step(v.tensor_reduce(rk[:, k, :], Mp3, AX.X, ALU.add))
                step(tt(Mp3, bc(tstart[:, 0:NE], 1, J), pick[k], ALU.mult))
                step(v.tensor_reduce(hi[:, k, :], Mp3, AX.X, ALU.add))
            step(tt(cmp_r, bc(rk.rearrange("p k j -> p (k j)"), 2, 15), bc(whole[:, 1:16], 1, 2 * J), ALU.is_ge))
            step(v.tensor_reduce(fl, cmp_r, AX.X, ALU.add))
            hi_f, rk_f = hi.rearrange("p k j -> p (k j)"), rk.rearrange("p k j -> p (k j)")
            step(tt(hi_f, hi_f, fl, ALU.add))
            step(v.scalar_tensor_tensor(rk_f, fl, -float(TS), rk_f, ALU.mult, ALU.add))
            step(tt(oh_lo, bc(iota, 1, 2 * J), bc(rk_f, 2, TS), ALU.is_equal))
            step(tt(oh_hi, bc(iota[:, 0:MAX_TILES], 1, 2 * J), bc(hi_f, 2, MAX_TILES), ALU.is_equal))
            for k in range(2):
                last = tt(oh_hi[:, J * k:J * k + J, :], oh_hi[:, J * k:J * k + J, :], bc(tokid, 2, MAX_TILES), ALU.mult)
            last.then_inc(sem("onehots_done"), 1)
            step(v.tensor_scalar(fl, hi_f, float(TS), None, ALU.mult))
            step(tt(fl, fl, rk_f, ALU.add))
            step(v.tensor_copy(ypos[:, :], fl))
            step(v.tensor_copy(wsave, wpick))
            dve.wait_ge(sem("slot_mm"), 1)
            v.tensor_copy(slot_tok[0:TS, 0:MAX_TILES], ps[0:TS, 0, 0:MAX_TILES]).then_inc(sem("routed"), 1)

            dve.wait_ge(sem("routed"), 1)
            n_tiles = dve.value_load(tstart_i[0:1, NE:NE + 1], min_val=NE, max_val=MAX_TILES)

            def times_up(g):
                dve.wait_ge(sem("silu_done"), g + 1)
                dve.wait_ge(sem("up_done"), g + 1)
                tt(hidden, hidden, ps[:, 1, 0:HE], ALU.mult).then_inc(sem("hidden_ready"), 1)

            def take_hidden(g):
                dve.wait_ge(sem("hidden_used"), g)
                v.tensor_copy(sg[:, HALF:HALF + HE], ps[:, 6, 0:HE]).then_inc(sem("hiddent_ready"), 1)

            def take_y(g):
                dve.wait_ge(sem("tiles_done"), g)
                dve.wait_ge(sem("y_rows_out"), g * 32)
                tt(y_tile, ps[:, 2, :], gate2_bc[:, 0:HD], ALU.mult).then_inc(sem("y_copied"), 1)

            dve.wait_ge(sem("gate2_mm"), 1)
            for c in range(2):
                v.tensor_copy(gate2_bc[TS * c:TS * c + TS, 0:HD], ps[TS * c:TS * c + TS, 4 + c, :]).then_inc(sem("gate2_rows"), 1)
            dve.wait_ge(sem("gate2_rows"), 2)
            v.memset(small[:, 51:52], 0.0).then_inc(sem("y_copied"), 1)
            times_up(0)
            with dve.Fori(1, n_tiles) as g:
                take_hidden(g)
                times_up(g)
                take_y(g)
            take_hidden(n_tiles)
            take_y(n_tiles)

            dve.wait_ge(sem("gf_in"), 16)
            for t in range(J + 1):
                if t < J:
                    dve.wait_ge(sem(f"ycomb_in{t}"), 32)
                    for k in range(2):
                        ins = v.scalar_tensor_tensor(h[:, t, :], ycomb[2 * t + k], wsave[:, k, t:t + 1], h[:, t, :], ALU.mult, ALU.add)
                        if k == 0:
                            ins.then_inc(sem("first_added"), 1)
                            dve.wait_ge(sem("first_added"), t + 1)
                    ins.then_inc(sem("combined"), 1)
                if t:
                    j = t - 1
                    dve.wait_ge(sem("rstd3_done"), j + 1)
                    v.scalar_tensor_tensor(h[:, j, :], h[:, j, :], rstd[:, j:j + 1], gf_bc[:, :], ALU.mult, ALU.mult).then_inc(sem("out_done"), 1)


_OUTS = [((1, SEQ, D), "float32")]


def kernel(**inputs):
    import numpy as _np
    import concourse.bacc as _bacc
    from concourse import mybir as _mybir
    from concourse.bass_utils import run_bass_kernel_spmd as _run

    nc = _bacc.Bacc("TRN2", target_bir_lowering=False, num_devices=1)
    arrays, args = {}, {}
    for name, value in inputs.items():
        value = _np.ascontiguousarray(value)
        arrays[f"in_{name}_dram"] = value
        args[name] = nc.dram_tensor(f"in_{name}_dram", value.shape, _mybir.dt.from_np(value.dtype), kind="ExternalInput").ap()
    for shape, dtype in _OUTS:
        args["out"] = nc.dram_tensor("out_0_dram", shape, _mybir.dt.from_np(_np.dtype(dtype)), kind="ExternalOutput").ap()
    program(nc, args)
    r = _run(nc, [arrays], core_ids=[0])
    return r.results[0]["out_0_dram"]
```

```python
from contextlib import ExitStack

import numpy as np

import concourse.bass as bass
from concourse import mybir

ALU = mybir.AluOpType
ACT = mybir.ActivationFunctionType
AX = mybir.AxisListType
F32 = mybir.dt.float32
I32 = mybir.dt.int32
ds = bass.ds

P = 128
D = 1024
SEQ = 1024
J = SEQ // P
KD = D // P
HALF = 512
D_SSM, D_POOL = 256, 512
G, CH, ST = 16, 16, 64
WINDOWS = (2, 4, 8, 16)
NG, EPG = 4, 8
NE = NG * EPG
DE = 512
KE = DE // P
EPS = 1e-6
TS = 64
MAX_TILES = 2 * SEQ // TS + NE
RING = 3
MODC = 256

V_BMOD, V_N1, V_N2, V_BIN, V_PSC, V_BGLU, V_C, V_ROWS = 0, 48, 56, 64, 86, 90, 92, 100

A_UT = 0
A_WRING = 8192
A_BT = 11264
A_WSP = A_BT + 4096
A_TMP = A_WSP + 6144
A_MERGED = A_WSP + 1024
A_POOL = 23552
A_COS = A_POOL + 3096
A_T = A_COS + 2064
A_CA = A_T + 2048
A_BPT = A_CA + 2304
A_SIN = A_BPT + 2048
A_WOUT = A_MERGED + 8192
A_ROUTE = A_WOUT + 8192
ARENA = A_SIN + 2048


def program(nc, a):
    ctx = ExitStack()
    sems = {}

    def sem(name):
        if name not in sems:
            sems[name] = ctx.enter_context(nc.semaphore(name))
        return sems[name]

    def sb(name, shape, dt=F32):
        return ctx.enter_context(nc.sbuf_tensor(name, shape, dt))

    with ctx:
        ps = ctx.enter_context(nc.psum_tensor("ps", [P, 8, HALF], F32))
        u2_rows = nc.dram_tensor("u2_rows", [SEQ, D], F32, kind="Internal").ap()
        y_rows = nc.dram_tensor("y_rows", [MAX_TILES * TS, D], F32, kind="Internal").ap()

        H = sb("H", [P, J * D])
        arena = sb("arena", [P, ARENA])
        work = sb("work", [P, 3456])
        gate2_bc = sb("gate2_bc", [P, D])
        ident = sb("ident", [P, P])
        ones = sb("ones", [P, P])
        vec = sb("vec", [P, V_ROWS])
        small = sb("small", [P, 96])
        bias_bc = sb("bias_bc", [P, 512])
        route = sb("route", [P, 204])
        tstart_i = sb("tstart_i", [P, NE + 2], I32)
        slot_tok = sb("slot_tok", [P, MAX_TILES + 2], I32)
        idx_now = sb("idx_now", [P, 2], I32)
        ypos = sb("ypos", [P, 2 * J], I32)

        def ar(off, n):
            return arena[:, off:off + n]

        h = H[:, :].rearrange("p (j d) -> p j d", j=J)
        uT = ar(A_UT, 8192).rearrange("p (k t) -> p k t", k=KD)
        wring = [ar(A_WRING + 1536 * s, 1536) for s in range(2)]
        wgate = [w[:, 0:1024].rearrange("p (k n) -> p k n", k=KD) for w in wring]
        wproj = [w[:, 1024:1536].rearrange("p (k n) -> p k n", k=4) for w in wring]
        bT = ar(A_BT, 4096).rearrange("p (g t) -> p g t", g=4)
        merged = ar(A_MERGED, 8192).rearrange("p (k t) -> p k t", k=KD)
        wsp = ar(A_WSP, 6144).rearrange("p (k n) -> p k n", k=KD)
        pool_buf = [ar(A_POOL + 1032 * i, 1032).rearrange("p (j c) -> p j c", j=J) for i in range(3)]
        cos_t = ar(A_COS, 2048).rearrange("p (g c) -> p g c", g=G)
        Xs = ar(A_COS, 2064).rearrange("p (g c) -> p g c", g=G)
        Tm = ar(A_T, 2048).rearrange("p (g n) -> p g n", g=G)
        CA = ar(A_CA, 2304).rearrange("p (g t h) -> p g t h", g=G, t=9)
        BPT = ar(A_BPT, 2048).rearrange("p (g n) -> p g n", g=G)
        yT = ar(A_BPT, 2048).rearrange("p (k t) -> p k t", k=2)
        sin_t = ar(A_SIN, 2048).rearrange("p (g c) -> p g c", g=G)
        zT = ar(A_SIN, 2048).rearrange("p (k t) -> p k t", k=2)
        modw = [ar(A_BT, 2048), ar(A_BT + 2048, 2048), ar(A_TMP, 2048), ar(A_WRING, 2048)]
        modw = [m.rearrange("p (k n) -> p k n", k=KD) for m in modw]
        MODR = len(modw)
        wout = ar(A_WOUT, 8192).rearrange("p (k n) -> p k n", k=KD)
        BP = ar(A_UT, 2048).rearrange("p (g n) -> p g n", g=G)
        ptmp = ar(A_UT + 2048, 2304)
        K0 = arena[0:CH, A_UT + 4352:A_UT + 8192].rearrange("p (g n) -> p g n", g=G)
        B_st, B_sw, C_st, C_sw = (work[:, 256 * i:256 * i + 256].rearrange("p (g h) -> p g h", g=G) for i in range(4))
        C_rows = work[:, 1024:1536].rearrange("p (s b n) -> p s b n", s=2, b=2)
        lam_rows = work[0:G, 1536:1792].rearrange("p (s n) -> p s n", s=2)
        pw_re = work[:, 1792:1936].rearrange("p (g t) -> p g t", g=G)
        pw_im = work[:, 1936:2080].rearrange("p (g t) -> p g t", g=G)
        Bb_st = work[:, 2080:2336].rearrange("p (g h) -> p g h", g=G)
        Bb_sw = work[:, 2336:2592].rearrange("p (g h) -> p g h", g=G)
        t16 = work[:, 2592:3456].rearrange("p (v g) -> p v g", g=G)
        vrows = ar(A_POOL, P)
        tab_tmp = ar(A_POOL + P, 1024).rearrange("p (g c) -> p g c", g=G)
        d_bc = bias_bc[:, 0:256]
        bu_bc = bias_bc[:, 256:512]
        U = H[:, 0:2048].rearrange("p (g j h) -> p g j h", g=G, j=J)
        V = H[:, 2048:4096].rearrange("p (g c) -> p g c", g=G)
        SA = H[:, 4096:6144].rearrange("p (g c) -> p g c", g=G)
        SB = H[:, 6144:8192].rearrange("p (g c) -> p g c", g=G)
        Ysp = H[:, 4096:6144].rearrange("p (j g h) -> p j g h", j=J, g=G)

        zeros = work[:, 3072:3328]
        POOL_OUT = (0, 2)
        OUT_ORDER = (1, 3, 0, 4, 2, 5, 6, 7)
        mod1_rows = [ar(A_POOL + 1160, D)[0:1, :], gate2_bc[0:1, :]]
        gate1_bc, S2_bc, A2_bc = (work[:, 1024 * i:1024 * i + 1024] for i in range(3))
        slotw = [ar(12288 * s, 12288) for s in range(RING)]
        e_gate = [w[:, 0:4096].rearrange("p (k n) -> p k n", k=KD) for w in slotw]
        e_up = [w[:, 4096:8192].rearrange("p (k n) -> p k n", k=KD) for w in slotw]
        e_down = [w[:, 8192:12288].rearrange("p (k n) -> p k n", k=KE) for w in slotw]
        x_land = [work[0:TS, 1024 * i:1024 * i + 1024] for i in range(2)]
        x_tile = work[TS:2 * TS, 0:1024]
        y_tile = [work[:, 2048 + 512 * i:2560 + 512 * i] for i in range(2)]
        xT = gate2_bc[:, 512:1024].rearrange("p (k t) -> p k t", k=KD)
        u2t = [ar(A_ROUTE + 1024 * i, 1024) for i in range(2)]
        u2T = [ar(A_ROUTE + 2048 + 1024 * i, 1024).rearrange("p (k t) -> p k t", k=KD) for i in range(2)]
        ROUTERW = KD * (NG + NE)
        rw = ar(A_ROUTE + 4096, ROUTERW).rearrange("p (k n) -> p k n", k=KD)
        assert A_ROUTE + 4096 + ROUTERW <= ARENA
        SLOT2_DOWN = 12288 * 2 + 8192
        assert SLOT2_DOWN >= A_WOUT + 8192 and A_MERGED >= 12288 + 4096

        csil = small[:, 0:8]
        A1, S1 = small[:, 8:16], small[:, 16:24]
        ssq, rstd = small[:, 32:40], small[:, 40:48]
        half_neg = small[:, 48:49]
        phase_r8 = route[:, 0:16]
        sgn = small[:, 49:50]
        nsgn = small[:, 50:51]
        pool_rcp = route[:, 16:80].rearrange("p (w j c) -> p w j c", w=4, j=J)
        iota = route[:, 16:16 + TS]
        tokid = route[:, 144:152]
        rbias = route[:, 152:188]
        whole = route[:, 188:204]
        sg = sb("sg", [P, 2 * HALF])
        HE, HD = DE // 2, D // 2
        hidden = sg[:, 0:HE]
        hiddenT = sg[:, HALF:HALF + HE].rearrange("p (f h t) -> p h f t", f=2, h=2)

        ycomb = [ar(1024 * i, 1024) for i in range(2 * J)]
        gf_bc = ar(12288 * 2, D)
        gtmp, Y_flat = H[:, 6144:8192], H[:, 4096:6144]
        m_buf = [1, 2, 1, 2]
        rooms = [[work[:, 0:3072], 0], [ar(SLOT2_DOWN, 4096), 0]]

        def table(n):
            room = next(r for r in rooms if r[1] + n <= r[0].shape[-1])
            room[1] += n
            return room[0][:, room[1] - n:room[1]]

        def per_tile(n):
            return table(J * n).rearrange("p (j n) -> p j n", j=J)

        later = table(P)
        L = per_tile(NG + NE)
        rsc = table(8 * J).rearrange("p (v j) -> p v j", j=J)
        falling = table(EPG)
        g_hot, cdiff, cexp = per_tile(NG), per_tile(NG), per_tile(NG)
        fsel4 = per_tile(NE).rearrange("p j (i g) -> p j i g", g=NG)
        fsel, fdiff = per_tile(EPG), table(J)
        hot = [per_tile(EPG), per_tile(EPG)]
        wpick = table(2 * J).rearrange("p (k j) -> p k j", k=2)
        pick = [per_tile(NE), per_tile(NE)]
        M_all, M_before = table(J * NE), table(J * NE)
        M3, Mb3 = (m.rearrange("p (j e) -> p j e", j=J) for m in (M_all, M_before))
        Mp3 = per_tile(NE)
        M_total, ntile, tstart = table(NE), table(NE), table(NE + 2)
        cmp_t = table(16 * NE).rearrange("p (e m) -> p e m", m=16)
        cmp_r = table(15 * 2 * J).rearrange("p (e m) -> p e m", m=15)
        fl = table(2 * J)
        rk, hi = (table(2 * J).rearrange("p (k j) -> p k j", k=2) for _ in range(2))
        oh_lo = table(2 * J * TS).rearrange("p (i s) -> p i s", s=TS)
        oh_hi = table(2 * J * MAX_TILES).rearrange("p (i s) -> p i s", s=MAX_TILES)
        wsave = small[:, 56:72].rearrange("p (k j) -> p k j", k=2)

        x_v = a["x"].rearrange("b (c j) d -> (b c) j d", j=J)
        out_v = a["out"].rearrange("b (c j) d -> (b c) j d", j=J)
        u2_v = u2_rows.rearrange("(c j) d -> c j d", j=J)
        wmod_v = a["w_mod"].rearrange("l (k p) n -> p (l k) n", p=P)
        win_v = a["w_in"].rearrange("l (k p) n -> p (l k) n", p=P)
        wps_v = a["w_proj_ssm"].rearrange("l (k p) n -> p (l k) n", p=P)
        wpp_v = a["w_proj_pool"].rearrange("l (k p) n -> p (l k) n", p=P)
        wout_v = a["w_out"].rearrange("l (k p) n -> p (l k) n", p=P)
        eg_v = a["moe_w_gate"].rearrange("l (g i) (k p) n -> (l g) i p k n", p=P, g=NG)
        eu_v = a["moe_w_up"].rearrange("l (g i) (k p) n -> (l g) i p k n", p=P, g=NG)
        ed_v = a["moe_w_down"].rearrange("l (g i) (k p) n -> (l g) i p k n", p=P, g=NG)
        GP0 = D_SSM + D_POOL + D
        GS0 = D_SSM + D_POOL

        def rows128(ap):
            return ap.rearrange("l (r n) -> (l r) n", n=P)

        def bcast(ap, n):
            return ap.rearrange("(o n) -> o n", o=1).to_broadcast([P, n]) if len(ap.shape) == 1 else ap.to_broadcast([P, n])

        wglu = sb("wglu", [P, 2 * D_SSM])[:, :].rearrange("p (k n) -> p k n", k=2)
        wpool = sb("wpool", [P, 4 * P])[:, :].rearrange("p (k n) -> p k n", k=4)
        NMOD1 = 2 * D // MODC
        NMOD = 6 * D // MODC

        def stand(eng, name):
            eng.sem_inc(sem("stood_" + name), 1)

        block = ctx.enter_context(nc.Block())

        @block.sync
        def _(sp):
            def load(dst, src, name):
                sp.dma_start(dst, src).then_inc(sem(name), 16)

            at = 0
            for name in ("b_mod", "norm1_g", "norm2_g", "b_in", "pool_scale", "ssm_b_glu", "c"):
                src = rows128(a[name])
                load(vrows[at:at + src.shape[0], :], src, "vrows_in")
                at += src.shape[0]
            for s, name in enumerate(("ssm_lam_re", "ssm_lam_im")):
                for half in range(2):
                    load(lam_rows[:, s, ST * half:ST * half + ST],
                         a[name].rearrange("l g p -> (l g) p"), "ssm_in")
            load(t16[:, 0, :], bcast(a["ssm_log_dt"], G), "ssm_in")
            for s, (first, second) in enumerate((("re", "im"), ("im", "re"))):
                for half, part in enumerate((first, second)):
                    load((B_st, B_sw)[s][ST * half:ST * half + ST, :, :],
                         a["ssm_b_" + part].rearrange("l g p h -> p (l g) h"), "ssm_in")
                    load(C_rows[:, s, :, ST * half:ST * half + ST],
                         a["ssm_c_" + part].rearrange("l (b g) h p -> (l g h) b p", b=2), "ssm_in")
            for i in range(NMOD1):
                if i >= MODR:
                    sp.wait_ge(sem("modw_used"), i - MODR + 1)
                load(modw[i % MODR], wmod_v[:, :, MODC * i:MODC * i + MODC], f"modw_in{i % MODR}")
                if i >= MODR - 1 and i < MODR + 3:
                    q = i - MODR + 1
                    load(h[:, 2 * q:2 * q + 2, :], x_v[:, 2 * q:2 * q + 2, :], f"x_in{q}")
            load(wsp[:, :, 0:D_SSM], win_v[:, :, 0:D_SSM], "wsp_in")
            load(wsp[:, :, D_SSM:768], win_v[:, :, D_SSM:768], "wsp_pool_in")
            load(d_bc, bcast(a["ssm_d"], D_SSM), "bias_in")
            load(bu_bc, bcast(a["b_in"][:, 0:D_SSM], D_SSM), "bias_in")
            for i in range(NMOD1, NMOD):
                if i - MODR < NMOD1:
                    sp.wait_ge(sem("modw_used"), i - MODR + 1)
                else:
                    sp.wait_ge(sem("mod_sum"), KD * (i - MODR - NMOD1 + 1))
                load(modw[i % MODR], wmod_v[:, :, MODC * i:MODC * i + MODC], f"modw_in{i % MODR}")
            load(wglu, a["ssm_w_glu"].rearrange("l (k p) n -> p (l k) n", p=P), "wglu_in")
            load(wpool, a["pool_w"].rearrange("l g c d -> c (l g) d"), "wpool_in")
            load(rbias[:, 0:NG], bcast(a["router_coarse_b"], NG), "rbias_in")
            load(rbias[:, NG:NG + NE], bcast(a["router_fine_b"], NE), "rbias_in")
            def gate_weights(item, step2, s, wait):
                proj_v, nk, first = (wps_v, 2, GS0) if step2 else (wpp_v, 4, GP0)
                if wait is not None:
                    sp.wait_ge(sem("gate_mm"), wait)
                sp.dma_start(wgate[s], win_v[:, :, ds(item * 128 + (first - step2 * D), P)]).then_inc(sem(f"wring_in{s}"), 16)
                sp.dma_start(wproj[s][:, 0:nk, :], proj_v[:, :, ds(item * 128 - step2 * D, P)]).then_inc(sem(f"wproj_in{s}"), 16)

            sp.wait_ge(sem("mod_sum"), KD * (NMOD - NMOD1))
            for s in range(2):
                gate_weights(s, 0, s, None)
            with sp.Fori(1, KD // 2) as n:
                for s in range(2):
                    gate_weights(n * 2 + s, 0, s, n * 4 + (2 * s - 2))
            with sp.Fori(KD // 2, KD) as n:
                for s in range(2):
                    gate_weights(n * 2 + s, 1, s, n * 4 + (2 * s - 2))
            sp.wait_ge(sem("z_done"), 4)
            load(wout, wout_v, "wout_in")
            load(h, x_v, "x_again")
            load(u2t[0], bcast(a["norm2_g"], D), "n2_in")
            sp.wait_ge(sem("gate_mm"), 4 * KD)
            load(rw[:, :, 0:NG], a["router_coarse_w"].rearrange("l (k p) n -> p (l k) n", p=P), "rw_in")
            load(rw[:, :, NG:NG + NE], a["router_fine_w"].rearrange("l (k p) n -> p (l k) n", p=P), "rw_in")

            def weights(view, q):
                g, i = q % NG, q // NG
                return view[ds(g, 1), ds(i, 1)].rearrange("g i p k n -> p (g i k) n")

            def load_gate(q, s):
                sp.dma_start(e_gate[s], weights(eg_v, q)).then_inc(sem(f"gate_in{s}"), 16)

            def load_up(q, s):
                sp.dma_start(e_up[s], weights(eu_v, q)).then_inc(sem(f"up_in{s}"), 16)

            def load_gate_up(q, s):
                load_gate(q, s)
                load_up(q, s)

            def load_down(q, s):
                sp.dma_start(e_down[s], weights(ed_v, q)).then_inc(sem(f"down_in{s}"), 16)

            def load_expert(q, s):
                load_gate_up(q, s)
                load_down(q, s)

            load_expert(0, 0)
            load_gate(1, 1)
            sp.wait_ge(sem("wout_done"), J)
            load_up(1, 1)
            for s in range(2):
                sp.wait_ge(sem(f"u2_out{s}"), 16 * (J // 2))
            load_down(1, 1)
            load_gate_up(2, 2)
            sp.wait_ge(sem("routed"), 1)
            for p in range(2):
                sp.wait_ge(sem(f"x_rows_in{p}"), 16)
            load_down(2, 2)

            def next_expert(e, s):
                last = sp.value_load(tstart_i[0:1, ds(e - (RING - 1), 1)], min_val=1, max_val=MAX_TILES)
                sp.wait_ge(sem("up_done"), last)
                load_gate_up(e, s)
                sp.wait_ge(sem("tiles_done"), last)
                load_down(e, s)

            with sp.Fori(1, NE // RING) as n:
                for s in range(RING):
                    next_expert(n * RING + s, s)
            for e in range(NE // RING * RING, NE):
                next_expert(e, e % RING)
            last = sp.value_load(tstart_i[0:1, NE - 2:NE - 1], min_val=1, max_val=MAX_TILES)
            sp.wait_ge(sem("tiles_done"), last)
            load(gf_bc, bcast(a["norm_f_g"], D), "gf_in")
            for j in OUT_ORDER:
                pools = j in POOL_OUT
                sp.wait_ge(sem("out_pool" if pools else "out_dve"), sum((i in POOL_OUT) == pools for i in range(j + 1)))
                load(out_v[:, j, :], h[:, j, :], "out_sent")
            sp.wait_ge(sem("out_sent"), 16 * J)

        @block.gpsimd
        def _(pool):
            own = [0]

            def step(ins):
                own[0] += 1
                ins.then_inc(sem("pool_step"), 1)
                pool.wait_ge(sem("pool_step"), own[0])

            gp = nc.gpsimd
            gp.memset(ident[:, :], 0.0)
            gp.memset(ones[:, :], 1.0)
            gp.memset(half_neg, -0.5)
            gp.memset(nsgn, 1.0)
            step(gp.memset(sgn, -1.0))
            step(gp.memset(nsgn[ST:P, :], -1.0))
            step(gp.memset(sgn[ST:P, :], 1.0))
            gp.affine_select(out=ident[:, :], in_=ident[:, :], compare_op=ALU.not_equal, fill=1.0,
                             base=0, pattern=[[-1, P]], channel_multiplier=1).then_inc(sem("ident_done"), 1)
            gp.memset(K0, 0.0).then_inc(sem("k0_zero"), 1)
            gp.iota(whole, [[TS, 16]], base=0, channel_multiplier=0, allow_small_or_imprecise_dtypes=True)
            gp.iota(tokid, [[1, J]], base=0, channel_multiplier=J, allow_small_or_imprecise_dtypes=True)
            for w in range(4):
                gp.iota(pool_rcp[:, w], [[1, J], [J, 2]], base=1, channel_multiplier=0,
                        allow_small_or_imprecise_dtypes=True)
            step(gp.memset(slot_tok[:, :], 0))
            for w in range(4):
                last = gp.tensor_scalar(pool_rcp[:, w], pool_rcp[:, w], float(WINDOWS[w]), None, ALU.min)
            last.then_inc(sem("consts_done"), 1)

            pool.wait_ge(sem("ssq1_done"), J)
            step(gp.tensor_scalar(rstd, ssq, 1.0 / D, EPS, ALU.mult, ALU.add))
            gp.tensor_tensor(rstd, rstd, half_neg.to_broadcast([P, J]), ALU.pow).then_inc(sem("rstd1_done"), 1)

            pool.wait_ge(sem("in_evac"), 12)
            gp.tensor_tensor(SA, SA, cos_t, ALU.mult)
            step(gp.tensor_tensor(SB, SB, sin_t, ALU.mult))
            gp.tensor_tensor(SA, SA, SB, ALU.subtract).then_inc(sem("turned"), 1)
            pool.wait_ge(sem("z_swapped"), 2)
            step(gp.tensor_tensor(SB, SB, cos_t, ALU.mult))
            step(gp.tensor_tensor(SA, SA, sin_t, ALU.mult))
            step(gp.memset(Xs[:, :, 0:1], 0.0))
            gp.tensor_tensor(Xs[:, :, 1:P + 1], SB, SA, ALU.add).then_inc(sem("state_done"), 1)

            gp.iota(iota, [[1, TS]], base=0, channel_multiplier=0, allow_small_or_imprecise_dtypes=True)

            for j in range(J):
                pool.wait_ge(sem("ssq2_done"), j + 1)
                step(gp.tensor_scalar(rstd[:, j:j + 1], ssq[:, j:j + 1], 1.0 / D, EPS, ALU.mult, ALU.add))
                gp.tensor_tensor(rstd[:, j:j + 1], rstd[:, j:j + 1], half_neg, ALU.pow).then_inc(sem("rstd2_done"), 1)

            pool.wait_ge(sem("u2_done"), J)
            step(gp.memset(later, 1.0))
            gp.affine_select(out=later, in_=later, compare_op=ALU.is_gt, fill=0.0,
                             base=0, pattern=[[1, P]], channel_multiplier=-1).then_inc(sem("later_done"), 1)
            pool.wait_ge(sem("tiles_counted"), 1)
            pairs = pool.value_load(tstart_i[0:1, NE + 1:NE + 2], min_val=NE // 2, max_val=MAX_TILES // 2)
            pool.wait_ge(sem("routed"), 1)
            for s in range(2):
                pool.wait_ge(sem(f"u2_out{s}"), 16 * (J // 2))
            gp.memset(idx_now[:, :], 0).then_inc(sem("x_moved"), 2)
            with pool.Fori(0, pairs + 1) as m:
                for p in range(2):
                    pool.wait_ge(sem("x_moved"), m * 2 + (p + 1))
                    gp.tensor_copy(idx_now[0:TS, p:p + 1], slot_tok[0:TS, ds(m * 2 + p, 1)]).then_inc(sem("idx_ready"), 1)
                    pool.wait_ge(sem("idx_ready"), m * 2 + (p + 1))
                    stand(pool, "pool")
                    gp.indirect_dma_start(x_land[p], None, u2_rows, bass.IndirectOffsetOnAxis(ap=idx_now[0:TS, p:p + 1], axis=0)).then_inc(sem(f"x_rows_in{p}"), 16)

            for p in range(2):
                pool.wait_ge(sem(f"y_rows_out{p}"), pairs * 32 + 32)
            stand(pool, "pool")
            def fetch(t):
                for k in range(2):
                    gp.indirect_dma_start(ycomb[2 * t + k], None, y_rows, bass.IndirectOffsetOnAxis(
                        ap=ypos[:, J * k + t:J * k + t + 1], axis=0)).then_inc(sem(f"ycomb_in{t}"), 16)

            def inverse_rms(j):
                pool.wait_ge(sem("ssq3_done"), j + 1)
                step(gp.tensor_scalar(rstd[:, j:j + 1], ssq[:, j:j + 1], 1.0 / D, EPS, ALU.mult, ALU.add))
                gp.tensor_tensor(rstd[:, j:j + 1], rstd[:, j:j + 1], half_neg, ALU.pow).then_inc(sem("rstd3_done"), 1)

            def gain(q):
                pool.wait_ge(sem("scaled"), POOL_OUT.index(q) + 1)
                gp.tensor_tensor(h[:, q, :], h[:, q, :], gf_bc, ALU.mult).then_inc(sem("out_pool"), 1)

            for t in range(J):
                fetch(t)
                if t >= 3:
                    inverse_rms(t - 3)
            pool.wait_ge(sem("gf_in"), 16)
            gain(0)
            inverse_rms(J - 3)
            gain(2)
            inverse_rms(J - 2)
            inverse_rms(J - 1)

        @block.tensor
        def _(pe):
            mm, tp = nc.tensor.matmul, nc.tensor.transpose

            def group(out, pairs):
                for i, (lhsT, rhs) in enumerate(pairs):
                    last = mm(out, lhsT, rhs, start=(i == 0), stop=(i == len(pairs) - 1))
                return last

            pe.wait_ge(sem("ident_done"), 1)
            pe.wait_ge(sem("vrows_in"), 16 * 7)
            tp(ps[:, 0, 0:V_ROWS], vrows[0:V_ROWS, :], ident[0:V_ROWS, 0:V_ROWS]).then_inc(sem("vec_mm"), 1)
            pe.wait_ge(sem("ssm_in"), 16 * 13)
            for s in range(2):
                tp(ps[:, 2, G * s:G * s + G], lam_rows[:, s, :], ident[0:G, 0:G])
            for s in range(2):
                for b in range(2):
                    last = tp(ps[:, 1, 256 * s + 128 * b:256 * s + 128 * b + 128], C_rows[:, s, b, :], ident[:, :])
            last.then_inc(sem("param_mm"), 1)

            pe.wait_ge(sem("csil_done"), 1)
            for i in range(NMOD1):
                pe.wait_ge(sem(f"modw_in{i % MODR}"), 16 * (i // MODR + 1))
                group(ps[0:1, (6, 7, 0, 1)[i // 2], MODC * (i % 2):MODC * (i % 2) + MODC],
                      [(csil[:, k:k + 1], modw[i % MODR][:, k, :]) for k in range(KD)]).then_inc(sem("modw_used"), 1)
            pe.wait_ge(sem("mod1_rows"), 4)
            for b in range(2 * KD):
                last = mm(ps[:, 6, b:b + 1], mod1_rows[b // KD][:, 128 * (b % KD):128 * (b % KD) + 128], ones[0:1, 0:1], start=True, stop=True)
            last.then_inc(sem("mod1_mm"), 1)

            pe.wait_ge(sem("tables_done"), 1)
            for g in range(G):
                last = mm(ps[0:CH, 2 + g // 4, 128 * (g % 4):128 * (g % 4) + 128], Bb_st[:, g, :], CA[:, g, 0:8, :],
                          start=True, stop=True)
            last.then_inc(sem("k0_mm"), 1)
            pe.wait_ge(sem("k0_evac"), 4)
            for g in range(G):
                last = tp(ps[:, 2 + g // 4, 128 * (g % 4):128 * (g % 4) + 128], BP[:, g, :], ident[:, :])
            last.then_inc(sem("bp_mm"), 1)

            pe.wait_ge(sem("bpt_evac"), 4)
            for half in range(2):
                pe.wait_ge(sem("xn_done"), 4 * half + 4)
                for k in range(KD):
                    n = KD * half + k
                    if n >= 4:
                        pe.wait_ge(sem("ut_evac"), n - 3)
                    for j in range(4):
                        last = tp(ps[:, n % 4, 128 * j:128 * j + 128], h[:, 4 * half + j, 128 * k:128 * k + 128], ident[:, :])
                    last.then_inc(sem("ut_mm"), 1)

            pe.wait_ge(sem("ut_evac"), 2 * KD)
            pe.wait_ge(sem("wsp_in"), 16)
            for j in range(J):
                group(ps[:, j // 2, 256 * (j % 2):256 * (j % 2) + 256],
                      [(uT[:, k, 128 * j:128 * j + 128], wsp[:, k, 0:D_SSM]) for k in range(KD)]).then_inc(sem("u_mm"), 1)

            def pool_project(gi, halves=range(2)):
                if gi >= 2:
                    pe.wait_ge(sem("gate_bank_free"), 2 * (gi - 1))
                col = D_SSM + 128 * (3 - gi)
                for half in halves:
                    group(ps[:, 4 + 2 * (gi % 2) + half, :],
                          [(wsp[:, k, col:col + 128], uT[:, k, HALF * half:HALF * half + HALF]) for k in range(KD)]).then_inc(sem("px_mm"), 1)

            def pool_mix(gi):
                pe.wait_ge(sem("m_ready"), gi + 1)
                if gi >= 2:
                    pe.wait_ge(sem("bt_evac"), 2 * (gi - 1))
                for half in range(2):
                    m = pool_buf[m_buf[gi]][:, 4 * half:4 * half + 4, 1:P + 1]
                    last = mm(ps[:, 2 * (gi % 2) + half, :], wpool[:, 3 - gi, :], m, start=True, stop=True)
                last.then_inc(sem("pmix_mm"), 1)

            pe.wait_ge(sem("wsp_pool_in"), 16)
            pool_project(0)
            pe.wait_ge(sem("u_evac"), 4)
            for g in range(G):
                last = tp(ps[:, g // 4, 128 * (g % 4):128 * (g % 4) + 128], U[:, g].rearrange("p j h -> p (j h)"), ident[:, :])
                if g % 4 == 3:
                    last.then_inc(sem("v_mm"), 1)
            pool_project(1)
            pe.wait_ge(sem("v_evac"), 4)
            for g in range(G):
                last = mm(ps[:, g // 4, 128 * (g % 4):128 * (g % 4) + 128], BPT[:, g, :], V[:, g, :], start=True, stop=True)
                if g % 4 == 3:
                    last.then_inc(sem("in_mm"), 1)
            pool_project(2, (0,))
            pe.wait_ge(sem("wpool_in"), 16)
            pe.wait_ge(sem("in_evac"), 12)
            pool_mix(0)
            pool_project(2, (1,))
            pool_mix(1)
            pool_project(3, (0,))
            pool_mix(2)
            pool_project(3, (1,))
            pool_mix(3)
            pe.wait_ge(sem("bt_evac"), 8)

            def gate_pair(n, step2):
                rhs, nk = (zT, 2) if step2 else (bT, 4)
                for s in range(2):
                    pe.wait_ge(sem(f"wring_in{s}"), n * 16 + 16 * (1 + 4 * step2))
                    pe.wait_ge(sem(f"wproj_in{s}"), n * 16 + 16 * (1 + 4 * step2))
                    for half in range(2):
                        it = n * 4 + (2 * s + half + 16 * step2)
                        pe.wait_ge(sem("gate_bank_free"), it + 7)
                        pe.wait_ge(sem("mul_done"), it + 1)
                        cols = slice(HALF * half, HALF * half + HALF)
                        group(ps[:, 5 + 2 * half, :], [(wproj[s][:, k, :], rhs[:, k, cols]) for k in range(nk)]).then_inc(sem("proj_mm"), 1)
                        group(ps[:, 4 + 2 * half, :], [(wgate[s][:, k, :], uT[:, k, cols]) for k in range(KD)]).then_inc(sem("gate_mm"), 1)

            with pe.Fori(0, 2) as n:
                gate_pair(n, 0)
            gate_pair(2, 0)
            pe.wait_ge(sem("state_done"), 1)
            pe.wait_ge(sem("t_in"), 16 * J)
            for g in range(G):
                last = group(ps[:, g // 4, 128 * (g % 4):128 * (g % 4) + 128],
                             [(V[:, g, :], Tm[:, g, :]), (Xs[:, g, 0:P], CA[:, g, 1:9, :])])
                if g % 4 == 3:
                    last.then_inc(sem("y_mm"), 1)
            gate_pair(3, 0)
            pe.wait_ge(sem("gelu_done"), 1)
            for cb in range(2):
                for half in range(2):
                    for j in range(4):
                        last = tp(ps[:, 2 * cb + half, 128 * j:128 * j + 128],
                                  Ysp[:, 4 * half + j, 8 * cb:8 * cb + 8].rearrange("p g h -> p (g h)"), ident[:, :])
                    last.then_inc(sem("yt_mm"), 1)
            pe.wait_ge(sem("yt_evac"), 4)
            pe.wait_ge(sem("wglu_in"), 16)
            for ob in range(2):
                for half in range(2):
                    group(ps[:, 2 * ob + half, :], [(wglu[:, k, 128 * ob:128 * ob + 128], yT[:, k, HALF * half:HALF * half + HALF])
                                                   for k in range(2)]).then_inc(sem("glu_mm"), 1)
            pe.wait_ge(sem("z_done"), 4)
            with pe.Fori(0, KD // 2) as n:
                gate_pair(n, 1)

            pe.wait_ge(sem("mod_sums_done"), 1)
            pe.wait_ge(sem("mul_done"), 4 * KD + 2)
            for q in range(6):
                last = mm(ps[:, q, :], ones[:, :], work[:, HALF * q:HALF * q + HALF], start=True, stop=True)
            last.then_inc(sem("mod_mm"), 1)
            pe.wait_ge(sem("mod_rows_done"), 1)
            pe.wait_ge(sem("wout_in"), 16)
            pe.wait_ge(sem("rw_in"), 32)
            for t in range(J + 2):
                if t < J:
                    if t >= 2:
                        pe.wait_ge(sem("h_psum_read"), 2 * (t - 1))
                    for half in range(2):
                        last = group(ps[:, 2 * (t % 2) + half, :],
                                     [(merged[:, k, 128 * t:128 * t + 128], wout[:, k, HALF * half:HALF * half + HALF]) for k in range(KD)])
                    last.then_inc(sem("wout_done"), 1)
                if 1 <= t <= J:
                    pe.wait_ge(sem("u2_done"), t)
                    if t >= 2:
                        pe.wait_ge(sem("u2t_evac"), 2 * (t - 1))
                    for k in range(KD):
                        last = tp(ps[:, 4 + k // 4, 128 * (k % 4):128 * (k % 4) + 128], u2t[(t - 1) % 2][:, 128 * k:128 * k + 128], ident[:, :])
                    last.then_inc(sem("u2t_mm"), 1)
                if t >= 2:
                    j = t - 2
                    pe.wait_ge(sem("u2t_evac"), 2 * (j + 1))
                    group(ps[:, 6, (NG + NE) * j:(NG + NE) * (j + 1)],
                          [(u2T[j % 2][:, k, :], rw[:, k, :]) for k in range(KD)]).then_inc(sem("router_mm"), 1)

            pe.wait_ge(sem("picks_done"), 1)
            pe.wait_ge(sem("later_done"), 1)
            group(ps[:, 7, 0:J * NE], [(later, M_all), (ones[:, :], M_before)])
            mm(ps[:, 7, J * NE:J * NE + NE], ones[:, :], M_total, start=True, stop=True).then_inc(sem("rank_mm"), 1)
            for q in range(2):
                last = mm(ps[:, 4 + q, :], ones[:, :], gate2_bc[:, HALF * q:HALF * q + HALF], start=True, stop=True)
            last.then_inc(sem("gate2_mm"), 1)
            pe.wait_ge(sem("onehots_done"), 1)
            group(ps[0:TS, 0, 0:MAX_TILES], [(oh_lo[:, i, :], oh_hi[:, i, :]) for i in range(2 * J)]).then_inc(sem("slot_mm"), 1)
            pe.wait_ge(sem("routed"), 1)

            def both(bank, pairs):
                for i, (lhsT, *halves) in enumerate(pairs):
                    for c in range(2):
                        last = mm(ps[TS * c:TS * c + TS, bank, 0:halves[c].shape[-1]], lhsT[c], halves[c],
                                  start=(i == 0), stop=(i == len(pairs) - 1))
                return last

            def hidden_product(bank, w):
                return both(bank, [((xT[:, k, :],) * 2, w[:, k, 0:HE], w[:, k, HE:DE]) for k in range(KD)])

            def gate(g, s):
                pe.wait_ge(sem("xt_ready"), g + 1)
                hidden_product(0, e_gate[s]).then_inc(sem("gate_done"), 1)

            def up(s):
                hidden_product(1, e_up[s]).then_inc(sem("up_done"), 1)

            def transpose_x(g1):
                pe.wait_ge(sem("x_moved"), g1 + 2)
                stand(pe, "pe")
                for k in range(KD):
                    last = tp(ps[:, 4, TS * k:TS * k + TS], x_tile[:, 128 * k:128 * k + 128], ident[TS:2 * TS, TS:2 * TS])
                last.then_inc(sem("x_rows_used"), 1)

            def transpose_hidden(g):
                pe.wait_ge(sem("hidden_ready"), g)
                for f in range(2):
                    last = tp(ps[:, 6, 128 * f:128 * f + 128], hidden[:, 128 * f:128 * f + 128], ident[:, :])
                last.then_inc(sem("hidden_used"), 1)

            def down(g, s):
                pe.wait_ge(sem("hiddent_ready"), g)
                pe.wait_ge(sem("y_copied"), g)
                both(2, [((hiddenT[:, f // 2, f % 2, :],) * 2, e_down[s][:, f, 0:HD], e_down[s][:, f, HD:D]) for f in range(KE)]).then_inc(sem("tiles_done"), 1)

            def tile(g, s, s_before):
                transpose_hidden(g)
                gate(g, s)
                up(s)
                transpose_x(g + 2)
                down(g, s_before)

            def expert(e, s, n):
                t0 = pe.value_load(tstart_i[0:1, ds(e, 1)], min_val=1, max_val=MAX_TILES)
                t1 = pe.value_load(tstart_i[0:1, ds(e + 1, 1)], min_val=1, max_val=MAX_TILES)
                before = (s - 1) % RING
                transpose_hidden(t0)
                pe.wait_ge(sem(f"gate_in{s}"), n * 16 + 16)
                stand(pe, "pe")
                gate(t0, s)
                pe.wait_ge(sem(f"up_in{s}"), n * 16 + 16)
                stand(pe, "pe")
                up(s)
                transpose_x(t0 + 2)
                pe.wait_ge(sem(f"down_in{before}"), n * 16 + (16 if s else 0))
                stand(pe, "pe")
                down(t0, before)
                with pe.If(t1 > t0 + 1):
                    pe.wait_ge(sem(f"down_in{s}"), n * 16 + 16)
                    stand(pe, "pe")
                    with pe.Fori(t0 + 1, t1) as g:
                        tile(g, s, s)

            pe.wait_ge(sem("tiles_counted"), 1)
            n_tiles = pe.value_load(tstart_i[0:1, NE:NE + 1], min_val=NE, max_val=MAX_TILES)
            t1 = pe.value_load(tstart_i[0:1, 1:2], min_val=1, max_val=MAX_TILES)
            pe.wait_ge(sem("gate2_rows"), 2)
            transpose_x(1)
            pe.wait_ge(sem("gate_in0"), 16)
            gate(0, 0)
            pe.wait_ge(sem("up_in0"), 16)
            up(0)
            transpose_x(2)
            with pe.If(t1 > 1):
                pe.wait_ge(sem("down_in0"), 16)
                with pe.Fori(1, t1) as g:
                    tile(g, 0, 0)
            with pe.Fori(0, (NE - 1) // RING) as n:
                expert(n * RING + 1, 1, n)
                expert(n * RING + 2, 2, n)
                expert(n * RING + 3, 0, n + 1)
            for e in range((NE - 1) // RING * RING + 1, NE):
                expert(e, e % RING, e // RING)
            transpose_hidden(n_tiles)
            pe.wait_ge(sem(f"down_in{(NE - 1) % RING}"), 16 * ((NE - 1) // RING + 1))
            down(n_tiles, (NE - 1) % RING)

        @block.scalar
        def _(act):
            fn = nc.scalar.activation

            act.wait_ge(sem("vec_done"), 1)
            fn(csil, vec[:, V_C:V_C + 8], ACT.Sigmoid).then_inc(sem("csig_done"), 1)
            for j in range(J):
                act.wait_ge(sem(f"x_in{j // 2}"), 16)
                if j:
                    act.wait_ge(sem("ssq1_done"), j)
                fn(sg[:, :], h[:, j, :], ACT.Square, accum_out=ssq[:, j:j + 1]).then_inc(sem("ssq1_done"), 1)

            for i in range(4):
                act.wait_ge(sem("modw_used"), 2 * i + 2)
                fn(mod1_rows[i // 2][:, HALF * (i % 2):HALF * (i % 2) + HALF], ps[0:1, (6, 7, 0, 1)[i], :], ACT.Copy).then_inc(sem("mod1_rows"), 1)
            act.wait_ge(sem("rstd1_done"), 1)
            for j in range(J):
                fn(h[:, j, :], h[:, j, :], ACT.Copy, scale=rstd[:, j:j + 1]).then_inc(sem("xn_done"), 1)
            act.wait_ge(sem("k0_mm"), 1)
            act.wait_ge(sem("k0_zero"), 1)
            for q in range(4):
                fn(K0[:, 4 * q:4 * q + 4, 112:240], ps[0:CH, 2 + q, :].rearrange("p (g n) -> p g n", g=4), ACT.Copy).then_inc(sem("k0_evac"), 1)
            act.wait_ge(sem("k0_evac"), 4)
            for j1 in range(J):
                act.dma_start(Tm[CH * j1:CH * j1 + CH, :, :], K0[:, :, 112 - CH * j1:240 - CH * j1]).then_inc(sem("t_in"), 16)
            act.wait_ge(sem("bp_mm"), 1)
            for q in range(4):
                fn(BPT[:, 4 * q:4 * q + 4, :], ps[:, 2 + q, :].rearrange("p (g n) -> p g n", g=4), ACT.Copy).then_inc(sem("bpt_evac"), 1)

            act.wait_ge(sem("mod1_done"), 1)
            act.wait_ge(sem("t_in"), 16 * J)
            for half in range(2):
                for k in range(KD):
                    n = KD * half + k
                    act.wait_ge(sem("ut_mm"), n + 1)
                    fn(uT[:, k, HALF * half:HALF * half + HALF], ps[:, n % 4, :], ACT.Identity,
                       scale=A1[:, k:k + 1], bias=S1[:, k:k + 1]).then_inc(sem("ut_evac"), 1)

            def pool_in(gi):
                if gi:
                    act.wait_ge(sem("m_ready"), gi)
                else:
                    act.wait_ge(sem("pads_done"), 1)
                for half in range(2):
                    act.wait_ge(sem("px_mm"), 2 * gi + half + 1)
                    fn(pool_buf[0][:, 4 * half:4 * half + 4, 1:P + 1],
                       ps[:, 4 + 2 * (gi % 2) + half, :].rearrange("p (j c) -> p j c", j=4), ACT.Identity,
                       bias=vec[:, V_BIN + 2 + 3 - gi:V_BIN + 3 + 3 - gi]).then_inc(sem("gate_bank_free"), 1)

            def pool_out(gi):
                act.wait_ge(sem("pmix_mm"), gi + 1)
                if gi == 0:
                    act.wait_ge(sem("mod_sum"), KD * (NMOD - NMOD1 - 2))
                for half in range(2):
                    fn(bT[:, 3 - gi, HALF * half:HALF * half + HALF], ps[:, 2 * (gi % 2) + half, :], ACT.Copy,
                       scale=vec[:, V_PSC + 3 - gi:V_PSC + 4 - gi]).then_inc(sem("bt_evac"), 1)

            pool_in(0)
            for q in range(4):
                act.wait_ge(sem("v_mm"), q + 1)
                fn(V[:, 4 * q:4 * q + 4, :], ps[:, q, :].rearrange("p (g n) -> p g n", g=4), ACT.Copy).then_inc(sem("v_evac"), 1)
            pool_in(1)
            for q in range(4):
                act.wait_ge(sem("in_mm"), q + 1)
                src = ps[:, q, :].rearrange("p (g n) -> p g n", g=4)
                dst = slice(4 * q, 4 * q + 4)
                fn(SA[:, dst, :], src, ACT.Copy).then_inc(sem("in_evac"), 1)
                fn(SB[0:ST, dst, :], src[ST:P], ACT.Copy).then_inc(sem("in_evac"), 1)
                fn(SB[ST:P, dst, :], src[0:ST], ACT.Copy).then_inc(sem("in_evac"), 1)
            pool_in(2)
            pool_out(0)
            pool_in(3)
            for gi in range(1, 4):
                pool_out(gi)

            def gate_pair(n, step2):
                for s in range(2):
                    for half in range(2):
                        it = n * 4 + (2 * s + half + 16 * step2)
                        act.wait_ge(sem("gate_mm"), it + 1)
                        act.wait_ge(sem("mul_done"), it + 1)
                        stand(act, "act")
                        col = V_BIN + (6 if step2 else 14) + s
                        fn(sg[:, HALF * half:HALF * half + HALF], ps[:, 4 + 2 * half, :], ACT.Sigmoid,
                           bias=vec[:, ds(n * 2 + col, 1)] if not isinstance(n, int) else vec[:, n * 2 + col:n * 2 + col + 1]).then_inc(sem("gate_bank_free"), 1)

            spare = y_rows[NE * TS:, :].rearrange("(p r) (c n) -> p (r c) n", p=P, n=256)
            act.wait_ge(sem("zeros_ready"), 1)
            for c in range(4):
                part = spare[:, c * spare.shape[1] // 4:(c + 1) * spare.shape[1] // 4]
                act.dma_start(part, zeros.unsqueeze(1).to_broadcast([P, part.shape[1], 256])).then_inc(sem(f"y_rows_out{c % 2}"), 16)

            with act.Fori(0, 2) as n:
                gate_pair(n, 0)
            gate_pair(2, 0)
            act.wait_ge(sem("y_evac"), 1)
            fn(gtmp, Y_flat, ACT.Square).then_inc(sem("ysq_done"), 1)
            act.wait_ge(sem("gelu_arg"), 1)
            fn(gtmp, gtmp, ACT.Sigmoid, scale=2.0 * (2.0 / np.pi) ** 0.5).then_inc(sem("gelu_sig"), 1)
            gate_pair(3, 0)
            for cb in range(2):
                for half in range(2):
                    act.wait_ge(sem("yt_mm"), 2 * cb + half + 1)
                    fn(yT[:, cb, HALF * half:HALF * half + HALF], ps[:, 2 * cb + half, :], ACT.Copy).then_inc(sem("yt_evac"), 1)
            for ob in range(2):
                for half in range(2):
                    act.wait_ge(sem("glu_mm"), 2 * ob + half + 1)
                    act.wait_ge(sem("mul_done"), 2 * KD + half + 1)
                    if ob:
                        act.wait_ge(sem("z_done"), half + 1)
                    fn(sg[:, HALF * half:HALF * half + HALF], ps[:, 2 * ob + half, :], ACT.Sigmoid,
                       bias=vec[:, V_BGLU + ob:V_BGLU + ob + 1]).then_inc(sem("glu_sig"), 1)
            act.wait_ge(sem("z_done"), 4)
            with act.Fori(0, KD // 2) as n:
                gate_pair(n, 1)

            def second_norm(j):
                act.wait_ge(sem("h_done"), j + 1)
                if j:
                    act.wait_ge(sem("ssq2_done"), j)
                fn(sg[:, :], h[:, j, :], ACT.Square, accum_out=ssq[:, j:j + 1]).then_inc(sem("ssq2_done"), 1)

            def rows_out(j):
                act.wait_ge(sem("u2_done"), j + 1)
                act.dma_start(u2_v[:, j, :], u2t[j % 2]).then_inc(sem(f"u2_out{j % 2}"), 16)
                act.wait_ge(sem("u2t_mm"), j + 1)
                if j >= 2:
                    act.wait_ge(sem("router_mm"), j - 1)
                for b in range(2):
                    fn(u2T[j % 2][:, 4 * b:4 * b + 4, :], ps[:, 4 + b, :].rearrange("p (k t) -> p k t", k=4), ACT.Copy).then_inc(sem("u2t_evac"), 1)

            for j in range(J):
                second_norm(j)
                rows_out(j)

            act.wait_ge(sem("coarse_diff"), 1)
            fn(cexp, cdiff, ACT.Exp).then_inc(sem("coarse_exp"), 1)
            act.wait_ge(sem("fine_diff"), 1)
            fn(wpick[:, 0, :], fdiff, ACT.Sigmoid, scale=-1.0)
            fn(wpick[:, 1, :], fdiff, ACT.Sigmoid).then_inc(sem("fine_sig"), 1)

            act.wait_ge(sem("routed"), 1)
            pairs = act.value_load(tstart_i[0:1, NE + 1:NE + 2], min_val=NE // 2, max_val=MAX_TILES // 2)

            def silu(g):
                act.wait_ge(sem("gate_done"), g + 1)
                fn(hidden, ps[:, 0, 0:HE], ACT.Silu).then_inc(sem("silu_done"), 1)

            def take_x(t):
                act.wait_ge(sem("x_rows_used"), t + 1)
                fn(xT, ps[:, 4, :].rearrange("p (k t) -> p k t", k=KD), ACT.Copy).then_inc(sem("xt_ready"), 1)

            def move_x(p, seen):
                act.wait_ge(sem(f"x_rows_in{p}"), seen * 16)
                fn(x_tile, x_land[p], ACT.Copy).then_inc(sem("x_moved"), 1)

            def rows_to_dram(q, p):
                act.wait_ge(sem("y_copied"), q + 2)
                for c in range(2):
                    act.dma_start(y_rows[ds(q * TS, TS), HD * c:HD * c + HD], y_tile[p][TS * c:TS * c + TS, :]).then_inc(sem(f"y_rows_out{p}"), 16)

            move_x(0, 1)
            take_x(0)
            move_x(1, 1)
            silu(0)
            take_x(1)
            move_x(0, 2)
            silu(1)
            take_x(2)
            move_x(1, 2)
            rows_to_dram(0, 0)
            with act.Fori(1, pairs) as m:
                for p in range(2):
                    silu(m * 2 + p)
                    take_x(m * 2 + (p + 1))
                    move_x(p, m + 2)
                    rows_to_dram(m * 2 + (p - 1), 1 - p)
            rows_to_dram(pairs * 2 - 1, 1)

            for j in range(J):
                act.wait_ge(sem("combined"), j + 1)
                if j:
                    act.wait_ge(sem("ssq3_done"), j)
                fn(sg[:, :], h[:, j, :], ACT.Square, accum_out=ssq[:, j:j + 1]).then_inc(sem("ssq3_done"), 1)
                if j in POOL_OUT:
                    act.wait_ge(sem("rstd3_done"), j + 1)
                    fn(h[:, j, :], h[:, j, :], ACT.Copy, scale=rstd[:, j:j + 1]).then_inc(sem("scaled"), 1)

        @block.vector
        def _(dve):
            v = nc.vector
            own = [0]

            def step(ins):
                own[0] += 1
                ins.then_inc(sem("dve_step"), 1)
                dve.wait_ge(sem("dve_step"), own[0])

            def tt(out, in0, in1, op):
                return v.tensor_tensor(out, in0, in1, op)

            def bc(ap, axis, n):
                ap = ap.unsqueeze(axis)
                shape = list(ap.shape)
                shape[axis] = n
                return ap.to_broadcast(shape)

            dve.wait_ge(sem("vec_mm"), 1)
            v.tensor_copy(vec[:, :], ps[:, 0, 0:V_ROWS]).then_inc(sem("vec_done"), 1)
            dve.wait_ge(sem("param_mm"), 1)
            LR, LI, DT, Y, N, R, Q, S, C, H1, H2 = (t16[:, i, :] for i in (1, 2, 0, 3, 4, 5, 6, 7, 8, 9, 10))
            MAG, CT, SN, LBR, LBI, FR, FI, FIS, T1, T2, DEN, NRE, CR, CI = (t16[:, i, :] for i in range(11, 25))
            NI = t16[:, 25, :].bitcast(I32)
            PR2, PI2, PR4, PI4 = (t16[:, i, :] for i in range(26, 30))
            v.tensor_copy(LR, ps[:, 2, 0:G])
            v.tensor_copy(LI, ps[:, 2, G:2 * G])
            v.tensor_copy(work[:, 512:1024], ps[:, 1, :])
            dve.wait_ge(sem("csig_done"), 1)
            dve.wait_ge(sem("ssm_in"), 16 * 13)
            step(v.tensor_scalar(T1, DT, 0.0, None, ALU.add))
            tt(csil, csil, vec[:, V_C:V_C + 8], ALU.mult).then_inc(sem("csil_done"), 1)

            MAGIC = 12582912.0

            def exp(out, y):
                step(v.tensor_scalar(Y, y, -110.0, 100.0, ALU.max, ALU.min))
                step(v.tensor_scalar(N, Y, 1.4426950408889634, MAGIC, ALU.mult, ALU.add))
                step(v.tensor_scalar(N, N, -MAGIC, None, ALU.add))
                step(v.scalar_tensor_tensor(R, N, -0.693359375, Y, ALU.mult, ALU.add))
                step(v.scalar_tensor_tensor(R, N, 2.12194440e-4, R, ALU.mult, ALU.add))
                step(v.tensor_scalar(Q, R, 1.0 / 5040, None, ALU.mult))
                for c in (1.0 / 720, 1.0 / 120, 1.0 / 24, 1.0 / 6, 0.5, 1.0):
                    step(v.scalar_tensor_tensor(Q, Q, c, R, ALU.add, ALU.mult))
                step(v.tensor_scalar(N, N, -127.0, 128.0, ALU.max, ALU.min))
                step(v.tensor_scalar(NI, N, 127.0, 8388608.0, ALU.add, ALU.mult))
                step(v.scalar_tensor_tensor(out, Q, 1.0, NI.bitcast(F32), ALU.add, ALU.mult))

            exp(T1, DT)
            step(tt(T2, T1, LR, ALU.mult))
            exp(MAG, T2)
            step(tt(Y, T1, LI, ALU.mult))
            step(v.tensor_scalar(N, Y, 1.0 / (2.0 * np.pi), MAGIC, ALU.mult, ALU.add))
            step(v.tensor_scalar(N, N, -MAGIC, None, ALU.add))
            TURN1, TURN2 = 6.28125, 0.0019350051879882812
            step(v.scalar_tensor_tensor(R, N, -TURN1, Y, ALU.mult, ALU.add))
            step(v.scalar_tensor_tensor(R, N, -TURN2, R, ALU.mult, ALU.add))
            step(v.scalar_tensor_tensor(R, N, -(2.0 * np.pi - TURN1 - TURN2), R, ALU.mult, ALU.add))
            step(v.tensor_scalar(R, R, 0.5, None, ALU.mult))
            step(tt(H2, R, R, ALU.mult))
            fact = [1.0]
            for i in range(1, 17):
                fact.append(fact[-1] * i)
            step(v.tensor_scalar(S, H2, 1.0 / fact[13], None, ALU.mult))
            for i, c in enumerate((11, 9, 7, 5, 3)):
                step(v.scalar_tensor_tensor(S, S, (-1.0) ** (i + 1) / fact[c], H2, ALU.add, ALU.mult))
            step(v.scalar_tensor_tensor(S, S, 1.0, R, ALU.add, ALU.mult))
            step(v.tensor_scalar(C, H2, 1.0 / fact[16], None, ALU.mult))
            for i, c in enumerate((14, 12, 10, 8, 6, 4, 2)):
                step(v.scalar_tensor_tensor(C, C, (-1.0) ** (i + 1) / fact[c], H2, ALU.add, ALU.mult))
            step(v.tensor_scalar(C, C, 1.0, None, ALU.add))
            step(v.scalar_tensor_tensor(SN, S, 2.0, C, ALU.mult, ALU.mult))
            step(tt(CT, S, S, ALU.mult))
            step(v.tensor_scalar(CT, CT, -2.0, 1.0, ALU.mult, ALU.add))
            step(tt(LBR, MAG, CT, ALU.mult))
            step(tt(LBI, MAG, SN, ALU.mult))
            step(tt(DEN, LR, LR, ALU.mult))
            step(tt(H1, LI, LI, ALU.mult))
            step(tt(DEN, DEN, H1, ALU.add))
            step(v.reciprocal(DEN, DEN))
            step(v.tensor_scalar(NRE, LBR, -1.0, None, ALU.add))
            step(tt(FR, NRE, LR, ALU.mult))
            step(tt(H1, LBI, LI, ALU.mult))
            step(tt(FR, FR, H1, ALU.add))
            step(tt(FR, FR, DEN, ALU.mult))
            step(tt(FI, LBI, LR, ALU.mult))
            step(tt(H1, NRE, LI, ALU.mult))
            step(tt(FI, FI, H1, ALU.subtract))
            step(tt(FI, FI, DEN, ALU.mult))
            dve.wait_ge(sem("ident_done"), 1)
            step(v.tensor_scalar(FIS, FI, sgn, None, ALU.mult))
            step(tt(Bb_st, B_st, bc(FR, 2, CH), ALU.mult))
            step(tt(Bb_sw, B_sw, bc(FIS, 2, CH), ALU.mult))
            step(tt(Bb_st, Bb_st, Bb_sw, ALU.add))
            step(tt(Bb_sw, B_sw, bc(FR, 2, CH), ALU.mult))
            step(tt(B_st, B_st, bc(FIS, 2, CH), ALU.mult))
            step(tt(Bb_sw, Bb_sw, B_st, ALU.subtract))

            def cmul(or_, oi, ar_, ai, br_, bi, t):
                step(tt(or_, ar_, br_, ALU.mult))
                step(tt(t, ai, bi, ALU.mult))
                step(tt(or_, or_, t, ALU.subtract))
                step(tt(oi, ar_, bi, ALU.mult))
                step(tt(t, ai, br_, ALU.mult))
                step(tt(oi, oi, t, ALU.add))

            step(v.memset(pw_re[:, :, 0:1], 1.0))
            step(v.memset(pw_im[:, :, 0:1], 0.0))
            step(v.tensor_copy(pw_re[:, :, 1], LBR))
            step(v.tensor_copy(pw_im[:, :, 1], LBI))
            pt = ptmp[:, 0:64].rearrange("p (g t) -> p g t", g=G)
            for n in (1, 2, 4):
                src, dst = slice(1, n + 1), slice(n + 1, 2 * n + 1)
                cmul(pw_re[:, :, dst], pw_im[:, :, dst], pw_re[:, :, src], pw_im[:, :, src],
                     bc(pw_re[:, :, n], 2, n), bc(pw_im[:, :, n], 2, n), pt[:, :, 0:n])
            ptm = ptmp[:, 0:2304].rearrange("p (g t h) -> p g t h", g=G, t=9)
            BP4 = BP.rearrange("p g (t h) -> p g t h", t=J)
            for j in range(J):
                tt(BP4[:, :, j, :], Bb_st, bc(pw_re[:, :, 7 - j], 2, CH), ALU.mult)
                last = tt(ptm[:, :, j, :], Bb_sw, bc(pw_im[:, :, 7 - j], 2, CH), ALU.mult)
            step(last)
            step(v.scalar_tensor_tensor(BP4, ptm[:, :, 0:J, :], sgn, BP4, ALU.mult, ALU.add))
            for t in range(9):
                tt(CA[:, :, t, :], C_st, bc(pw_re[:, :, t], 2, CH), ALU.mult)
                last = tt(ptm[:, :, t, :], C_sw, bc(pw_im[:, :, t], 2, CH), ALU.mult)
            step(last)
            step(v.scalar_tensor_tensor(CA, CA, nsgn, ptm, ALU.mult, ALU.subtract))
            v.memset(pool_buf[0][:, 0, 0:1], 0.0).then_inc(sem("tables_done"), 1)
            dve.wait_ge(sem("mod1_mm"), 1)
            step(tt(S1, ps[:, 6, 0:8], vec[:, V_BMOD:V_BMOD + 8], ALU.add))
            step(tt(A1, ps[:, 6, 8:16], vec[:, V_BMOD + 8:V_BMOD + 16], ALU.add))
            step(v.scalar_tensor_tensor(A1, A1, 1.0, vec[:, V_N1:V_N1 + 8], ALU.add, ALU.mult))
            v.memset(pool_buf[0][:, 0, 0:1], 0.0).then_inc(sem("mod1_done"), 1)
            step(tt(MAG, MAG, MAG, ALU.mult))
            step(tt(MAG, MAG, MAG, ALU.mult))
            step(tt(phase_r8, MAG, MAG, ALU.mult))

            def csquare(c, s):
                tt(T1, c, c, ALU.mult)
                step(tt(T2, s, s, ALU.mult))
                step(v.scalar_tensor_tensor(s, c, 2.0, s, ALU.mult, ALU.mult))
                step(tt(c, T1, T2, ALU.subtract))

            for _ in range(3):
                csquare(CT, SN)
            step(v.memset(cos_t[:, :, 0:1], 1.0))
            step(v.memset(sin_t[:, :, 0:1], 0.0))
            n = 1
            while n < P:
                cmul(cos_t[:, :, n:2 * n], sin_t[:, :, n:2 * n], cos_t[:, :, 0:n], sin_t[:, :, 0:n],
                     bc(CT, 2, n), bc(SN, 2, n), tab_tmp[:, :, 0:n])
                n *= 2
                if n < P:
                    csquare(CT, SN)
            step(v.tensor_scalar(sin_t, sin_t, sgn, None, ALU.mult))
            dve.wait_ge(sem("k0_mm"), 1)

            v.memset(zeros, 0.0).then_inc(sem("zeros_ready"), 1)

            def mod_part(n):
                return work[:, MODC * n:MODC * n + MODC] if n < 3 * D // MODC else gate2_bc[:, MODC * n - 3 * D:MODC * n - 3 * D + MODC]

            def mod_sums(first, end):
                for n in range(first, end):
                    i = NMOD1 + n
                    dve.wait_ge(sem(f"modw_in{i % MODR}"), 16 * (i // MODR + 1))
                    w, dst = modw[i % MODR], mod_part(n)
                    for k in range(KD):
                        if k == 0:
                            ins = v.tensor_scalar(dst, w[:, 0, :], csil[:, 0:1], None, ALU.mult)
                        else:
                            dve.wait_ge(sem("mod_sum"), KD * n + k)
                            ins = v.scalar_tensor_tensor(dst, w[:, k, :], csil[:, k:k + 1], dst, ALU.mult, ALU.add)
                        ins.then_inc(sem("mod_sum"), 1)

            def mod_biases(first, end):
                dve.wait_ge(sem("mod_sum"), KD * (NMOD - NMOD1))
                for b in range(first, end):
                    dst = mod_part(b // 2)[:, 128 * (b % 2):128 * (b % 2) + 128]
                    last = v.scalar_tensor_tensor(dst, ident[:, :], vec[:, V_BMOD + 2 * KD + b:V_BMOD + 2 * KD + b + 1], dst, ALU.mult, ALU.add)
                return last

            dve.wait_ge(sem("consts_done"), 1)
            step(v.reciprocal(pool_rcp, pool_rcp))
            for i in range(3):
                last = v.memset(pool_buf[i][:, :, 0:1], 0.0)
            last.then_inc(sem("pads_done"), 1)
            dve.wait_ge(sem("pads_done"), 1)
            dve.wait_ge(sem("bias_in"), 32)
            dve.wait_ge(sem("ut_mm"), 2 * KD)
            mod_sums(0, 2)
            for q in range(4):
                dve.wait_ge(sem("u_mm"), 2 * q + 2)
                tt(U[:, :, 2 * q:2 * q + 2, :].rearrange("p g j h -> p j g h"),
                   ps[:, q, :].rearrange("p (j g h) -> p j g h", j=2, g=G),
                   bc(bu_bc.rearrange("p (g h) -> p g h", g=G), 1, 2), ALU.add).then_inc(sem("u_evac"), 1)
                mod_sums(2 + 2 * q, 4 + 2 * q)

            for gi in range(4):
                wi = 3 - gi
                dve.wait_ge(sem("gate_bank_free"), 2 * gi + 2)
                if gi:
                    dve.wait_ge(sem("pmix_mm"), gi)
                src, dst = 0, 1
                for lvl in range(wi + 1):
                    sh = 1 << lvl
                    X_, Y_ = pool_buf[src], pool_buf[dst]
                    if sh < J:
                        tt(Y_[:, sh:J, :], X_[:, sh:J, :], X_[:, 0:J - sh, :], ALU.add)
                    step(tt(Y_[:, 0:sh, 1:P + 1], X_[:, 0:sh, 1:P + 1], X_[:, J - sh:J, 0:P], ALU.add))
                    src, dst = dst, (2 if dst == 1 else 1)
                assert dst == m_buf[gi]
                win, m, X_ = pool_buf[src], pool_buf[dst], pool_buf[0]
                step(v.scalar_tensor_tensor(m[:, :, 1:P + 1], win[:, :, 1:P + 1], 1.0 / WINDOWS[wi], X_[:, :, 1:P + 1], ALU.mult, ALU.subtract))
                step(tt(m[:, :, 1:3], win[:, :, 1:3], pool_rcp[:, wi], ALU.mult))
                tt(m[:, :, 1:3], m[:, :, 1:3], X_[:, :, 1:3], ALU.subtract).then_inc(sem("m_ready"), 1)
                if gi < 3:
                    mod_sums(10 + 2 * gi, 12 + 2 * gi)

            v.memset(small[:, 51:52], 0.0).then_inc(sem("mul_done"), 2)
            mod_biases(0, 4 * KD).then_inc(sem("mod_sums_done"), 1)

            def gate_pair(n, step2):
                for s in range(2):
                    for half in range(2):
                        it = n * 4 + (2 * s + half + 16 * step2)
                        dve.wait_ge(sem("gate_bank_free"), it + 9)
                        dve.wait_ge(sem("proj_mm"), it + 1)
                        sgh = sg[:, HALF * half:HALF * half + HALF]
                        if isinstance(n, int):
                            dst = merged[:, 2 * n + s, HALF * half:HALF * half + HALF]
                        else:
                            dst = merged[:, ds(n * 2 + s, 1), HALF * half:HALF * half + HALF].rearrange("p k t -> p (k t)")
                        if not step2:
                            tt(dst, sgh, ps[:, 5 + 2 * half, :], ALU.mult).then_inc(sem("mul_done"), 1)
                        else:
                            tt(sgh, sgh, ps[:, 5 + 2 * half, :], ALU.mult).then_inc(sem("sg_mul"), 1)
                            dve.wait_ge(sem("sg_mul"), it - 15)
                            tt(dst, dst, sgh, ALU.add).then_inc(sem("mul_done"), 1)

            with dve.Fori(0, 2) as n:
                gate_pair(n, 0)
            dve.wait_ge(sem("turned"), 1)
            for g in range(G):
                last = v.tensor_tensor_scan(SB[:, g, :], phase_r8[:, g:g + 1].to_broadcast([P, P]), SA[:, g, :], 0.0, ALU.mult, ALU.add)
            step(last)
            v.tensor_copy(SA[0:ST], SB[ST:P]).then_inc(sem("z_swapped"), 1)
            v.tensor_copy(SA[ST:P], SB[0:ST]).then_inc(sem("z_swapped"), 1)
            step(tt(U.rearrange("p g j h -> p j g h"), U.rearrange("p g j h -> p j g h"),
                    bc(d_bc.rearrange("p (g h) -> p g h", g=G), 1, J), ALU.mult))
            gate_pair(2, 0)
            for q in range(4):
                dve.wait_ge(sem("y_mm"), q + 1)
                gs = slice(4 * q, 4 * q + 4)
                last = tt(Ysp[:, :, gs, :].rearrange("p j g h -> p g j h"), ps[:, q, :].rearrange("p (g j h) -> p g j h", g=4, j=J),
                          U[:, gs], ALU.add)
            last.then_inc(sem("y_evac"), 1)
            dve.wait_ge(sem("ysq_done"), 1)
            step(v.tensor_scalar(gtmp, gtmp, 0.044715, 1.0, ALU.mult, ALU.add))
            tt(gtmp, gtmp, Y_flat, ALU.mult).then_inc(sem("gelu_arg"), 1)
            dve.wait_ge(sem("gelu_sig"), 1)
            tt(Y_flat, Y_flat, gtmp, ALU.mult).then_inc(sem("gelu_done"), 1)
            gate_pair(3, 0)
            for ob in range(2):
                for half in range(2):
                    dve.wait_ge(sem("glu_sig"), 2 * ob + half + 1)
                    cols = slice(HALF * half, HALF * half + HALF)
                    tt(zT[:, ob, cols], yT[:, ob, cols], sg[:, cols], ALU.mult).then_inc(sem("z_done"), 1)
            with dve.Fori(0, KD // 2) as n:
                gate_pair(n, 1)

            dve.wait_ge(sem("mod_mm"), 1)
            dve.wait_ge(sem("n2_in"), 16)
            v.tensor_copy(work[:, 0:2048], ps[:, 0:4, :].rearrange("p b n -> p (b n)"))
            v.scalar_tensor_tensor(A2_bc, ps[:, 4:6, :].rearrange("p b n -> p (b n)"), 1.0, u2t[0], ALU.add, ALU.mult)
            step(v.memset(small[:, 51:52], 0.0))
            v.memset(small[:, 51:52], 0.0).then_inc(sem("mod_rows_done"), 1)
            dve.wait_ge(sem("x_again"), 16)

            for t in range(J):
                dve.wait_ge(sem("wout_done"), t + 1)
                if t >= 2:
                    dve.wait_ge(sem("u2t_mm"), t - 1)
                    dve.wait_ge(sem(f"u2_out{t % 2}"), 16 * (t // 2))
                for half in range(2):
                    cols = slice(HALF * half, HALF * half + HALF)
                    tt(u2t[t % 2][:, cols], ps[:, 2 * (t % 2) + half, :], gate1_bc[:, cols], ALU.mult).then_inc(sem("h_psum_read"), 1)
                dve.wait_ge(sem("h_psum_read"), 2 * t + 2)
                tt(h[:, t, :], h[:, t, :], u2t[t % 2], ALU.add).then_inc(sem("h_done"), 1)
                dve.wait_ge(sem("rstd2_done"), t + 1)
                step(v.scalar_tensor_tensor(u2t[t % 2], h[:, t, :], rstd[:, t:t + 1], A2_bc, ALU.mult, ALU.mult))
                tt(u2t[t % 2], u2t[t % 2], S2_bc, ALU.add).then_inc(sem("u2_done"), 1)

            dve.wait_ge(sem("router_mm"), J)
            for s in range(2):
                dve.wait_ge(sem(f"u2_out{s}"), 16 * (J // 2))
            dve.wait_ge(sem("rbias_in"), 32)
            step(tt(L, ps[:, 6, 0:J * (NG + NE)].rearrange("p (j n) -> p j n", j=J), bc(rbias, 1, J), ALU.add))
            coarse, fine = L[:, :, 0:NG], L[:, :, NG:NG + NE].rearrange("p j (g i) -> p j g i", g=NG)
            m1, m2, mc, csum, t8 = (rsc[:, i, :] for i in range(5))

            def first_best(out, val, n, best, scratch):
                step(v.tensor_reduce(best, val, AX.X, ALU.max))
                step(tt(out, val, bc(best, 2, n), ALU.is_equal))
                step(tt(out, out, bc(falling[:, 0:n], 1, J), ALU.mult))
                step(v.tensor_reduce(scratch, out, AX.X, ALU.max))
                step(tt(out, out, bc(scratch, 2, n), ALU.is_equal))

            step(v.tensor_scalar(falling, iota[:, 0:8], -1.0, 9.0, ALU.mult, ALU.add))
            first_best(g_hot, coarse, NG, mc, t8)
            tt(cdiff, coarse, bc(mc, 2, NG), ALU.subtract).then_inc(sem("coarse_diff"), 1)
            step(tt(fsel4, fine.rearrange("p j g i -> p j i g"), bc(g_hot, 2, EPG), ALU.mult))
            step(v.tensor_reduce(fsel, fsel4, AX.X, ALU.add))
            first_best(hot[0], fsel, EPG, m1, t8)
            step(v.scalar_tensor_tensor(fsel, hot[0], -3.0e38, fsel, ALU.mult, ALU.add))
            first_best(hot[1], fsel, EPG, m2, t8)
            tt(fdiff, m2, m1, ALU.subtract).then_inc(sem("fine_diff"), 1)
            dve.wait_ge(sem("coarse_exp"), 1)
            step(v.tensor_reduce(csum, cexp, AX.X, ALU.add))
            step(v.reciprocal(csum, csum))
            dve.wait_ge(sem("fine_sig"), 1)
            step(tt(wpick, wpick, bc(csum, 1, 2), ALU.mult))
            for k in range(2):
                step(tt(pick[k].rearrange("p j (i g) -> p j g i", g=NG), bc(g_hot, 3, EPG), bc(hot[k], 2, NG), ALU.mult))
            step(tt(M3, pick[0], pick[1], ALU.add))
            step(v.memset(Mb3[:, 0, :], 0.0))
            for j in range(1, J):
                step(tt(Mb3[:, j, :], Mb3[:, j - 1, :], M3[:, j - 1, :], ALU.add))
            tt(M_total, Mb3[:, J - 1, :], M3[:, J - 1, :], ALU.add).then_inc(sem("picks_done"), 1)
            dve.wait_ge(sem("rank_mm"), 1)
            rank = ps[:, 7, 0:J * NE].rearrange("p (j e) -> p j e", j=J)
            step(tt(cmp_t, bc(ps[:, 7, J * NE:J * NE + NE], 2, 16), bc(whole, 1, NE), ALU.is_gt))
            step(v.tensor_reduce(ntile, cmp_t, AX.X, ALU.add))
            step(v.tensor_scalar(ntile, ntile, 1.0, None, ALU.max))
            step(v.memset(tstart[:, 0:1], 0.0))
            step(v.tensor_tensor_scan(tstart[:, 1:NE + 1], ones[:, 0:NE], ntile, 0.0, ALU.mult, ALU.add))
            pairs, total = tstart[:, NE + 1:NE + 2], tstart[:, NE:NE + 1]
            step(v.tensor_scalar(pairs, total, 0.5, 0.25, ALU.mult, ALU.add))
            step(v.tensor_scalar(pairs, pairs, MAGIC, None, ALU.add))
            step(v.tensor_scalar(pairs, pairs, -MAGIC, None, ALU.add))
            step(v.tensor_scalar(total, pairs, 2.0, None, ALU.mult))
            v.tensor_copy(tstart_i[:, :], tstart).then_inc(sem("tiles_counted"), 1)
            for k in range(2):
                step(tt(Mp3, rank, pick[k], ALU.mult))
                step(v.tensor_reduce(rk[:, k, :], Mp3, AX.X, ALU.add))
                step(tt(Mp3, bc(tstart[:, 0:NE], 1, J), pick[k], ALU.mult))
                step(v.tensor_reduce(hi[:, k, :], Mp3, AX.X, ALU.add))
            step(tt(cmp_r, bc(rk.rearrange("p k j -> p (k j)"), 2, 15), bc(whole[:, 1:16], 1, 2 * J), ALU.is_ge))
            step(v.tensor_reduce(fl, cmp_r, AX.X, ALU.add))
            hi_f, rk_f = hi.rearrange("p k j -> p (k j)"), rk.rearrange("p k j -> p (k j)")
            step(tt(hi_f, hi_f, fl, ALU.add))
            step(v.scalar_tensor_tensor(rk_f, fl, -float(TS), rk_f, ALU.mult, ALU.add))
            step(tt(oh_lo, bc(iota, 1, 2 * J), bc(rk_f, 2, TS), ALU.is_equal))
            step(tt(oh_hi, bc(iota[:, 0:MAX_TILES], 1, 2 * J), bc(hi_f, 2, MAX_TILES), ALU.is_equal))
            for k in range(2):
                last = tt(oh_hi[:, J * k:J * k + J, :], oh_hi[:, J * k:J * k + J, :], bc(tokid, 2, MAX_TILES), ALU.mult)
            last.then_inc(sem("onehots_done"), 1)
            step(v.tensor_scalar(fl, hi_f, float(TS), None, ALU.mult))
            step(tt(fl, fl, rk_f, ALU.add))
            step(v.tensor_copy(ypos[:, :], fl))
            step(v.tensor_copy(wsave, wpick))
            dve.wait_ge(sem("slot_mm"), 1)
            v.tensor_copy(slot_tok[0:TS, 0:MAX_TILES], ps[0:TS, 0, 0:MAX_TILES]).then_inc(sem("routed"), 1)

            dve.wait_ge(sem("routed"), 1)
            pairs = dve.value_load(tstart_i[0:1, NE + 1:NE + 2], min_val=NE // 2, max_val=MAX_TILES // 2)

            def times_up(g):
                dve.wait_ge(sem("silu_done"), g + 1)
                dve.wait_ge(sem("up_done"), g + 1)
                tt(hidden, hidden, ps[:, 1, 0:HE], ALU.mult).then_inc(sem("hidden_ready"), 1)

            def take_hidden(g):
                dve.wait_ge(sem("hidden_used"), g)
                v.tensor_copy(sg[:, HALF:HALF + HE], ps[:, 6, 0:HE]).then_inc(sem("hiddent_ready"), 1)

            def take_y(g, p, seen):
                dve.wait_ge(sem("tiles_done"), g)
                dve.wait_ge(sem(f"y_rows_out{p}"), seen * 32)
                tt(y_tile[p], ps[:, 2, :], gate2_bc[:, 0:HD], ALU.mult).then_inc(sem("y_copied"), 1)

            dve.wait_ge(sem("gate2_mm"), 1)
            for c in range(2):
                v.tensor_copy(gate2_bc[TS * c:TS * c + TS, 0:HD], ps[TS * c:TS * c + TS, 4 + c, :]).then_inc(sem("gate2_rows"), 1)
            dve.wait_ge(sem("gate2_rows"), 2)
            v.memset(small[:, 51:52], 0.0).then_inc(sem("y_copied"), 1)
            times_up(0)
            take_hidden(1)
            times_up(1)
            take_y(1, 0, 1)
            with dve.Fori(1, pairs) as m:
                for p in range(2):
                    g = m * 2 + p
                    take_hidden(g)
                    times_up(g)
                    take_y(g, 1 - p, m + p)
            take_hidden(pairs * 2)
            take_y(pairs * 2, 1, pairs)

            dve.wait_ge(sem("gf_in"), 16)
            def combine(t):
                dve.wait_ge(sem(f"ycomb_in{t}"), 32)
                v.scalar_tensor_tensor(h[:, t, :], ycomb[2 * t], wsave[:, 0, t:t + 1], h[:, t, :], ALU.mult, ALU.add).then_inc(sem("first_added"), 1)
                dve.wait_ge(sem("first_added"), t + 1)
                v.scalar_tensor_tensor(h[:, t, :], ycomb[2 * t + 1], wsave[:, 1, t:t + 1], h[:, t, :], ALU.mult, ALU.add).then_inc(sem("combined"), 1)

            def finish(j):
                if j not in POOL_OUT:
                    dve.wait_ge(sem("rstd3_done"), j + 1)
                    v.scalar_tensor_tensor(h[:, j, :], h[:, j, :], rstd[:, j:j + 1], gf_bc, ALU.mult, ALU.mult).then_inc(sem("out_dve"), 1)

            for t in range(J):
                combine(t)
                if t >= 2:
                    finish(t - 2)
            finish(J - 2)
            finish(J - 1)


_OUTS = [((1, SEQ, D), "float32")]


def kernel(**inputs):
    import numpy as _np
    import concourse.bacc as _bacc
    from concourse import mybir as _mybir
    from concourse.bass_utils import run_bass_kernel_spmd as _run

    nc = _bacc.Bacc("TRN2", target_bir_lowering=False, num_devices=1)
    arrays, args = {}, {}
    for name, value in inputs.items():
        value = _np.ascontiguousarray(value)
        arrays[f"in_{name}_dram"] = value
        args[name] = nc.dram_tensor(f"in_{name}_dram", value.shape, _mybir.dt.from_np(value.dtype), kind="ExternalInput").ap()
    for shape, dtype in _OUTS:
        args["out"] = nc.dram_tensor("out_0_dram", shape, _mybir.dt.from_np(_np.dtype(dtype)), kind="ExternalOutput").ap()
    program(nc, args)
    r = _run(nc, [arrays], core_ids=[0])
    return r.results[0]["out_0_dram"]
```
